# Optimizing a Trainium2 kernel written in Bass

```python
import math
import jax, jax.numpy as jnp
from jax import lax
import numpy as np

D_MODEL = 2048
BATCH = 1
SEQ = 256
DEPTH = 2

CHUNK = 64
Q_BLOCK = 128
MLA_HEADS = 8
Q_LORA = 512
KV_LORA = 256
NOPE_DIM = 128
ROPE_DIM = 64
QK_HEAD = NOPE_DIM + ROPE_DIM
MLA_V_DIM = 128
MLA_WIDTH = MLA_HEADS * MLA_V_DIM
ROPE_BASE = 10000.0
GLA_HEADS = 4
GLA_DK = 128
GLA_DV = 256
GLA_K_WIDTH = GLA_HEADS * GLA_DK
GLA_WIDTH = GLA_HEADS * GLA_DV
GATE_RANK = 16
GATE_TAU = 16.0
MIX_WIDTH = MLA_WIDTH + GLA_WIDTH
IN_SPLITS = (Q_LORA, KV_LORA, ROPE_DIM, GLA_K_WIDTH, GLA_K_WIDTH, GLA_WIDTH, GATE_RANK, GLA_WIDTH)
IN_DIM = sum(IN_SPLITS)
D_FF = 5632
CONV_W = 3
NORM_EPS = 1e-6

kernel_name = "hybrid_mla_gla_convffn_trunk"

def rms_norm(x, gain):
    x32 = x.astype(jnp.float32)
    y = x32 * lax.rsqrt(jnp.mean(x32 * x32, axis=-1, keepdims=True) + NORM_EPS)
    return (y * gain.astype(jnp.float32)).astype(x.dtype)

def split_cols(z, sizes):
    outs, start = [], 0
    for s in sizes:
        outs.append(z[..., start:start + s])
        start += s
    return outs

def apply_rope(x, cos, sin):
    x1, x2 = x[..., :ROPE_DIM // 2], x[..., ROPE_DIM // 2:]
    return jnp.concatenate([x1 * cos - x2 * sin, x2 * cos + x1 * sin], axis=-1)

def block_causal_attention(q, k, v):
    B, H, S, Dq = q.shape
    nb = S // Q_BLOCK
    scale = 1.0 / math.sqrt(Dq)
    qb = q.reshape(B, H, nb, Q_BLOCK, Dq).transpose(2, 0, 1, 3, 4)
    key_chunk = jnp.arange(S) // CHUNK

    def one_block(args):
        q_blk, b = args
        q_chunk = (b * Q_BLOCK + jnp.arange(Q_BLOCK)) // CHUNK
        s = jnp.einsum('bhqd,bhkd->bhqk', q_blk, k).astype(jnp.float32) * scale
        mask = key_chunk[None, :] <= q_chunk[:, None]
        s = jnp.where(mask[None, None], s, jnp.float32(-1e30))
        p = jax.nn.softmax(s, axis=-1)
        return jnp.einsum('bhqk,bhkd->bhqd', p.astype(v.dtype), v)

    out = lax.map(one_block, (qb, jnp.arange(nb)))
    return out.transpose(1, 2, 0, 3, 4).reshape(B, H, S, v.shape[-1])

def mla_mixer(z_cq, z_ckv, z_kr, cos, sin, cq_norm, w_uq, ckv_norm, w_ukv, q_norm, k_norm):
    B, S, _ = z_cq.shape
    q = (rms_norm(z_cq, cq_norm) @ w_uq).reshape(B, S, MLA_HEADS, QK_HEAD)
    kv = (rms_norm(z_ckv, ckv_norm) @ w_ukv).reshape(B, S, MLA_HEADS, NOPE_DIM + MLA_V_DIM)
    k_nope, v = kv[..., :NOPE_DIM], kv[..., NOPE_DIM:]
    k_rope = jnp.broadcast_to(z_kr[:, :, None, :], (B, S, MLA_HEADS, ROPE_DIM))
    k = jnp.concatenate([k_nope, k_rope], axis=-1)
    q = rms_norm(q, q_norm)
    k = rms_norm(k, k_norm)
    q = jnp.concatenate([q[..., :NOPE_DIM], apply_rope(q[..., NOPE_DIM:], cos, sin)], axis=-1)
    k = jnp.concatenate([k[..., :NOPE_DIM], apply_rope(k[..., NOPE_DIM:], cos, sin)], axis=-1)
    out = block_causal_attention(q.transpose(0, 2, 1, 3), k.transpose(0, 2, 1, 3), v.transpose(0, 2, 1, 3))
    return out.transpose(0, 2, 1, 3).reshape(B, S, MLA_WIDTH)

def gla_mixer(z_q, z_k, z_v, z_a, z_g, w_gate, b_gate, out_norm):
    B, S, _ = z_q.shape
    N = S // CHUNK

    def heads(t, d):
        return t.reshape(B, N, CHUNK, GLA_HEADS, d).transpose(0, 3, 1, 2, 4)

    q = heads(z_q, GLA_DK) * (GLA_DK ** -0.5)
    k = heads(z_k, GLA_DK)
    v = heads(z_v, GLA_DV)
    log_a = jax.nn.log_sigmoid((z_a @ w_gate + b_gate).astype(jnp.float32)) / GATE_TAU
    log_a = heads(log_a, GLA_DK)
    bcum = jnp.cumsum(log_a, axis=3)
    bend = bcum[:, :, :, -1:, :]
    k_dec = (k.astype(jnp.float32) * jnp.exp(bend - bcum)).astype(k.dtype)
    u = jnp.einsum('bhncd,bhnce->nbhde', k_dec, v)
    decay = jnp.exp(bend[:, :, :, 0, :]).transpose(2, 0, 1, 3)
    qn = q.transpose(2, 0, 1, 3, 4)

    def step(state, xs):
        u_c, d_c, q_c = xs
        state = state * d_c[..., None] + u_c.astype(jnp.float32)
        o = jnp.einsum('bhcd,bhde->bhce', q_c.astype(jnp.float32), state)
        return state, o

    init = jnp.zeros((B, GLA_HEADS, GLA_DK, GLA_DV), jnp.float32)
    _, o = lax.scan(step, init, (u, decay, qn))
    o = o.transpose(1, 0, 3, 2, 4).reshape(B, S, GLA_HEADS, GLA_DV).astype(z_v.dtype)
    o = rms_norm(o, out_norm).reshape(B, S, GLA_WIDTH)
    return o * jax.nn.silu(z_g)

def causal_dwconv(u, w, b):
    S = u.shape[1]
    up = jnp.pad(u, ((0, 0), (CONV_W - 1, 0), (0, 0)))
    y = b
    for j in range(CONV_W):
        y = y + up[:, j:j + S, :] * w[j]
    return y

def setup_inputs(seed: int = 0) -> dict:
    key = jax.random.key(seed)
    ks = jax.random.split(key, 24)
    L = DEPTH

    def nrm(k, shape, fan_in):
        return jax.random.normal(k, shape, jnp.float32) * (fan_in ** -0.5)

    def gain(k, shape):
        return 1.0 + 0.02 * jax.random.normal(k, shape, jnp.float32)

    x = jax.random.normal(ks[0], (BATCH, SEQ, D_MODEL), jnp.float32)
    positions = jnp.broadcast_to(jnp.arange(SEQ, dtype=jnp.int32), (BATCH, SEQ))
    return {
        "x": x,
        "positions": positions,
        "attn_norm": gain(ks[1], (L, D_MODEL)),
        "w_in": nrm(ks[2], (L, D_MODEL, IN_DIM), D_MODEL),
        "cq_norm": gain(ks[3], (L, Q_LORA)),
        "w_uq": nrm(ks[4], (L, Q_LORA, MLA_HEADS * QK_HEAD), Q_LORA),
        "ckv_norm": gain(ks[5], (L, KV_LORA)),
        "w_ukv": nrm(ks[6], (L, KV_LORA, MLA_HEADS * (NOPE_DIM + MLA_V_DIM)), KV_LORA),
        "q_norm": gain(ks[7], (L, QK_HEAD)),
        "k_norm": gain(ks[8], (L, QK_HEAD)),
        "w_gate": nrm(ks[9], (L, GATE_RANK, GLA_K_WIDTH), GATE_RANK),
        "b_gate": 0.1 * jax.random.normal(ks[10], (L, GLA_K_WIDTH), jnp.float32),
        "gla_out_norm": gain(ks[11], (L, GLA_DV)),
        "mla_out_norm": gain(ks[12], (L, MLA_WIDTH)),
        "w_out": nrm(ks[13], (L, MIX_WIDTH, D_MODEL), MIX_WIDTH),
        "ffn_norm": gain(ks[14], (L, D_MODEL)),
        "w_up": nrm(ks[15], (L, D_MODEL, 2 * D_FF), D_MODEL),
        "conv_w": nrm(ks[16], (L, CONV_W, 2 * D_FF), CONV_W),
        "conv_b": 0.02 * jax.random.normal(ks[17], (L, 2 * D_FF), jnp.float32),
        "w_down": nrm(ks[18], (L, D_FF, D_MODEL), D_FF),
    }

def reference(x, positions, attn_norm, w_in, cq_norm, w_uq, ckv_norm, w_ukv, q_norm, k_norm,
              w_gate, b_gate, gla_out_norm, mla_out_norm, w_out, ffn_norm, w_up, conv_w, conv_b, w_down):
    inv_freq = ROPE_BASE ** (-jnp.arange(0, ROPE_DIM, 2, dtype=jnp.float32) / ROPE_DIM)
    angle = positions.astype(jnp.float32)[..., None] * inv_freq
    cos = jnp.cos(angle)[:, :, None, :].astype(x.dtype)
    sin = jnp.sin(angle)[:, :, None, :].astype(x.dtype)
    for l in range(DEPTH):
        h = rms_norm(x, attn_norm[l])
        z = h @ w_in[l]
        z_cq, z_ckv, z_kr, z_q, z_k, z_v, z_a, z_g = split_cols(z, IN_SPLITS)
        a_out = mla_mixer(z_cq, z_ckv, z_kr, cos, sin, cq_norm[l], w_uq[l], ckv_norm[l], w_ukv[l],
                          q_norm[l], k_norm[l])
        a_out = rms_norm(a_out, mla_out_norm[l])
        g_out = gla_mixer(z_q, z_k, z_v, z_a, z_g, w_gate[l], b_gate[l], gla_out_norm[l])
        x = x + jnp.concatenate([a_out, g_out], axis=-1) @ w_out[l]
        h = rms_norm(x, ffn_norm[l])
        u = causal_dwconv(h @ w_up[l], conv_w[l], conv_b[l])
        gate, up = u[..., :D_FF], u[..., D_FF:]
        x = x + (jax.nn.silu(gate) * up) @ w_down[l]
    return x


_drawn_inputs = setup_inputs


def setup_inputs(seed=0):
    import zlib

    import numpy as np

    out = dict(_drawn_inputs(seed))
    spreads = {}
    factors = {'cq_norm': 4.569,
     'q_norm': 4.064,
     'k_norm': 4.696,
     'gla_out_norm': 5.676,
     'mla_out_norm': 3.046,
     'ffn_norm': 3.231,
     'conv_b': 3.091}
    for name, (base, spread) in spreads.items():
        noise = np.random.default_rng([zlib.crc32(name.encode()), seed]).standard_normal(out[name].shape)
        drawn = base * np.exp(spread * noise) if base else spread * noise
        out[name] = __import__('jax').numpy.asarray(drawn.astype(out[name].dtype))
    for name, factor in factors.items():
        out[name] = (out[name] * factor).astype(out[name].dtype)
    return out
```

```python
from contextlib import ExitStack

import numpy as np

import concourse.bass as bass
from concourse import mybir

F32 = mybir.dt.float32
F32R = mybir.dt.float32r
I32 = mybir.dt.int32
ACT = mybir.ActivationFunctionType
ALU = mybir.AluOpType
AX_X = mybir.AxisListType.X

P = 128
T = 256
TT = T // P
D = 2048
KT = D // P
DEPTH = 2
EPS = 1e-6
NEG = -1e30

Q_LORA, KV_LORA, ROPE, NOPE, VD, HEADS = 512, 256, 64, 128, 128, 8
QK = NOPE + ROPE
GH, GDK, GDV, RANK, TAU, CHUNK = 4, 128, 256, 16, 16.0, 64
GK_W, GV_W = GH * GDK, GH * GDV
C_CQ, C_CKV = 0, Q_LORA
C_KR = C_CKV + KV_LORA
C_GQ = C_KR + ROPE
C_GK = C_GQ + GK_W
C_GV = C_GK + GK_W
C_A = C_GV + GV_W
C_G = C_A + RANK
D_FF = 5632
FT = D_FF // P
GROUP = 4
NG = FT // GROUP
CONV = 3

SLOTS = 3
WORDS = 2048

K_TOK = 0
K_MISC = K_TOK + 12
K_FEAT = K_MISC + 2
K_UQ = K_FEAT + 18
K_UKV = K_UQ + HEADS // 2
K_OUT = K_UKV + HEADS // 4
K_FFN = K_OUT + 16
GROUP_CHUNKS = 12
CHUNKS = K_FFN + NG * GROUP_CHUNKS
ROUNDS = CHUNKS // SLOTS
U_TOK = 0
U_FEAT = U_TOK + 3
U_UQ = U_FEAT + 9
U_UKV = U_UQ + HEADS
U_OUT = U_UKV + 6
U_FFN = U_OUT + 8
GROUP_UNITS = 12
UNITS = U_FFN + NG * GROUP_UNITS
PAIRS = UNITS // 2
assert CHUNKS % SLOTS == 0 and UNITS % 2 == 0 and K_FFN % SLOTS == 0 and U_FFN % 2 == 0

FEAT_COLS = [C_GQ, C_GQ + 256, C_CQ, C_CQ + 256, C_CKV, C_G, C_G + 256, C_G + 512, C_G + 768]
Z_GQ, Z_CQ, Z_CKV, Z_G = 0, 4, 8, 10
H_FEAT, H_UQ, H_UKV, H_FFN = 0, 9, 17, 21
HALF_COPIES = H_FFN + NG * 4
MID_UNITS = 8 + NG * 4
ROW_LOADS = DEPTH * 16 + 1
TWO_PI = 6.283185307179586
TURN_PARTS = (6.28125, 0.0019350051879882812, 3.01991598196686e-07)
NEARLY_PI = 3.1415925
ROUNDER = 12582912.0
ROPE_BASE = 10000.0

G_ATTN, G_FFN, G_CQ, G_CKV, G_MLA, G_GLA, G_QN, G_QR, G_KN, G_KR = 0, 16, 32, 36, 38, 46, 48, 49, 50, 51
GAINS = 52
FT2 = 2 * FT
PARAMS = GAINS + (CONV + 1) * FT2
CO_ID, CO_ONES, CO_SEL, CO_SUF, CO_ROT, CO_IND, CO_FREQ, CO_EPS = 0, 128, 256, 512, 640, 768, 770, 771
CONSTS = 772


class Signal:

    def __init__(self, sem, n):
        self.sem, self.n = sem, n

    def at(self, turn, count):
        return turn * self.n + count


def trunk_program(nc, t, out):
    with ExitStack() as ctx:
        def sb(name, shape, dt=F32):
            return ctx.enter_context(nc.sbuf_tensor(name, shape, dt))

        def semaphore(name):
            return ctx.enter_context(nc.semaphore(name))

        def signal(name, n):
            return Signal(semaphore(name), n)

        raw = sb("raw", [P, SLOTS, WORDS])
        hi = sb("hi", [P, SLOTS, WORDS], F32R)
        lo = sb("lo", [P, SLOTS, WORDS], F32R)
        xT = sb("xT", [P, KT, T])
        hx = sb("hx", [P, KT, 2 * T], F32R)
        mid = sb("mid", [P, 2 * GROUP, 2 * T], F32R)
        z = sb("z", [P, 18, T])
        zm = sb("zm", [P, T])
        qkn = sb("qkn", [P, 16, T])
        gv = sb("gv", [P, TT, GV_W])
        v = sb("v", [P, TT, HEADS * VD])
        half = sb("half", [P, 2, 2, T])
        sq = sb("sq", [P, 2, 2, T])
        gains = sb("gains", [P, GAINS])
        conv_p = sb("conv_p", [P, CONV + 1, 2, GROUP])
        params_all = sb("params_all", [P, DEPTH, PARAMS])
        cst = sb("cst", [P, CONSTS])
        cos = sb("cos", [P, T])
        sin = sb("sin", [P, T])
        wg = sb("wg", [P, GK_W])
        rs = sb("rs", [P, 2 * T])
        small = sb("small", [P, 64])

        xtok = [z[:, 0:8, :].rearrange("p a b -> p (a b)"), qkn[:, 0:8, :].rearrange("p a b -> p (a b)")]
        rows = gv[:, :, :].rearrange("p a b -> p (a b)")
        gk = qkn[:, 8:12, :].rearrange("p a b -> p (a b)").rearrange("p (t c) -> p t c", t=TT)
        la = qkn[:, 12:16, :].rearrange("p a b -> p (a b)").rearrange("p (t c) -> p t c", t=TT)
        state = v[:, 0, :].rearrange("p (h e) -> p h e", h=GH)
        oT = qkn[:, 0:8, :].rearrange("p (e h) t -> p e (h t)", e=2)
        rope_tmp = gv[:, 0, 0:2 * T].rearrange("p (a t) -> p a t", a=2)
        htmp = z[:, 0:4, :].rearrange("p (a b) t -> p a b t", a=2)
        qkr = z[:, 0:8, :]
        prob = half[:, :, :, :].rearrange("p a b t -> p a (b t)")
        probT = sq[:, :, :, :].rearrange("p a b t -> p a (b t)")
        vflat = v[:, :, :].rearrange("p a b -> p (a b)")
        yg = vflat[:, 0:512].rearrange("p (a t) -> p a t", a=2)
        yu = vflat[:, 512:1024].rearrange("p (a t) -> p a t", a=2)
        qkn_flat = qkn[:, :, :].rearrange("p a b -> p (a b)")
        ubuf = [x[:, 0:2 * (T + CONV - 1)].rearrange("p (a t) -> p a t", a=2) for x in (vflat[:, 1024:2048], qkn_flat)]

        conv_all = params_all[:, :, GAINS:PARAMS].rearrange("p l (j s f) -> p l j s f", j=CONV + 1, s=2)
        ident = cst[:, CO_ID:CO_ID + P]
        ones = cst[:, CO_ONES:CO_ONES + P]
        sel = [cst[:, CO_SEL + i * P:CO_SEL + (i + 1) * P] for i in range(2)]
        suf = cst[:, CO_SUF:CO_SUF + P]
        rot = cst[:, CO_ROT:CO_ROT + P]
        ind = cst[:, CO_IND:CO_IND + 2]
        freq = cst[:, CO_FREQ:CO_FREQ + 1]
        eps = cst[:, CO_EPS:CO_EPS + 1]
        decay = small[:, 0:16]
        top = small[:, 16:20]
        ntop = small[:, 20:24]
        sums = small[:, 24:28]
        rsum = small[:, 28:32]

        G = ctx.enter_context(nc.psum_tensor("G", [P, 4, 512], F32))
        X = ctx.enter_context(nc.psum_tensor("X", [P, 4, 512], F32))

        def gain(col):
            return gains[:, col:col + 1]

        def bank2(u):
            return G[:, 2 * (u % 2):2 * (u % 2) + 2, :]

        def head_parts(buf, k):
            rows = buf[:, k % SLOTS, 0:4 * 2 * QK].rearrange("p (a c) -> p a c", a=4)
            as_loaded = rows.rearrange("p a (h c) -> p a h c", h=2)
            for a, b in ((0, NOPE), (NOPE, QK)):
                used = rows[:, :, 2 * a:2 * b].rearrange("p a (h c) -> p a h c", h=2)
                yield used, as_loaded[:, :, :, a:b]

        raw_landed = [semaphore(f"raw_landed{s}") for s in range(SLOTS)]
        hi_ready = semaphore("hi_ready")
        lo_ready = semaphore("lo_ready")
        slot_free = semaphore("slot_free")
        unit_done = semaphore("unit_done")
        unit_free = semaphore("unit_free")
        half_copied = semaphore("half_copied")
        const_landed = semaphore("const_landed")
        rows_landed = semaphore("rows_landed")
        at_column_0 = semaphore("at_column_0")
        x_landed = semaphore("x_landed")
        zeroed = semaphore("zeroed")
        rows_turned = semaphore("rows_turned")
        rows_copied = semaphore("rows_copied")
        x_turned = semaphore("x_turned")
        x_copied = semaphore("x_copied")
        angle_step = semaphore("angle_step")
        angle_small = semaphore("angle_small")
        table_step = semaphore("table_step")
        out_turned = semaphore("out_turned")
        out_copied = semaphore("out_copied")
        out_stored = semaphore("out_stored")
        params_set = signal("params_set", 1)
        gate_landed = signal("gate_landed", 32)
        misc_landed = [signal(f"misc_landed{i}", 16) for i in range(2)]
        norm_squared = signal("norm_squared", 16)
        norm_square_used = signal("norm_square_used", 16)
        norm_root = signal("norm_root", 2)
        norm_scale = signal("norm_scale", 2)
        h_scaled = signal("h_scaled", 32)
        h_high = signal("h_high", 16)
        h_ready = signal("h_ready", 16)
        misc_done = signal("misc_done", 1)
        misc_half = signal("misc_half", 1)
        misc_ready = signal("misc_ready", 1)
        c_squared = signal("c_squared", 3)
        c_square_used = signal("c_square_used", 3)
        c_root = signal("c_root", 2)
        c_scale = signal("c_scale", 1)
        c_scaled = signal("c_scaled", 6)
        c_high = signal("c_high", 3)
        c_ready = signal("c_ready", 3)
        gate_logits = signal("gate_logits", 1)
        gate_soft = signal("gate_soft", 3)
        gate_log = signal("gate_log", 1)
        gate_sums = signal("gate_sums", 1)
        gate_decay = signal("gate_decay", 2)
        keys_decayed = signal("keys_decayed", 1)
        update_done = signal("update_done", 4)
        state_ready = signal("state_ready", 16)
        reads_done = signal("reads_done", 4)
        reads_copied = signal("reads_copied", 4)
        o_squared = signal("o_squared", 4)
        o_summed = signal("o_summed", 4)
        o_root = signal("o_root", 4)
        o_scale = signal("o_scale", 4)
        o_scaled = signal("o_scaled", 8)
        g_silu = signal("g_silu", 1)
        o_gated = signal("o_gated", 4)
        o_high = signal("o_high", 4)
        o_ready = signal("o_ready", 4)
        kr_spread = signal("kr_spread", 2)
        qk_squared = signal("qk_squared", 16)
        qk_summed = signal("qk_summed", 8)
        qk_root = signal("qk_root", 8)
        qk_scale = signal("qk_scale", 8)
        qk_normed = signal("qk_normed", 24)
        rope_turned = signal("rope_turned", 8)
        rope_parts = signal("rope_parts", 16)
        rope_done = signal("rope_done", 8)
        scores_done = signal("scores_done", HEADS)
        scores_masked = signal("scores_masked", 2 * HEADS)
        tops_found = signal("tops_found", 2 * HEADS)
        tops_scaled = signal("tops_scaled", HEADS)
        exps_done = signal("exps_done", 2 * HEADS)
        sums_inverted = signal("sums_inverted", HEADS)
        probs_ready = signal("probs_ready", 2 * HEADS)
        probs_turned = signal("probs_turned", HEADS)
        probs_copied = signal("probs_copied", HEADS)
        values_done = signal("values_done", HEADS)
        values_copied = signal("values_copied", HEADS)
        a_squared = signal("a_squared", 4)
        a_square_used = signal("a_square_used", 4)
        a_root = signal("a_root", 1)
        a_scale = signal("a_scale", 1)
        a_scaled = signal("a_scaled", 8)
        a_high = signal("a_high", 4)
        a_ready = signal("a_ready", 4)
        x_added = semaphore("x_added")
        pads_zeroed = signal("pads_zeroed", 2)
        X_ADDS = U_FFN - U_OUT + NG * 8
        taps_set = signal("taps_set", 1)
        conv_step = signal("conv_step", 24)
        gate_done = signal("gate_done", 2)
        product_done = signal("product_done", 2)
        mid_high = signal("mid_high", 2)
        mid_ready = signal("mid_ready", 2)

        w_in = t["w_in"].rearrange("l (k p) n -> l p k n", p=P)
        w_uq = t["w_uq"].rearrange("l (k p) n -> l p k n", p=P)
        w_ukv = t["w_ukv"].rearrange("l (k p) n -> l p k n", p=P)
        w_out = t["w_out"].rearrange("l (k p) n -> l p k n", p=P)
        w_up = t["w_up"].rearrange("l (k p) n -> l p k n", p=P)
        w_down = t["w_down"].rearrange("l (k p) n -> l p k n", p=P)

        TURN_ROUNDS, TURN_PAIRS = 2 * GROUP_CHUNKS // SLOTS, GROUP_UNITS

        def mlp_order(e, l, up, down):
            r0, p0 = l * ROUNDS, l * PAIRS
            up(l, 0, 0, r0, K_FFN, p0, U_FFN)
            with e.Fori(0, (NG - 1) // 2) as j:
                r, p = r0 + j * TURN_ROUNDS, p0 + j * TURN_PAIRS
                up(l, 2 * j + 1, 1, r, K_FFN + 8, p, U_FFN + 4)
                down(l, 2 * j, 0, r, K_FFN + 16, p, U_FFN + 8)
                up(l, 2 * j + 2, 0, r, K_FFN + 20, p, U_FFN + 16)
                down(l, 2 * j + 1, 1, r, K_FFN + 28, p, U_FFN + 20)
            down(l, NG - 1, 0, r0, CHUNKS - 4, p0, UNITS - 8)

        block = ctx.enter_context(nc.Block())

        @block.sync
        def _(sp):
            def load(r, k, shape, src, at_start=False):
                n = shape[0] * shape[1]
                dst = raw[:, k % SLOTS, 0:n].rearrange("p (a b) -> p a b", a=shape[0])
                sp.wait_ge(lo_ready, r * SLOTS + k + 1)
                if at_start:
                    sp.sem_inc(at_column_0, 1)
                sp.dma_start(dst, src.rearrange("o p k n -> p (o k) n")).then_inc(raw_landed[k % SLOTS], 16)

            sp.dma_start(cst[:, :], t["consts"]).then_inc(const_landed, 16)
            for i in range(TT):
                sp.dma_start(xtok[i], t["x"][0, i * P:(i + 1) * P, :]).then_inc(x_landed, 16)

            def row(l, at, n, src):
                sp.dma_start(rows[at:at + n, l * P:(l + 1) * P], src).then_inc(rows_landed, 16)

            for l in range(DEPTH):
                row(l, G_ATTN, 16, t["attn_norm"][l].rearrange("(a b) -> a b", b=P))
                row(l, G_FFN, 16, t["ffn_norm"][l].rearrange("(a b) -> a b", b=P))
                row(l, G_CQ, 4, t["cq_norm"][l].rearrange("(a b) -> a b", b=P))
                row(l, G_CKV, 2, t["ckv_norm"][l].rearrange("(a b) -> a b", b=P))
                row(l, G_MLA, 8, t["mla_out_norm"][l].rearrange("(a b) -> a b", b=P))
                row(l, G_GLA, 2, t["gla_out_norm"][l].rearrange("(a b) -> a b", b=P))
                for col, name in ((G_QN, "q_norm"), (G_KN, "k_norm")):
                    row(l, col, 1, t[name][l:l + 1, 0:NOPE])
                    for i in range(2):
                        sp.dma_start(rows[col + 1:col + 2, l * P + i * ROPE:l * P + (i + 1) * ROPE],
                                     t[name][l:l + 1, NOPE:QK]).then_inc(rows_landed, 16)
                for j in range(CONV + 1):
                    src = t["conv_w"][l, j] if j < CONV else t["conv_b"][l]
                    at = (DEPTH + l * (CONV + 1) + j) * P
                    sp.dma_start(rows[0:FT2, at:at + P], src.rearrange("(a b) -> a b", b=P)).then_inc(rows_landed, 16)
            sp.dma_start(cos[:, :].bitcast(I32), t["positions"].to_broadcast([P, T])).then_inc(rows_landed, 16)

            def up(l, g, par, r, k, ur, u):
                for f in range(2):
                    for side in range(2):
                        for h in range(2):
                            load(r, k + 4 * f + 2 * side + h, (8, 256),
                                 w_up[bass.ds(l, 1), :, 8 * h:8 * h + 8,
                                      bass.ds(g * (GROUP * P) + (f * 256 + side * D_FF), 256)])

            def down(l, g, par, r, k, ur, u):
                for q in range(4):
                    load(r, k + q, (4, 512),
                         w_down[bass.ds(l, 1), :, bass.ds(g * GROUP, GROUP), 512 * q:512 * q + 512])

            with sp.Fori(0, DEPTH) as l:
                L, r = bass.ds(l, 1), l * ROUNDS
                for j in range(3):
                    for q in range(4):
                        c0 = C_GK + 512 * j
                        load(r, K_TOK + 4 * j + q, (4, 512), w_in[L, :, 4 * q:4 * q + 4, c0:c0 + 512])
                for h in range(2):
                    k = K_MISC + h
                    dst = raw[:, k % SLOTS, 0:8 * 80].rearrange("p (a b) -> p a b", a=8)
                    sp.wait_ge(lo_ready, r * SLOTS + k + 1)
                    for a, b, c0 in ((0, ROPE, C_KR), (ROPE, ROPE + RANK, C_A)):
                        src = w_in[L, :, 8 * h:8 * h + 8, c0:c0 + b - a].rearrange("o p k n -> p (o k) n")
                        if a == 0:
                            sp.dma_start(dst[:, :, a:b], src).then_inc(raw_landed[k % SLOTS], 16)
                        else:
                            sp.dma_start(dst[:, :, a:b], src).then_inc(misc_landed[h].sem, 16)
                for i, c0 in enumerate(FEAT_COLS):
                    for h in range(2):
                        load(r, K_FEAT + 2 * i + h, (8, 256), w_in[L, :, 8 * h:8 * h + 8, c0:c0 + 256], c0 + h == 0)
                for j in range(4):
                    load(r, K_UQ + j, (4, 384), w_uq[L, :, :, 384 * j:384 * j + 384])
                for j in range(2):
                    load(r, K_UKV + j, (2, 1024), w_ukv[L, :, :, 1024 * j:1024 * j + 1024])
                for i in range(8):
                    for h in range(2):
                        load(r, K_OUT + 2 * i + h, (8, 256), w_out[L, :, 8 * h:8 * h + 8, 256 * i:256 * i + 256])
                mlp_order(sp, l, up, down)
            for i in range(TT):
                sp.wait_ge(out_copied, 4 * (i + 1))
                sp.dma_start(out[0, i * P:(i + 1) * P, :], xtok[i]).then_inc(out_stored, 16)
            sp.wait_ge(out_stored, 16 * TT)

        @block.gpsimd
        def _(pool):
            with pool.Fori(0, DEPTH) as l:
                pool.wait_ge(params_set.sem, params_set.at(l, 1))
                pool.dma_start(wg[64:64 + RANK, :], t["w_gate"][bass.ds(l, 1)].rearrange("o a b -> (o a) b")).then_inc(gate_landed.sem, 16)
                pool.dma_start(wg[64 + RANK:64 + RANK + 1, :], t["b_gate"][bass.ds(l, 1)]).then_inc(gate_landed.sem, 16)

        @block.scalar
        def _(act):
            def split(r, k):
                n = 640 if K_MISC <= k < K_FEAT else WORDS
                act.wait_ge(raw_landed[k % SLOTS], (r + k // SLOTS + 1) * 16)
                act.wait_ge(slot_free, r * SLOTS + k + 1)
                if K_UQ <= k < K_UKV:
                    for (_, part), (dst, _) in zip(head_parts(raw, k), head_parts(hi, k)):
                        ins = act.activation(dst, part, ACT.Copy)
                    ins.then_inc(hi_ready, 1)
                else:
                    act.activation(hi[:, k % SLOTS, 0:n], raw[:, k % SLOTS, 0:n], ACT.Copy).then_inc(hi_ready, 1)

            def copy_half(u, banks=2):
                act.activation(half[:, u % 2, 0:banks, :], bank2(u)[:, 0:banks, T:2 * T],
                               ACT.Copy).then_inc(half_copied, 1)

            def norm(l, which):
                for i in range(8):
                    if i >= 2:
                        act.wait_ge(norm_square_used.sem, norm_square_used.at(l, 8 * which + i - 1))
                    act.activation(sq[:, i % 2, :, :], xT[:, 2 * i:2 * i + 2, :], ACT.Square).then_inc(norm_squared.sem, 1)
                act.wait_ge(norm_square_used.sem, norm_square_used.at(l, 8 * which + 8))
                act.activation(rs[:, 0:T], X[:, which, 0:T], ACT.Sqrt, bias=eps, scale=1.0 / D).then_inc(norm_root.sem, 1)
                for i in range(8):
                    act.wait_ge(h_scaled.sem, h_scaled.at(l, 16 * which + 2 * i + 2))
                    act.activation(hx[:, 2 * i:2 * i + 2, 0:T], htmp[:, i % 2, :, :], ACT.Copy).then_inc(h_high.sem, 1)

            def up(l, g, par, r, k, ur, u):
                turn = l * NG + g
                for s in range(8):
                    split(r, k + s + 2)
                    f = s // 4
                    if s % 2:
                        act.wait_ge(slot_free, r * SLOTS + (k + s + 1 + SLOTS))
                        copy_half(u + s // 2)
                    if s % 4 == 3:
                        act.wait_ge(conv_step.sem, conv_step.at(turn, 12 * f + 6))
                        act.activation(yg, yg, ACT.Silu).then_inc(gate_done.sem, 1)
                        act.wait_ge(product_done.sem, product_done.at(turn, f + 1))
                        m = GROUP * par + 2 * f
                        act.activation(mid[:, m:m + 2, 0:T], yu, ACT.Copy).then_inc(mid_high.sem, 1)

            def down(l, g, par, r, k, ur, u):
                for q in range(4):
                    if k + q + 2 < CHUNKS:
                        split(r, k + q + 2)

            act.wait_ge(angle_small, 1)
            act.activation(rs[:, 0:T], sin[:, :], ACT.Abs).then_inc(table_step, 1)
            act.wait_ge(angle_small, 2)
            act.activation(cos[:, :], rs[:, T:2 * T], ACT.Sin).then_inc(table_step, 1)
            act.wait_ge(table_step, 2)
            act.activation(sin[:, :], sin[:, :], ACT.Sin).then_inc(table_step, 1)

            with act.Fori(0, DEPTH) as l:
                r = l * ROUNDS
                split(r, 0)
                split(r, 1)
                act.wait_ge(params_set.sem, params_set.at(l, 1))
                norm(l, 0)
                for s in range(14):
                    if s in (10, 11):
                        act.wait_ge(misc_landed[s - 10].sem, misc_landed[s - 10].at(l, 16))
                    split(r, s + 2)
                act.wait_ge(slot_free, r * SLOTS + K_FEAT + SLOTS)
                act.activation(rs[0:80, 0:T], X[0:80, 1, T:2 * T], ACT.Copy).then_inc(misc_half.sem, 1)
                for i in range(9):
                    split(r, K_FEAT + 2 * i + 2)
                    split(r, K_FEAT + 2 * i + 3)
                    act.wait_ge(slot_free, r * SLOTS + K_FEAT + 2 * i + 2 + SLOTS)
                    copy_half(U_FEAT + i)
                for i in range(3):
                    act.wait_ge(unit_free, l * UNITS + U_FEAT + 3 + i + 2)
                    if i == 2:
                        act.wait_ge(c_square_used.sem, c_square_used.at(l, 1))
                    act.activation(sq[:, i % 2, :, :], z[:, Z_CQ + 2 * i:Z_CQ + 2 * i + 2, :], ACT.Square).then_inc(c_squared.sem, 1)
                act.wait_ge(c_square_used.sem, c_square_used.at(l, 3))
                act.wait_ge(misc_ready.sem, misc_ready.at(l, 1))
                act.activation(rs[:, 0:T], X[:, 0, 0:T], ACT.Sqrt, bias=eps, scale=1.0 / Q_LORA).then_inc(c_root.sem, 1)
                act.activation(rs[:, T:2 * T], X[:, 0, T:2 * T], ACT.Sqrt, bias=eps, scale=1.0 / KV_LORA).then_inc(c_root.sem, 1)
                for i in range(3):
                    act.wait_ge(c_scaled.sem, c_scaled.at(l, 2 * i + 2))
                    act.activation(mid[:, 2 * i:2 * i + 2, 0:T], z[:, Z_CQ + 2 * i:Z_CQ + 2 * i + 2, :], ACT.Copy).then_inc(c_high.sem, 1)
                act.wait_ge(gate_logits.sem, gate_logits.at(l, 1))
                act.activation(la, X[:, 2:4, :], ACT.Abs).then_inc(gate_soft.sem, 1)
                act.wait_ge(gate_soft.sem, gate_soft.at(l, 1))
                act.activation(la, la, ACT.Exp, scale=-1.0).then_inc(gate_soft.sem, 1)
                act.wait_ge(gate_soft.sem, gate_soft.at(l, 2))
                act.activation(la, la, ACT.Ln, bias=ones[:, 0:1]).then_inc(gate_soft.sem, 1)
                act.wait_ge(gate_sums.sem, gate_sums.at(l, 1))
                act.activation(la, X[:, 2:4, :], ACT.Exp, scale=1.0 / TAU).then_inc(gate_decay.sem, 1)
                act.activation(decay, X[:, 1, 0:16], ACT.Exp, scale=1.0 / TAU).then_inc(gate_decay.sem, 1)
                act.wait_ge(unit_free, l * UNITS + U_UQ + 2)
                act.activation(z[:, Z_G:Z_G + 8, :], z[:, Z_G:Z_G + 8, :], ACT.Silu).then_inc(g_silu.sem, 1)
                act.wait_ge(reads_copied.sem, reads_copied.at(l, 4))
                for h in range(GH):
                    if h >= 2:
                        act.wait_ge(o_summed.sem, o_summed.at(l, h - 1))
                    act.activation(sq[:, h % 2, :, :], oT[:, :, h * T:(h + 1) * T], ACT.Square).then_inc(o_squared.sem, 1)
                for h in range(GH):
                    act.wait_ge(o_summed.sem, o_summed.at(l, h + 1))
                    if h >= 2:
                        act.wait_ge(o_scaled.sem, o_scaled.at(l, 2 * h - 2))
                    act.activation(rs[:, (h % 2) * T:(h % 2 + 1) * T], X[:, h, 0:T], ACT.Sqrt,
                                   bias=eps, scale=1.0 / GDV).then_inc(o_root.sem, 1)
                for h in range(GH):
                    act.wait_ge(o_gated.sem, o_gated.at(l, h + 1))
                    act.activation(hx[:, 8 + 2 * h:10 + 2 * h, 0:T], oT[:, :, h * T:(h + 1) * T], ACT.Copy).then_inc(o_high.sem, 1)
                for j in range(4):
                    split(r, K_UQ + j + 2)
                    act.wait_ge(unit_done, l * MID_UNITS + j + 1)
                    copy_half(U_UQ + 2 * j)
                    act.wait_ge(slot_free, r * SLOTS + K_UQ + j + 1 + SLOTS)
                    copy_half(U_UQ + 2 * j + 1, 1)
                for j in range(2):
                    split(r, K_UKV + j + 2)
                    for i in range(2):
                        act.wait_ge(unit_done, l * MID_UNITS + 4 + 2 * j + i + 1)
                        copy_half(U_UKV + 3 * j + i)
                for i in range(2):
                    act.activation(qkr[64 * i:64 * i + 64, 4:8, :],
                                   zm[0:64, :].rearrange("p (o t) -> p o t", o=1).to_broadcast([64, 4, T]),
                                   ACT.Copy).then_inc(kr_spread.sem, 1)
                act.wait_ge(kr_spread.sem, kr_spread.at(l, 2))
                act.wait_ge(unit_free, l * UNITS + U_OUT + 2)
                for j in range(8):
                    if j >= 1:
                        act.wait_ge(qk_summed.sem, qk_summed.at(l, j))
                    act.activation(sq[:, 0, :, :], qkn[:, 2 * j:2 * j + 2, :], ACT.Square).then_inc(qk_squared.sem, 1)
                    act.activation(sq[:, 1, 0, :], qkr[:, j, :], ACT.Square).then_inc(qk_squared.sem, 1)
                    act.wait_ge(qk_summed.sem, qk_summed.at(l, j + 1))
                    if j >= 1:
                        act.wait_ge(qk_normed.sem, qk_normed.at(l, 3 * j))
                    act.activation(rs[:, :], X[:, j % 2, :], ACT.Sqrt, bias=eps, scale=1.0 / QK).then_inc(qk_root.sem, 1)
                for h in range(HEADS):
                    act.wait_ge(tops_scaled.sem, tops_scaled.at(l, h + 1))
                    if h >= 2:
                        act.wait_ge(probs_turned.sem, probs_turned.at(l, h - 1))
                    for b in range(TT):
                        a0, a1 = (0, P) if b == 0 else (P, 3 * P)
                        at = 2 * (h % 2) + b
                        act.activation(prob[:, h % 2, a0:a1], X[:, h % 2, a0:a1], ACT.Exp,
                                       bias=ntop[:, at:at + 1], scale=QK ** -0.5,
                                       accum_out=sums[:, at:at + 1]).then_inc(exps_done.sem, 1)
                    act.wait_ge(probs_turned.sem, probs_turned.at(l, h + 1))
                    if h >= 2:
                        act.wait_ge(values_done.sem, values_done.at(l, h - 1))
                    act.activation(probT[:, h % 2, 0:3 * P], X[:, 2, 0:3 * P], ACT.Copy).then_inc(probs_copied.sem, 1)
                act.wait_ge(values_copied.sem, values_copied.at(l, HEADS))
                for i in range(4):
                    if i >= 2:
                        act.wait_ge(a_square_used.sem, a_square_used.at(l, i - 1))
                    act.activation(sq[:, i % 2, :, :], qkn[:, 2 * i:2 * i + 2, :], ACT.Square).then_inc(a_squared.sem, 1)
                act.wait_ge(a_square_used.sem, a_square_used.at(l, 4))
                act.activation(rs[:, 0:T], X[:, 0, 0:T], ACT.Sqrt, bias=eps, scale=1.0 / (HEADS * VD)).then_inc(a_root.sem, 1)
                for i in range(4):
                    act.wait_ge(a_scaled.sem, a_scaled.at(l, 2 * i + 2))
                    act.activation(hx[:, 2 * i:2 * i + 2, 0:T], qkn[:, 2 * i:2 * i + 2, :], ACT.Copy).then_inc(a_high.sem, 1)
                for s in range(16):
                    split(r, K_OUT + s + 2)
                act.wait_ge(unit_free, l * UNITS + U_FFN + 2)
                norm(l, 1)
                mlp_order(act, l, up, down)

        @block.vector
        def _(dve):
            def split(r, k):
                n = 640 if K_MISC <= k < K_FEAT else WORDS
                s = k % SLOTS
                dve.wait_ge(hi_ready, r * SLOTS + k + 1)
                if K_UQ <= k < K_UKV:
                    for (_, part), (h, _), (dst, _) in zip(head_parts(raw, k), head_parts(hi, k), head_parts(lo, k)):
                        ins = dve.tensor_tensor(dst, part, h.bitcast(F32), ALU.subtract)
                    ins.then_inc(lo_ready, 1)
                else:
                    dve.tensor_tensor(lo[:, s, 0:n], raw[:, s, 0:n], hi[:, s, 0:n].bitcast(F32),
                                      ALU.subtract).then_inc(lo_ready, 1)

            def add_halves(u, dst, banks=2):
                dve.tensor_tensor(dst, bank2(u)[:, 0:banks, 0:T], half[:, u % 2, 0:banks, :],
                                  ALU.add).then_inc(unit_free, 1)

            def add_to_x(l, u, n, tile):
                two = xT[:, tile:tile + 2, :]
                dve.tensor_tensor(two, bank2(u)[:, :, 0:T], two, ALU.add).then_inc(x_added, 1)
                dve.wait_ge(x_added, l * X_ADDS + n + 1)
                dve.tensor_tensor(two, bank2(u)[:, :, T:2 * T], two, ALU.add).then_inc(unit_free, 1)

            def norm(l, which):
                col = G_FFN if which else G_ATTN
                dve.wait_ge(norm_root.sem, norm_root.at(l, which + 1))
                dve.reciprocal(rs[:, 0:T], rs[:, 0:T]).then_inc(norm_scale.sem, 1)
                dve.wait_ge(norm_scale.sem, norm_scale.at(l, which + 1))
                for i in range(8):
                    for j in range(2):
                        dve.scalar_tensor_tensor(htmp[:, i % 2, j, :], xT[:, 2 * i + j, :], gain(col + 2 * i + j),
                                                 rs[:, 0:T], ALU.mult, ALU.mult).then_inc(h_scaled.sem, 1)
                    dve.wait_ge(h_high.sem, h_high.at(l, 8 * which + i + 1))
                    dve.tensor_tensor(hx[:, 2 * i:2 * i + 2, T:2 * T], htmp[:, i % 2, :, :],
                                      hx[:, 2 * i:2 * i + 2, 0:T].bitcast(F32), ALU.subtract).then_inc(h_ready.sem, 1)

            def up(l, g, par, r, k, ur, u):
                turn = l * NG + g
                if k > K_FFN:
                    dve.wait_ge(mid_ready.sem, mid_ready.at(turn, 0))
                dve.tensor_copy(conv_p[:, :, :, :], conv_all[:, bass.ds(l, 1), :, :, bass.ds(g * GROUP, GROUP)]
                                .rearrange("p o j s f -> p (o j) s f")).then_inc(taps_set.sem, 1)
                for s in range(8):
                    split(r, k + s + 2)
                    if s % 2 == 0:
                        continue
                    f, side = s // 4, s // 2 % 2
                    ub, y = ubuf[side], (yg, yu)[side]
                    un = u + s // 2
                    dve.wait_ge(half_copied, l * HALF_COPIES + g * 4 + (H_FFN + s // 2 + 1))
                    if s == 5:
                        dve.wait_ge(mid_ready.sem, mid_ready.at(turn, 1))
                    add_halves(un, ub[:, :, CONV - 1:CONV - 1 + T])
                    dve.wait_ge(unit_free, ur * 2 + un + 3)
                    if s == 1:
                        dve.wait_ge(taps_set.sem, taps_set.at(turn, 1))
                    step = 12 * f + 6 * side
                    for n, j in enumerate((2, 1, 0)):
                        if n:
                            dve.wait_ge(conv_step.sem, conv_step.at(turn, step + 2 * n))
                        for i in range(2):
                            tap = conv_p[:, j, side, 2 * f + i:2 * f + i + 1]
                            if n == 0:
                                dve.tensor_scalar(y[:, i, :], ub[:, i, j:j + T], tap,
                                                  conv_p[:, CONV, side, 2 * f + i:2 * f + i + 1],
                                                  ALU.mult, ALU.add).then_inc(conv_step.sem, 1)
                            else:
                                dve.scalar_tensor_tensor(y[:, i, :], ub[:, i, j:j + T], tap, y[:, i, :],
                                                         ALU.mult, ALU.add).then_inc(conv_step.sem, 1)
                    if side == 1:
                        dve.wait_ge(conv_step.sem, conv_step.at(turn, 12 * f + 12))
                        dve.wait_ge(gate_done.sem, gate_done.at(turn, f + 1))
                        dve.tensor_tensor(yu, yg, yu, ALU.mult).then_inc(product_done.sem, 1)
                        m = GROUP * par + 2 * f
                        dve.wait_ge(mid_high.sem, mid_high.at(turn, f + 1))
                        dve.tensor_tensor(mid[:, m:m + 2, T:2 * T], yu, mid[:, m:m + 2, 0:T].bitcast(F32),
                                          ALU.subtract).then_inc(mid_ready.sem, 1)

            def down(l, g, par, r, k, ur, u):
                for q in range(4):
                    if k + q + 2 < CHUNKS:
                        split(r, k + q + 2)
                    for i in range(2):
                        if i == 0:
                            dve.wait_ge(unit_done, l * MID_UNITS + g * 4 + (8 + q + 1))
                        else:
                            dve.wait_ge(slot_free, r * SLOTS + (k + q + 1 + SLOTS))
                        add_to_x(l, u + 2 * q + i, g * 8 + (8 + 2 * q + i), 4 * q + 2 * i)

            dve.sem_inc(lo_ready, SLOTS)
            dve.sem_inc(unit_free, 2)
            dve.memset(zm[64:96, :], 1.0).then_inc(zeroed, 1)
            dve.wait_ge(zeroed, 1)
            for s in range(8):
                dve.wait_ge(x_turned, s + 1)
                dve.tensor_copy(xT[:, 2 * s:2 * s + 2, :], X[:, s % 4, :].rearrange("p (a t) -> p a t", a=2)).then_inc(x_copied, 1)
            for l in range(DEPTH):
                dve.wait_ge(rows_turned, l + 1)
                dve.tensor_copy(params_all[:, l, :], G[:, l, 0:PARAMS]).then_inc(rows_copied, 1)
            dve.wait_ge(rows_landed, ROW_LOADS * 16)
            dve.wait_ge(const_landed, 16)
            dve.tensor_copy(rs[:, 0:T], cos[:, :].bitcast(I32)).then_inc(angle_step, 1)
            dve.wait_ge(angle_step, 1)
            dve.tensor_scalar(sin[:, :], rs[:, 0:T], freq, None, ALU.mult).then_inc(angle_step, 1)
            dve.wait_ge(angle_step, 2)
            dve.tensor_scalar(rs[:, T:2 * T], sin[:, :], 1.0 / TWO_PI, ROUNDER, ALU.mult, ALU.add).then_inc(angle_step, 1)
            dve.wait_ge(angle_step, 3)
            dve.tensor_scalar(rs[:, T:2 * T], rs[:, T:2 * T], ROUNDER, None, ALU.subtract).then_inc(angle_step, 1)
            dve.wait_ge(angle_step, 4)
            for i, part in enumerate(TURN_PARTS):
                dve.scalar_tensor_tensor(sin[:, :], rs[:, T:2 * T], -part, sin[:, :], ALU.mult, ALU.add).then_inc(angle_step, 1)
                dve.wait_ge(angle_step, 5 + i)
            dve.tensor_scalar(sin[:, :], sin[:, :], NEARLY_PI, -NEARLY_PI, ALU.min, ALU.max).then_inc(angle_small, 1)
            dve.wait_ge(table_step, 1)
            dve.tensor_scalar(rs[:, T:2 * T], rs[:, 0:T], -1.0, TWO_PI / 4, ALU.mult, ALU.add).then_inc(angle_small, 1)
            dve.wait_ge(rows_copied, DEPTH)
            dve.wait_ge(x_copied, 8)
            dve.wait_ge(table_step, 3)

            with dve.Fori(0, DEPTH) as l:
                r, ur = l * ROUNDS, l * PAIRS
                dve.tensor_copy(gains[:, :], params_all[:, bass.ds(l, 1), 0:GAINS]
                                .rearrange("p o g -> p (o g)")).then_inc(params_set.sem, 1)
                dve.wait_ge(params_set.sem, params_set.at(l, 1))
                split(r, 0)
                split(r, 1)
                norm(l, 0)
                for j in range(3):
                    for q in range(4):
                        split(r, K_TOK + 4 * j + q + 2)
                    dve.wait_ge(slot_free, r * SLOTS + K_TOK + 4 * j + 4 + SLOTS)
                    dst = gk if j == 0 else gv[:, :, 512 * (j - 1):512 * j]
                    dve.tensor_copy(dst, bank2(U_TOK + j)).then_inc(unit_free, 1)
                for s in range(2):
                    split(r, K_MISC + s + 2)
                dve.wait_ge(misc_half.sem, misc_half.at(l, 1))
                dve.tensor_tensor(zm[0:80, :], X[0:80, 1, 0:T], rs[0:80, 0:T], ALU.add).then_inc(misc_ready.sem, 1)
                for i in range(9):
                    split(r, K_FEAT + 2 * i + 2)
                    split(r, K_FEAT + 2 * i + 3)
                    dve.wait_ge(half_copied, l * HALF_COPIES + H_FEAT + i + 1)
                    add_halves(U_FEAT + i, z[:, 2 * i:2 * i + 2, :])
                dve.wait_ge(c_root.sem, c_root.at(l, 2))
                dve.reciprocal(rs[:, :], rs[:, :]).then_inc(c_scale.sem, 1)
                dve.wait_ge(c_scale.sem, c_scale.at(l, 1))
                for i in range(6):
                    tile = z[:, Z_CQ + i, :]
                    dve.scalar_tensor_tensor(tile, tile, gain(G_CQ + i), rs[:, 0:T] if i < 4 else rs[:, T:2 * T],
                                             ALU.mult, ALU.mult).then_inc(c_scaled.sem, 1)
                for i in range(3):
                    dve.wait_ge(c_high.sem, c_high.at(l, i + 1))
                    dve.tensor_tensor(mid[:, 2 * i:2 * i + 2, T:2 * T], z[:, Z_CQ + 2 * i:Z_CQ + 2 * i + 2, :],
                                      mid[:, 2 * i:2 * i + 2, 0:T].bitcast(F32), ALU.subtract).then_inc(c_ready.sem, 1)
                dve.wait_ge(gate_soft.sem, gate_soft.at(l, 3))
                dve.scalar_tensor_tensor(la, X[:, 2:4, :], 0.0, la, ALU.min, ALU.subtract).then_inc(gate_log.sem, 1)
                dve.wait_ge(gate_decay.sem, gate_decay.at(l, 1))
                dve.tensor_tensor(gk, gk, la, ALU.mult).then_inc(keys_decayed.sem, 1)
                dve.wait_ge(gate_decay.sem, gate_decay.at(l, 2))

                def state_step(n):
                    dve.wait_ge(update_done.sem, update_done.at(l, n + 1))
                    if n >= 1:
                        dve.wait_ge(reads_done.sem, reads_done.at(l, n))
                        dve.wait_ge(state_ready.sem, state_ready.at(l, 4 * n))
                    for h in range(GH):
                        new = X[:, h // 2, (h % 2) * GDV:(h % 2 + 1) * GDV]
                        if n == 0:
                            dve.tensor_copy(state[:, h, :], new).then_inc(state_ready.sem, 1)
                        else:
                            dve.scalar_tensor_tensor(state[:, h, :], state[:, h, :], decay[:, 4 * h + n:4 * h + n + 1],
                                                     new, ALU.mult, ALU.add).then_inc(state_ready.sem, 1)

                for n in range(T // CHUNK):
                    state_step(n)
                    dve.wait_ge(reads_done.sem, reads_done.at(l, n + 1))
                    o_chunk = oT.rearrange("p e (h t) -> p h e t", h=GH)[:, :, :, n * CHUNK:(n + 1) * CHUNK]
                    dve.tensor_scalar(o_chunk, X[:, 2 + n % 2, :].rearrange("p (h e t) -> p h e t", h=GH, e=2),
                                      GDK ** -0.5, None, ALU.mult).then_inc(reads_copied.sem, 1)
                for h in range(GH):
                    s = rs[:, (h % 2) * T:(h % 2 + 1) * T]
                    dve.wait_ge(o_root.sem, o_root.at(l, h + 1))
                    dve.reciprocal(s, s).then_inc(o_scale.sem, 1)
                    dve.wait_ge(o_scale.sem, o_scale.at(l, h + 1))
                    for e in range(2):
                        o = oT[:, e, h * T:(h + 1) * T]
                        dve.scalar_tensor_tensor(o, o, gain(G_GLA + e), s, ALU.mult, ALU.mult).then_inc(o_scaled.sem, 1)
                    dve.wait_ge(o_scaled.sem, o_scaled.at(l, 2 * h + 2))
                    if h == 0:
                        dve.wait_ge(g_silu.sem, g_silu.at(l, 1))
                    o = oT[:, :, h * T:(h + 1) * T]
                    dve.tensor_tensor(o, o, z[:, Z_G + 2 * h:Z_G + 2 * h + 2, :], ALU.mult).then_inc(o_gated.sem, 1)
                for h in range(GH):
                    m = 8 + 2 * h
                    dve.wait_ge(o_high.sem, o_high.at(l, h + 1))
                    dve.tensor_tensor(hx[:, m:m + 2, T:2 * T], oT[:, :, h * T:(h + 1) * T],
                                      hx[:, m:m + 2, 0:T].bitcast(F32), ALU.subtract).then_inc(o_ready.sem, 1)
                dve.wait_ge(o_ready.sem, o_ready.at(l, GH))
                for j in range(4):
                    split(r, K_UQ + j + 2)
                    dve.wait_ge(half_copied, l * HALF_COPIES + H_UQ + 2 * j + 1)
                    add_halves(U_UQ + 2 * j, qkn[:, 2 * j:2 * j + 2, :])
                    dve.wait_ge(half_copied, l * HALF_COPIES + H_UQ + 2 * j + 2)
                    add_halves(U_UQ + 2 * j + 1, qkr[:, j:j + 1, :], 1)
                for j in range(2):
                    split(r, K_UKV + j + 2)
                    for i in range(2):
                        dve.wait_ge(half_copied, l * HALF_COPIES + H_UKV + 2 * j + i + 1)
                        add_halves(U_UKV + 3 * j + i, qkn[:, 8 + 4 * j + 2 * i:10 + 4 * j + 2 * i, :])
                    dve.wait_ge(slot_free, r * SLOTS + K_UKV + j + 1 + SLOTS)
                    dve.tensor_copy(v[:, :, 512 * j:512 * j + 512], bank2(U_UKV + 3 * j + 2)).then_inc(unit_free, 1)

                def rope(j):
                    dve.wait_ge(rope_turned.sem, rope_turned.at(l, j + 1))
                    dve.tensor_tensor(rope_tmp[:, j % 2, :], X[:, 2 + j % 2, 0:T], sin[:, :],
                                      ALU.mult).then_inc(rope_parts.sem, 1)
                    dve.tensor_tensor(qkr[:, j, :], qkr[:, j, :], cos[:, :], ALU.mult).then_inc(rope_parts.sem, 1)
                    dve.wait_ge(rope_parts.sem, rope_parts.at(l, 2 * j + 2))
                    dve.tensor_tensor(qkr[:, j, :], qkr[:, j, :], rope_tmp[:, j % 2, :], ALU.add).then_inc(rope_done.sem, 1)

                for j in range(8):
                    gn, gr = (G_QN, G_QR) if j < 4 else (G_KN, G_KR)
                    dve.wait_ge(qk_root.sem, qk_root.at(l, j + 1))
                    dve.reciprocal(rs[:, :], rs[:, :]).then_inc(qk_scale.sem, 1)
                    dve.wait_ge(qk_scale.sem, qk_scale.at(l, j + 1))
                    two = qkn[:, 2 * j:2 * j + 2, :]
                    dve.scalar_tensor_tensor(two, two, gain(gn), rs[:, :].rearrange("p (a t) -> p a t", a=2),
                                             ALU.mult, ALU.mult).then_inc(qk_normed.sem, 1)
                    for i in range(2):
                        lanes = slice(64 * i, 64 * i + 64)
                        one = qkr[lanes, j, :]
                        dve.scalar_tensor_tensor(one, one, gains[lanes, gr:gr + 1], rs[lanes, i * T:(i + 1) * T],
                                                 ALU.mult, ALU.mult).then_inc(qk_normed.sem, 1)
                    if j >= 1:
                        rope(j - 1)
                rope(7)

                def find_top(h):
                    dve.wait_ge(scores_done.sem, scores_done.at(l, h + 1))
                    dve.memset(X[0:CHUNK, h % 2, P - CHUNK:P], NEG).then_inc(scores_masked.sem, 1)
                    dve.memset(X[0:CHUNK, h % 2, 3 * P - CHUNK:3 * P], NEG).then_inc(scores_masked.sem, 1)
                    dve.wait_ge(scores_masked.sem, scores_masked.at(l, 2 * h + 2))
                    at = 2 * (h % 2)
                    dve.tensor_reduce(top[:, at:at + 1], X[:, h % 2, 0:P], AX_X, ALU.max).then_inc(tops_found.sem, 1)
                    dve.tensor_reduce(top[:, at + 1:at + 2], X[:, h % 2, P:3 * P], AX_X, ALU.max).then_inc(tops_found.sem, 1)
                    dve.wait_ge(tops_found.sem, tops_found.at(l, 2 * h + 2))
                    dve.tensor_scalar(ntop[:, at:at + 2], top[:, at:at + 2], -QK ** -0.5, None, ALU.mult).then_inc(tops_scaled.sem, 1)

                def copy_values(h):
                    dve.wait_ge(values_done.sem, values_done.at(l, h + 1))
                    dve.tensor_copy(qkn[:, h, :], X[:, 3, 0:T]).then_inc(values_copied.sem, 1)

                find_top(0)
                for h in range(HEADS):
                    if h + 1 < HEADS:
                        find_top(h + 1)
                    at = 2 * (h % 2)
                    dve.wait_ge(exps_done.sem, exps_done.at(l, 2 * h + 2))
                    dve.reciprocal(rsum[:, at:at + 2], sums[:, at:at + 2]).then_inc(sums_inverted.sem, 1)
                    dve.wait_ge(sums_inverted.sem, sums_inverted.at(l, h + 1))
                    for b in range(TT):
                        part = prob[:, h % 2, 0:P] if b == 0 else prob[:, h % 2, P:3 * P]
                        dve.tensor_scalar(part, part, rsum[:, at + b:at + b + 1], None, ALU.mult).then_inc(probs_ready.sem, 1)
                    if h >= 1:
                        copy_values(h - 1)
                copy_values(HEADS - 1)
                dve.wait_ge(a_root.sem, a_root.at(l, 1))
                dve.reciprocal(rs[:, 0:T], rs[:, 0:T]).then_inc(a_scale.sem, 1)
                dve.wait_ge(a_scale.sem, a_scale.at(l, 1))
                for h in range(HEADS):
                    dve.scalar_tensor_tensor(qkn[:, h, :], qkn[:, h, :], gain(G_MLA + h), rs[:, 0:T],
                                             ALU.mult, ALU.mult).then_inc(a_scaled.sem, 1)
                for i in range(4):
                    dve.wait_ge(a_high.sem, a_high.at(l, i + 1))
                    dve.tensor_tensor(hx[:, 2 * i:2 * i + 2, T:2 * T], qkn[:, 2 * i:2 * i + 2, :],
                                      hx[:, 2 * i:2 * i + 2, 0:T].bitcast(F32), ALU.subtract).then_inc(a_ready.sem, 1)
                for i in range(8):
                    split(r, K_OUT + 2 * i + 2)
                    split(r, K_OUT + 2 * i + 3)
                    dve.wait_ge(slot_free, r * SLOTS + K_OUT + 2 * i + 2 + SLOTS)
                    add_to_x(l, U_OUT + i, i, 2 * i)
                for side in range(2):
                    dve.memset(ubuf[side][:, :, 0:CONV - 1], 0.0).then_inc(pads_zeroed.sem, 1)
                dve.wait_ge(pads_zeroed.sem, pads_zeroed.at(l, 2))
                dve.wait_ge(unit_free, l * UNITS + U_FFN + 2)
                norm(l, 1)
                mlp_order(dve, l, up, down)
                dve.wait_ge(unit_free, l * UNITS + UNITS + 2)
            for n in range(8):
                dve.wait_ge(out_turned, n + 1)
                dve.tensor_copy(xtok[n // 4][:, (n % 4) * 512:(n % 4 + 1) * 512], X[:, n % 4, :]).then_inc(out_copied, 1)

        @block.tensor
        def _(pe):
            def take(r, k):
                pe.wait_ge(lo_ready, r * SLOTS + (k + 1 + SLOTS))
                return hi[:, k % SLOTS, :], lo[:, k % SLOTS, :]

            def tile_pass(bank, w_hi, w_lo, x2, first, last):
                pe.matmul(bank, w_hi, x2, start=first, stop=False)
                return pe.matmul(bank[:, T:2 * T], w_lo, x2[:, 0:T], start=False, stop=last)

            def pair_half(r, k, u, half_of_k, src, h_from=None, l=None):
                w_hi, w_lo = take(r, k)
                for i in range(2):
                    for a in range(8):
                        kt = 8 * half_of_k + a
                        if h_from is not None and i == 0 and a % 2 == 0:
                            pe.wait_ge(h_ready.sem, h_ready.at(l, h_from + kt // 2 + 1))
                        at = a * 256 + i * P
                        mm = tile_pass(bank2(u)[:, i, :], w_hi[:, at:at + P], w_lo[:, at:at + P],
                                       src[:, kt, :], kt == 0, kt == KT - 1)
                mm.then_inc(slot_free, 1)

            def up(l, g, par, r, k, ur, u):
                first = k == K_FFN
                for s in range(8):
                    un = u + s // 2
                    if s % 2 == 0:
                        pe.wait_ge(unit_free, ur * 2 + un + 1)
                    pair_half(r, k + s, un, s % 2, hx, 8 if first and s < 2 else None, l)

            def down(l, g, par, r, k, ur, u):
                pe.wait_ge(mid_ready.sem, mid_ready.at(l * NG + g, 2))
                for q in range(4):
                    w_hi, w_lo = take(r, k + q)
                    for i in range(4):
                        un = u + 2 * q + i // 2
                        if i % 2 == 0:
                            pe.wait_ge(unit_free, ur * 2 + un + 1)
                        for a in range(GROUP):
                            at = a * 512 + i * P
                            mm = tile_pass(bank2(un)[:, i % 2, :], w_hi[:, at:at + P], w_lo[:, at:at + P],
                                           mid[:, GROUP * par + a, :], a == 0, a == GROUP - 1)
                        if i == 1:
                            mm.then_inc(unit_done, 1)
                    mm.then_inc(slot_free, 1)

            pe.sem_inc(slot_free, SLOTS)
            pe.wait_ge(const_landed, 16)
            pe.wait_ge(x_landed, 32)
            for s in range(8):
                if s >= 4:
                    pe.wait_ge(x_copied, s - 3)
                for j in range(2):
                    for i in range(TT):
                        mm = pe.transpose(X[:, s % 4, j * T + i * P:j * T + (i + 1) * P],
                                          xtok[i][:, (2 * s + j) * P:(2 * s + j + 1) * P], ident)
                mm.then_inc(x_turned, 1)
            pe.wait_ge(rows_landed, ROW_LOADS * 16)
            for l in range(DEPTH):
                pe.transpose(G[:, l, 0:GAINS], rows[0:GAINS, l * P:(l + 1) * P], ident[0:GAINS, 0:GAINS])
                for j in range(CONV + 1):
                    at = (DEPTH + l * (CONV + 1) + j) * P
                    mm = pe.transpose(G[:, l, GAINS + j * FT2:GAINS + (j + 1) * FT2], rows[0:FT2, at:at + P],
                                      ident[0:FT2, 0:FT2])
                mm.then_inc(rows_turned, 1)
            pe.wait_ge(rows_copied, DEPTH)
            pe.wait_ge(x_copied, 8)

            with pe.Fori(0, DEPTH) as l:
                r, ur = l * ROUNDS, l * PAIRS

                def norm_sums(which):
                    for i in range(8):
                        pe.wait_ge(norm_squared.sem, norm_squared.at(l, 8 * which + i + 1))
                        for j in range(2):
                            mm = pe.matmul(X[:, which, 0:T], ones, sq[:, i % 2, j, :], start=i + j == 0, stop=i + j == 8)
                        mm.then_inc(norm_square_used.sem, 1)

                norm_sums(0)
                for j in range(3):
                    pe.wait_ge(unit_free, ur * 2 + U_TOK + j + 1)
                    for q in range(4):
                        w_hi, w_lo = take(r, K_TOK + 4 * j + q)
                        for a in range(4):
                            kt = 4 * q + a
                            if j == 0 and a % 2 == 0:
                                pe.wait_ge(h_ready.sem, h_ready.at(l, kt // 2 + 1))
                            for i in range(TT):
                                x_hi, x_lo = (hx[:, kt, b * T + i * P:b * T + (i + 1) * P] for b in range(2))
                                bank = bank2(U_TOK + j)[:, i, :]
                                pe.matmul(bank, x_hi, w_hi[:, 512 * a:512 * a + 512], start=kt == 0, stop=False)
                                pe.matmul(bank, x_lo, w_hi[:, 512 * a:512 * a + 512], start=False, stop=False)
                                mm = pe.matmul(bank, x_hi, w_lo[:, 512 * a:512 * a + 512], start=False, stop=kt == KT - 1)
                        mm.then_inc(slot_free, 1)
                for h in range(2):
                    w_hi, w_lo = take(r, K_MISC + h)
                    for a in range(8):
                        kt = 8 * h + a
                        mm = tile_pass(X[0:80, 1, :], w_hi[:, 80 * a:80 * a + 80], w_lo[:, 80 * a:80 * a + 80],
                                       hx[:, kt, :], kt == 0, kt == KT - 1)
                    mm.then_inc(slot_free, 1)
                for i in range(9):
                    pe.wait_ge(unit_free, ur * 2 + U_FEAT + i + 1)
                    for h in range(2):
                        pair_half(r, K_FEAT + 2 * i + h, U_FEAT + i, h, hx)
                for i in range(3):
                    pe.wait_ge(c_squared.sem, c_squared.at(l, i + 1))
                    for j in range(2):
                        mm = pe.matmul(X[:, 0, 0:T] if i < 2 else X[:, 0, T:2 * T], ones, sq[:, i % 2, j, :],
                                       start=i != 1 and j == 0, stop=i != 0 and j == 1)
                    mm.then_inc(c_square_used.sem, 1)
                pe.wait_ge(misc_ready.sem, misc_ready.at(l, 1))
                pe.wait_ge(gate_landed.sem, gate_landed.at(l, 32))
                for i in range(TT):
                    mm = pe.matmul(X[:, 2 + i, :], zm[64:64 + RANK + 1, i * P:(i + 1) * P], wg[64:64 + RANK + 1, :],
                                   start=True, stop=True)
                mm.then_inc(gate_logits.sem, 1)
                pe.wait_ge(gate_log.sem, gate_log.at(l, 1))
                for i in range(TT):
                    pe.matmul(X[:, 2 + i, :], suf, la[:, i, :], start=True, stop=True)
                for h in range(GH):
                    for i in range(TT):
                        mm = pe.matmul(X[:, 1, 4 * h + 2 * i:4 * h + 2 * i + 2], la[:, i, h * GDK:(h + 1) * GDK], ind,
                                       start=True, stop=True)
                mm.then_inc(gate_sums.sem, 1)

                def update(n):
                    lanes, i = slice(64 * (n % 2), 64 * (n % 2) + 64), n // 2
                    for h in range(GH):
                        mm = pe.matmul(X[:, h // 2, (h % 2) * GDV:(h % 2 + 1) * GDV], gk[lanes, i, h * GDK:(h + 1) * GDK],
                                       gv[lanes, i, h * GDV:(h + 1) * GDV], start=True, stop=True)
                    mm.then_inc(update_done.sem, 1)

                pe.wait_ge(keys_decayed.sem, keys_decayed.at(l, 1))
                pe.wait_ge(gate_decay.sem, gate_decay.at(l, 2))
                pe.wait_ge(c_root.sem, c_root.at(l, 2))
                update(0)
                for n in range(T // CHUNK):
                    pe.wait_ge(state_ready.sem, state_ready.at(l, 4 * n + 4))
                    if n + 1 < T // CHUNK:
                        update(n + 1)
                    if n >= 2:
                        pe.wait_ge(reads_copied.sem, reads_copied.at(l, n - 1))
                    for h in range(GH):
                        for e in range(2):
                            mm = pe.matmul(X[:, 2 + n % 2, (2 * h + e) * CHUNK:(2 * h + e + 1) * CHUNK],
                                           state[:, h, e * P:(e + 1) * P], z[:, Z_GQ + h, n * CHUNK:(n + 1) * CHUNK],
                                           start=True, stop=True)
                    mm.then_inc(reads_done.sem, 1)
                pe.wait_ge(reads_copied.sem, reads_copied.at(l, 4))
                for h in range(GH):
                    pe.wait_ge(o_squared.sem, o_squared.at(l, h + 1))
                    for e in range(2):
                        mm = pe.matmul(X[:, h, 0:T], ones, sq[:, h % 2, e, :],
                                       start=e == 0, stop=e == 1)
                    mm.then_inc(o_summed.sem, 1)
                pe.wait_ge(c_ready.sem, c_ready.at(l, 3))
                for j in range(4):
                    w_hi, w_lo = take(r, K_UQ + j)
                    for i in range(3):
                        un = U_UQ + 2 * j + i // 2
                        if i != 1:
                            pe.wait_ge(unit_free, ur * 2 + un + 1)
                        for a in range(4):
                            at = a * 384 + i * P
                            mm = tile_pass(bank2(un)[:, i % 2, :], w_hi[:, at:at + P], w_lo[:, at:at + P],
                                           mid[:, a, :], a == 0, a == 3)
                        if i == 1:
                            mm.then_inc(unit_done, 1)
                    mm.then_inc(slot_free, 1)
                for j in range(2):
                    w_hi, w_lo = take(r, K_UKV + j)
                    for i in range(4):
                        un = U_UKV + 3 * j + i // 2
                        if i % 2 == 0:
                            pe.wait_ge(unit_free, ur * 2 + un + 1)
                        for a in range(2):
                            at = a * 1024 + i * 256
                            mm = tile_pass(bank2(un)[:, i % 2, :], w_hi[:, at:at + P], w_lo[:, at:at + P],
                                           mid[:, 4 + a, :], a == 0, a == 1)
                        if i % 2:
                            mm.then_inc(unit_done, 1)
                    un = U_UKV + 3 * j + 2
                    pe.wait_ge(unit_free, ur * 2 + un + 1)
                    for a in range(2):
                        wv_hi, wv_lo = (w[:, a * 1024:(a + 1) * 1024].rearrange("p (h c) -> p h c", h=4)[:, :, NOPE:]
                                        for w in (w_hi, w_lo))
                        for i in range(TT):
                            x_hi, x_lo = (mid[:, 4 + a, b * T + i * P:b * T + (i + 1) * P] for b in range(2))
                            bank = bank2(un)[:, i, :].rearrange("p (h c) -> p h c", h=4)
                            pe.matmul(bank, x_hi, wv_hi, start=a == 0, stop=False)
                            pe.matmul(bank, x_lo, wv_hi, start=False, stop=False)
                            mm = pe.matmul(bank, x_hi, wv_lo, start=False, stop=a == 1)
                    mm.then_inc(slot_free, 1)

                def exchange(j):
                    pe.wait_ge(qk_normed.sem, qk_normed.at(l, 3 * j + 3))
                    if j >= 2:
                        pe.wait_ge(rope_parts.sem, rope_parts.at(l, 2 * j - 2))
                    pe.matmul(X[:, 2 + j % 2, 0:T], rot, qkr[:, j, :], start=True, stop=True).then_inc(rope_turned.sem, 1)

                pe.wait_ge(o_root.sem, o_root.at(l, 4))
                for j in range(8):
                    pe.wait_ge(qk_squared.sem, qk_squared.at(l, 2 * j + 2))
                    if j >= 2:
                        pe.wait_ge(qk_root.sem, qk_root.at(l, j - 1))
                    for i in range(2):
                        where = X[:, j % 2, i * T:(i + 1) * T]
                        pe.matmul(where, ones, sq[:, 0, i, :], start=True, stop=False)
                        mm = pe.matmul(where, sel[i], sq[:, 1, 0, :], start=False, stop=True)
                    mm.then_inc(qk_summed.sem, 1)
                    if j >= 1:
                        exchange(j - 1)
                exchange(7)

                def scores(h):
                    if h >= 2:
                        pe.wait_ge(exps_done.sem, exps_done.at(l, 2 * h - 2))
                    lanes = slice(64 * (h % 2), 64 * (h % 2) + 64)
                    for b in range(TT):
                        where = X[:, h % 2, 0:P] if b == 0 else X[:, h % 2, P:3 * P]
                        qs, ks = slice(b * P, (b + 1) * P), slice(0, (b + 1) * P)
                        pe.matmul(where, qkn[:, h, qs], qkn[:, 8 + h, ks], start=True, stop=False)
                        mm = pe.matmul(where, qkr[lanes, h // 2, qs], qkr[lanes, 4 + h // 2, ks], start=False, stop=True)
                    mm.then_inc(scores_done.sem, 1)

                pe.wait_ge(rope_done.sem, rope_done.at(l, 8))
                pe.wait_ge(qk_root.sem, qk_root.at(l, 8))
                scores(0)
                scores(1)
                for h in range(HEADS):
                    pe.wait_ge(probs_ready.sem, probs_ready.at(l, 2 * h + 2))
                    if h >= 1:
                        pe.wait_ge(probs_copied.sem, probs_copied.at(l, h))
                    for i in range(3):
                        mm = pe.transpose(X[:, 2, i * P:(i + 1) * P], prob[:, h % 2, i * P:(i + 1) * P], ident)
                    mm.then_inc(probs_turned.sem, 1)
                    if h + 2 < HEADS:
                        scores(h + 2)
                    pe.wait_ge(probs_copied.sem, probs_copied.at(l, h + 1))
                    if h >= 1:
                        pe.wait_ge(values_copied.sem, values_copied.at(l, h))
                    turned = probT[:, h % 2, :]
                    pe.matmul(X[:, 3, 0:T], v[:, 0, h * VD:(h + 1) * VD], turned[:, 0:T], start=True, stop=False)
                    pe.matmul(X[:, 3, P:T], v[:, 1, h * VD:(h + 1) * VD], turned[:, T:T + P], start=False,
                              stop=True).then_inc(values_done.sem, 1)
                for i in range(4):
                    pe.wait_ge(a_squared.sem, a_squared.at(l, i + 1))
                    for j in range(2):
                        mm = pe.matmul(X[:, 0, 0:T], ones, sq[:, i % 2, j, :], start=i + j == 0, stop=i + j == 4)
                    mm.then_inc(a_square_used.sem, 1)
                pe.wait_ge(a_ready.sem, a_ready.at(l, 4))
                pe.wait_ge(o_ready.sem, o_ready.at(l, 4))
                for i in range(8):
                    pe.wait_ge(unit_free, ur * 2 + U_OUT + i + 1)
                    for h in range(2):
                        pair_half(r, K_OUT + 2 * i + h, U_OUT + i, h, hx)
                norm_sums(1)
                mlp_order(pe, l, up, down)
                pe.wait_ge(unit_free, l * UNITS + UNITS + 2)
            for n in range(8):
                if n >= 4:
                    pe.wait_ge(out_copied, n - 3)
                for i in range(4):
                    mm = pe.transpose(X[:, n % 4, i * P:(i + 1) * P],
                                      xT[:, 4 * (n % 4) + i, (n // 4) * P:(n // 4 + 1) * P], ident)
                mm.then_inc(out_turned, 1)


def shape_constants():
    c = np.zeros((P, CONSTS), np.float32)
    at = np.arange(P)
    c[:, CO_ID:CO_ID + P] = np.eye(P)
    c[:, CO_ONES:CO_ONES + P] = 1
    for i in range(2):
        c[64 * i:64 * i + 64, CO_SEL + i * P:CO_SEL + (i + 1) * P] = 1
    c[:, CO_SUF:CO_SUF + P] = (at[:, None] > at[None, :]) & (at[:, None] // CHUNK == at[None, :] // CHUNK)
    for m in range(P):
        if m % ROPE < ROPE // 2:
            c[m + ROPE // 2, CO_ROT + m] = -1
        else:
            c[m - ROPE // 2, CO_ROT + m] = 1
    for i in range(2):
        c[64 * i:64 * i + 64, CO_IND + i] = 1
    c[:, CO_FREQ] = (ROPE_BASE ** (-(at % (ROPE // 2)) * 2.0 / ROPE)).astype(np.float32)
    c[:, CO_EPS] = EPS
    return c


def kernel(**inputs):
    import concourse.bacc as bacc
    from concourse.bass_utils import run_bass_kernel_spmd

    nc = bacc.Bacc("TRN2", target_bir_lowering=False, num_devices=1)
    arrays, aps = {}, {}
    for name, a in [*inputs.items(), ("consts", shape_constants())]:
        a = np.ascontiguousarray(a)
        arrays[f"in_{name}"] = a
        aps[name] = nc.dram_tensor(f"in_{name}", a.shape, mybir.dt.from_np(a.dtype), kind="ExternalInput").ap()
    out = nc.dram_tensor("out_0", (1, T, D), F32, kind="ExternalOutput").ap()
    trunk_program(nc, aps, out)
    r = run_bass_kernel_spmd(nc, [arrays], core_ids=[0])
    return r.results[0]["out_0"]
```

```python
from contextlib import ExitStack

import numpy as np

import concourse.bass as bass
from concourse import mybir

F32 = mybir.dt.float32
F32R = mybir.dt.float32r
I32 = mybir.dt.int32
ACT = mybir.ActivationFunctionType
ALU = mybir.AluOpType
AX_X = mybir.AxisListType.X

P = 128
T = 256
TT = T // P
D = 2048
KT = D // P
DEPTH = 2
EPS = 1e-6
NEG = -1e30

Q_LORA, KV_LORA, ROPE, NOPE, VD, HEADS = 512, 256, 64, 128, 128, 8
QK = NOPE + ROPE
GH, GDK, GDV, RANK, TAU, CHUNK = 4, 128, 256, 16, 16.0, 64
GK_W, GV_W = GH * GDK, GH * GDV
C_CQ, C_CKV = 0, Q_LORA
C_KR = C_CKV + KV_LORA
C_GQ = C_KR + ROPE
C_GK = C_GQ + GK_W
C_GV = C_GK + GK_W
C_A = C_GV + GV_W
C_G = C_A + RANK
D_FF = 5632
FT = D_FF // P
GROUP = 4
NG = FT // GROUP
CONV = 3

SLOTS = 3
WORDS = 2048

K_TOK = [0, 6, 10]
K_MISC = 4
K_FEAT = K_TOK[2] + 4
K_UQ = K_FEAT + 18
K_UKV = K_UQ + HEADS // 2
K_OUT = K_UKV + HEADS // 4
K_FFN = K_OUT + 16
GROUP_CHUNKS = 12
CHUNKS = K_FFN + NG * GROUP_CHUNKS
ROUNDS = CHUNKS // SLOTS
U_TOK = 0
U_FEAT = U_TOK + 3
U_UQ = U_FEAT + 9
U_UKV = U_UQ + HEADS
U_OUT = U_UKV + 6
U_FFN = U_OUT + 16
GROUP_UNITS = 12
UNITS = U_FFN + NG * GROUP_UNITS
PAIRS = UNITS // 2
assert CHUNKS % SLOTS == 0 and UNITS % 2 == 0 and K_FFN % SLOTS == 0 and U_FFN % 2 == 0

FEAT_COLS = [C_GQ, C_GQ + 256, C_CQ, C_CQ + 256, C_CKV, C_G, C_G + 256, C_G + 512, C_G + 768]
Z_GQ, Z_CQ, Z_CKV, Z_G = 0, 4, 8, 10
H_FEAT, H_UQ, H_UKV, H_FFN = 0, 9, 17, 21
HALF_COPIES = H_FFN + NG * 4
MID_UNITS = 8 + NG * 4
ROW_LOADS = DEPTH * 16 + 1
TWO_PI = 6.283185307179586
TURN_PARTS = (6.28125, 0.0019350051879882812, 3.01991598196686e-07)
NEARLY_PI = 3.1415925
ROUNDER = 12582912.0
ROPE_BASE = 10000.0

G_ATTN, G_FFN, G_CQ, G_CKV, G_MLA, G_GLA, G_QN, G_QR, G_KN, G_KR = 0, 16, 32, 36, 38, 46, 48, 49, 50, 51
GAINS = 52
FT2 = 2 * FT
PARAMS = GAINS + (CONV + 1) * FT2
CO_ID, CO_ONES, CO_SEL, CO_SUF, CO_ROT, CO_IND, CO_FREQ, CO_EPS, CO_EPSQ = 0, 128, 256, 512, 640, 768, 770, 771, 772
CONSTS = 773


class Signal:

    def __init__(self, sem, n):
        self.sem, self.n = sem, n

    def at(self, turn, count):
        return turn * self.n + count


def trunk_program(nc, t, out):
    with ExitStack() as ctx:
        def sb(name, shape, dt=F32):
            return ctx.enter_context(nc.sbuf_tensor(name, shape, dt))

        def semaphore(name):
            return ctx.enter_context(nc.semaphore(name))

        def signal(name, n):
            return Signal(semaphore(name), n)

        raw = sb("raw", [P, SLOTS, WORDS])
        hi = sb("hi", [P, SLOTS, WORDS], F32R)
        lo = sb("lo", [P, SLOTS, WORDS], F32R)
        xT = sb("xT", [P, KT, T])
        hx = sb("hx", [P, KT, 2 * T], F32R)
        mid = sb("mid", [P, 2 * GROUP, 2 * T], F32R)
        z = sb("z", [P, 18, T])
        zm = sb("zm", [P, T])
        qkn = sb("qkn", [P, 16, T])
        gv = sb("gv", [P, TT, GV_W])
        v = sb("v", [P, TT, HEADS * VD])
        half = sb("half", [P, 2, 2, T])
        sq = sb("sq", [P, 2, 2, T])
        gains = sb("gains", [P, GAINS])
        conv_p = sb("conv_p", [P, CONV + 1, 2, GROUP])
        params_all = sb("params_all", [P, DEPTH, PARAMS])
        cst = sb("cst", [P, CONSTS])
        cos = sb("cos", [P, T])
        sin = sb("sin", [P, T])
        wg = sb("wg", [P, GK_W])
        rs = sb("rs", [P, 2 * T])
        small = sb("small", [P, 66])

        xtok = [z[:, 0:8, :].rearrange("p a b -> p (a b)"), qkn[:, 0:8, :].rearrange("p a b -> p (a b)")]
        rows = gv[:, :, :].rearrange("p a b -> p (a b)")
        gk = qkn[:, 8:12, :].rearrange("p a b -> p (a b)").rearrange("p (t c) -> p t c", t=TT)
        la = qkn[:, 12:16, :].rearrange("p a b -> p (a b)").rearrange("p (t c) -> p t c", t=TT)
        state = v[:, 0, :].rearrange("p (h e) -> p h e", h=GH)
        oT = qkn[:, 0:8, :].rearrange("p (e h) t -> p e (h t)", e=2)
        qn = gv[:, :, :].rearrange("p a b -> p (a b)").rearrange("p (h t) -> p h t", t=T)
        kn = qkn[:, 8:16, :]
        rope_tmp = qkn[:, 0:2, :]
        diag = z[:, 12:14, :].rearrange("p a b -> p (a b)").rearrange("p (c t) -> p c t", t=P)
        sq_sum = z[:, 10:12, :]
        a_sq = z[:, 14:16, :]
        a_sum = z[:, 16, :]
        htmp = z[:, 0:4, :].rearrange("p (a b) t -> p a b t", a=2)
        qkr = z[:, 0:8, :]
        prob = half[:, :, :, :].rearrange("p a b t -> p a (b t)")
        probT = sq[:, :, :, :].rearrange("p a b t -> p a (b t)")
        vflat = v[:, :, :].rearrange("p a b -> p (a b)")
        yg = vflat[:, 0:512].rearrange("p (a t) -> p a t", a=2)
        yu = vflat[:, 512:1024].rearrange("p (a t) -> p a t", a=2)
        qkn_flat = qkn[:, :, :].rearrange("p a b -> p (a b)")
        ubuf = [x[:, 0:2 * (T + CONV - 1)].rearrange("p (a t) -> p a t", a=2) for x in (vflat[:, 1024:2048], qkn_flat)]

        conv_all = params_all[:, :, GAINS:PARAMS].rearrange("p l (j s f) -> p l j s f", j=CONV + 1, s=2)
        ident = cst[:, CO_ID:CO_ID + P]
        ones = cst[:, CO_ONES:CO_ONES + P]
        sel = [cst[:, CO_SEL + i * P:CO_SEL + (i + 1) * P] for i in range(2)]
        suf = cst[:, CO_SUF:CO_SUF + P]
        rot = cst[:, CO_ROT:CO_ROT + P]
        ind = cst[:, CO_IND:CO_IND + 2]
        freq = cst[:, CO_FREQ:CO_FREQ + 1]
        eps = cst[:, CO_EPS:CO_EPS + 1]
        eps_q = cst[:, CO_EPSQ:CO_EPSQ + 1]
        decay = small[:, 0:16]
        top = small[:, 16:20]
        ntop = small[:, 20:24]
        sums = small[:, 24:28]
        rsum = small[:, 28:32]
        norms = small[:, 32:64]
        gain_qk = small[:, 64:65]

        G = ctx.enter_context(nc.psum_tensor("G", [P, 4, 512], F32))
        X = ctx.enter_context(nc.psum_tensor("X", [P, 4, 512], F32))

        def gain(col):
            return gains[:, col:col + 1]

        def bank2(u):
            if u >= U_FFN and (u - U_FFN) % 4 >= 2:
                return X[:, 2 * (u % 2):2 * (u % 2) + 2, :]
            return G[:, 2 * (u % 2):2 * (u % 2) + 2, :]

        def head_parts(buf, k):
            rows = buf[:, k % SLOTS, 0:4 * 2 * QK].rearrange("p (a c) -> p a c", a=4)
            as_loaded = rows.rearrange("p a (h c) -> p a h c", h=2)
            for a, b in ((0, NOPE), (NOPE, QK)):
                used = rows[:, :, 2 * a:2 * b].rearrange("p a (h c) -> p a h c", h=2)
                yield used, as_loaded[:, :, :, a:b]

        raw_landed = [semaphore(f"raw_landed{s}") for s in range(SLOTS)]
        hi_ready = semaphore("hi_ready")
        lo_ready = semaphore("lo_ready")
        slot_free = semaphore("slot_free")
        unit_done = semaphore("unit_done")
        unit_free = semaphore("unit_free")
        half_copied = semaphore("half_copied")
        const_landed = semaphore("const_landed")
        rows_landed = semaphore("rows_landed")
        at_column_0 = semaphore("at_column_0")
        x_landed = semaphore("x_landed")
        zeroed = semaphore("zeroed")
        rows_turned = semaphore("rows_turned")
        rows_copied = semaphore("rows_copied")
        x_turned = semaphore("x_turned")
        x_copied = semaphore("x_copied")
        angle_step = semaphore("angle_step")
        angle_small = semaphore("angle_small")
        table_step = semaphore("table_step")
        out_turned = semaphore("out_turned")
        out_copied = semaphore("out_copied")
        out_stored = semaphore("out_stored")
        params_set = signal("params_set", 1)
        gate_landed = signal("gate_landed", 32)
        misc_landed = [signal(f"misc_landed{i}", 16) for i in range(2)]
        in_squared = signal("in_squared", 8)
        in_square_used = signal("in_square_used", 6)
        ff_squared = signal("ff_squared", 8)
        ff_square_used = signal("ff_square_used", 6)
        norm_summed = signal("norm_summed", 2)
        norm_root = signal("norm_root", 2)
        norm_scale = signal("norm_scale", 2)
        h_scaled = signal("h_scaled", 32)
        h_high = signal("h_high", 16)
        h_ready = signal("h_ready", 16)
        misc_done = signal("misc_done", 1)
        misc_half = signal("misc_half", 1)
        misc_ready = signal("misc_ready", 1)
        c_squared = signal("c_squared", 3)
        c_square_used = signal("c_square_used", 3)
        c_root = signal("c_root", 2)
        c_scale = signal("c_scale", 1)
        c_scaled = signal("c_scaled", 6)
        c_high = signal("c_high", 3)
        c_ready = signal("c_ready", 3)
        gate_logits = signal("gate_logits", 1)
        gate_soft = signal("gate_soft", 3)
        gate_log = signal("gate_log", 1)
        gate_sums = signal("gate_sums", 1)
        gate_decay = signal("gate_decay", 2)
        keys_decayed = signal("keys_decayed", 1)
        update_done = signal("update_done", 4)
        state_ready = signal("state_ready", 16)
        reads_done = signal("reads_done", 4)
        reads_copied = signal("reads_copied", 4)
        o_squared = signal("o_squared", 4)
        o_summed = signal("o_summed", 4)
        o_root = signal("o_root", 4)
        o_scale = signal("o_scale", 4)
        o_scaled = signal("o_scaled", 8)
        g_silu = signal("g_silu", 1)
        o_gated = signal("o_gated", 4)
        o_high = signal("o_high", 4)
        o_ready = signal("o_ready", 4)
        kr_spread = signal("kr_spread", 2)
        qk_squared = signal("qk_squared", 16)
        qk_summed = signal("qk_summed", 8)
        qk_root = signal("qk_root", 8)
        qk_inverse = signal("qk_inverse", 8)
        diag_ready = signal("diag_ready", 4)
        k_scale_spread = signal("k_scale_spread", 4)
        gains_joined = signal("gains_joined", 1)
        qk_normed = signal("qk_normed", 16)
        rope_turned = signal("rope_turned", 8)
        rope_parts = signal("rope_parts", 16)
        rope_done = signal("rope_done", 8)
        scores_done = signal("scores_done", HEADS)
        scores_masked = signal("scores_masked", 2 * HEADS)
        tops_found = signal("tops_found", 2 * HEADS)
        tops_scaled = signal("tops_scaled", HEADS)
        exps_done = signal("exps_done", 2 * HEADS)
        sums_inverted = signal("sums_inverted", HEADS)
        probs_ready = signal("probs_ready", 2 * HEADS)
        probs_turned = signal("probs_turned", HEADS)
        probs_copied = signal("probs_copied", HEADS)
        values_done = signal("values_done", HEADS)
        values_copied = signal("values_copied", HEADS)
        a_squared = signal("a_squared", HEADS)
        a_square_used = signal("a_square_used", 6)
        a_summed = signal("a_summed", 1)
        a_root = signal("a_root", 1)
        a_scale = signal("a_scale", 1)
        a_scaled = signal("a_scaled", 8)
        a_high = signal("a_high", 4)
        a_ready = signal("a_ready", 4)
        x_added = semaphore("x_added")
        pads_zeroed = signal("pads_zeroed", 2)
        X_ADDS = U_FFN - U_OUT + NG * 8
        taps_set = signal("taps_set", 1)
        conv_step = signal("conv_step", 24)
        gate_done = signal("gate_done", 2)
        product_done = signal("product_done", 2)
        mid_high = signal("mid_high", 2)
        mid_ready = signal("mid_ready", 2)

        w_in = t["w_in"].rearrange("l (k p) n -> l p k n", p=P)
        w_uq = t["w_uq"].rearrange("l (k p) n -> l p k n", p=P)
        w_ukv = t["w_ukv"].rearrange("l (k p) n -> l p k n", p=P)
        w_out = t["w_out"].rearrange("l (k p) n -> l p k n", p=P)
        w_up = t["w_up"].rearrange("l (k p) n -> l p k n", p=P)
        w_down = t["w_down"].rearrange("l (k p) n -> l p k n", p=P)

        TURN_ROUNDS, TURN_PAIRS = 2 * GROUP_CHUNKS // SLOTS, GROUP_UNITS

        def mlp_order(e, l, up, down):
            r0, p0 = l * ROUNDS, l * PAIRS
            up(l, 0, 0, r0, K_FFN, p0, U_FFN)
            with e.Fori(0, (NG - 1) // 2) as j:
                r, p = r0 + j * TURN_ROUNDS, p0 + j * TURN_PAIRS
                up(l, 2 * j + 1, 1, r, K_FFN + 8, p, U_FFN + 4)
                down(l, 2 * j, 0, r, K_FFN + 16, p, U_FFN + 8)
                up(l, 2 * j + 2, 0, r, K_FFN + 20, p, U_FFN + 16)
                down(l, 2 * j + 1, 1, r, K_FFN + 28, p, U_FFN + 20)
            down(l, NG - 1, 0, r0, CHUNKS - 4, p0, UNITS - 8)

        block = ctx.enter_context(nc.Block())

        @block.sync
        def _(sp):
            def load(r, k, shape, src, at_start=False):
                n = shape[0] * shape[1]
                dst = raw[:, k % SLOTS, 0:n].rearrange("p (a b) -> p a b", a=shape[0])
                sp.wait_ge(lo_ready, r * SLOTS + k + 1)
                if at_start:
                    sp.sem_inc(at_column_0, 1)
                sp.dma_start(dst, src.rearrange("o p k n -> p (o k) n")).then_inc(raw_landed[k % SLOTS], 16)

            sp.dma_start(cst[:, :], t["consts"]).then_inc(const_landed, 16)
            for i in range(TT):
                sp.dma_start(xtok[i], t["x"][0, i * P:(i + 1) * P, :]).then_inc(x_landed, 16)

            def row(l, at, n, src):
                sp.dma_start(rows[at:at + n, l * P:(l + 1) * P], src).then_inc(rows_landed, 16)

            for l in range(DEPTH):
                row(l, G_ATTN, 16, t["attn_norm"][l].rearrange("(a b) -> a b", b=P))
                row(l, G_FFN, 16, t["ffn_norm"][l].rearrange("(a b) -> a b", b=P))
                row(l, G_CQ, 4, t["cq_norm"][l].rearrange("(a b) -> a b", b=P))
                row(l, G_CKV, 2, t["ckv_norm"][l].rearrange("(a b) -> a b", b=P))
                row(l, G_MLA, 8, t["mla_out_norm"][l].rearrange("(a b) -> a b", b=P))
                row(l, G_GLA, 2, t["gla_out_norm"][l].rearrange("(a b) -> a b", b=P))
                for col, name in ((G_QN, "q_norm"), (G_KN, "k_norm")):
                    row(l, col, 1, t[name][l:l + 1, 0:NOPE])
                    for i in range(2):
                        sp.dma_start(rows[col + 1:col + 2, l * P + i * ROPE:l * P + (i + 1) * ROPE],
                                     t[name][l:l + 1, NOPE:QK]).then_inc(rows_landed, 16)
                for j in range(CONV + 1):
                    src = t["conv_w"][l, j] if j < CONV else t["conv_b"][l]
                    at = (DEPTH + l * (CONV + 1) + j) * P
                    sp.dma_start(rows[0:FT2, at:at + P], src.rearrange("(a b) -> a b", b=P)).then_inc(rows_landed, 16)
            sp.dma_start(cos[:, :].bitcast(I32), t["positions"].to_broadcast([P, T])).then_inc(rows_landed, 16)

            def up(l, g, par, r, k, ur, u):
                for f in range(2):
                    for side in range(2):
                        for h in range(2):
                            load(r, k + 4 * f + 2 * side + h, (8, 256),
                                 w_up[bass.ds(l, 1), :, 8 * h:8 * h + 8,
                                      bass.ds(g * (GROUP * P) + (f * 256 + side * D_FF), 256)])

            def down(l, g, par, r, k, ur, u):
                for q in range(4):
                    load(r, k + q, (4, 512),
                         w_down[bass.ds(l, 1), :, bass.ds(g * GROUP, GROUP), 512 * q:512 * q + 512])

            with sp.Fori(0, DEPTH) as l:
                L, r = bass.ds(l, 1), l * ROUNDS
                def tokens_block(j):
                    for q in range(4):
                        c0 = C_GK + 512 * j
                        load(r, K_TOK[j] + q, (4, 512), w_in[L, :, 4 * q:4 * q + 4, c0:c0 + 512])

                tokens_block(0)
                for h in range(2):
                    k = K_MISC + h
                    dst = raw[:, k % SLOTS, 0:8 * 80].rearrange("p (a b) -> p a b", a=8)
                    sp.wait_ge(lo_ready, r * SLOTS + k + 1)
                    for a, b, c0 in ((0, ROPE, C_KR), (ROPE, ROPE + RANK, C_A)):
                        src = w_in[L, :, 8 * h:8 * h + 8, c0:c0 + b - a].rearrange("o p k n -> p (o k) n")
                        if a == 0:
                            sp.dma_start(dst[:, :, a:b], src).then_inc(raw_landed[k % SLOTS], 16)
                        else:
                            sp.dma_start(dst[:, :, a:b], src).then_inc(misc_landed[h].sem, 16)
                tokens_block(1)
                tokens_block(2)
                for i, c0 in enumerate(FEAT_COLS):
                    for h in range(2):
                        load(r, K_FEAT + 2 * i + h, (8, 256), w_in[L, :, 8 * h:8 * h + 8, c0:c0 + 256], c0 + h == 0)
                for j in range(4):
                    load(r, K_UQ + j, (4, 384), w_uq[L, :, :, 384 * j:384 * j + 384])
                for j in range(2):
                    load(r, K_UKV + j, (2, 1024), w_ukv[L, :, :, 1024 * j:1024 * j + 1024])
                for h in (1, 0):
                    for i in range(8):
                        load(r, K_OUT + 8 * (1 - h) + i, (8, 256), w_out[L, :, 8 * h:8 * h + 8, 256 * i:256 * i + 256],
                             i + h == 0)
                mlp_order(sp, l, up, down)
            for i in range(TT):
                sp.wait_ge(out_copied, 4 * (i + 1))
                sp.dma_start(out[0, i * P:(i + 1) * P, :], xtok[i]).then_inc(out_stored, 16)
            sp.wait_ge(out_stored, 16 * TT)

        @block.gpsimd
        def _(pool):
            def sum_squares(squared, used, turn):
                for i in range(1, 7):
                    pool.wait_ge(squared.sem, squared.at(turn, i + 1))
                    if i > 1:
                        pool.wait_ge(used.sem, used.at(turn, i - 1))
                    pool.tensor_tensor(sq_sum, sq[:, 0, :, :] if i == 1 else sq_sum, sq[:, i % 2, :, :],
                                       ALU.add).then_inc(used.sem, 1)

            sum_squares(in_squared, in_square_used, 0)
            with pool.Fori(0, DEPTH) as l:
                pool.wait_ge(params_set.sem, params_set.at(l, 1))
                pool.dma_start(wg[64:64 + RANK, :], t["w_gate"][bass.ds(l, 1)].rearrange("o a b -> (o a) b")).then_inc(gate_landed.sem, 16)
                pool.dma_start(wg[64 + RANK:64 + RANK + 1, :], t["b_gate"][bass.ds(l, 1)]).then_inc(gate_landed.sem, 16)
                for h in range(1, HEADS - 1):
                    pool.wait_ge(a_squared.sem, a_squared.at(l, h + 1))
                    if h > 1:
                        pool.wait_ge(a_square_used.sem, a_square_used.at(l, h - 1))
                    pool.tensor_tensor(a_sum, a_sq[:, 0, :] if h == 1 else a_sum, a_sq[:, h % 2, :],
                                       ALU.add).then_inc(a_square_used.sem, 1)
                sum_squares(ff_squared, ff_square_used, l)
                sum_squares(in_squared, in_square_used, l + 1)

        @block.scalar
        def _(act):
            def a_square(l, h):
                act.wait_ge(values_copied.sem, values_copied.at(l, h + 1))
                if h >= 2:
                    act.wait_ge(a_square_used.sem, a_square_used.at(l, h - 1))
                act.activation(a_sq[:, h % 2, :], qn[:, h, :], ACT.Square).then_inc(a_squared.sem, 1)

            def split(r, k, l=None):
                n = WORDS
                if k in (K_MISC, K_MISC + 1):
                    n = 640
                    act.wait_ge(misc_landed[k - K_MISC].sem, misc_landed[k - K_MISC].at(l, 16))
                act.wait_ge(raw_landed[k % SLOTS], (r + k // SLOTS + 1) * 16)
                act.wait_ge(slot_free, r * SLOTS + k + 1)
                if K_UQ <= k < K_UKV:
                    for (_, part), (dst, _) in zip(head_parts(raw, k), head_parts(hi, k)):
                        ins = act.activation(dst, part, ACT.Copy)
                    ins.then_inc(hi_ready, 1)
                else:
                    act.activation(hi[:, k % SLOTS, 0:n], raw[:, k % SLOTS, 0:n], ACT.Copy).then_inc(hi_ready, 1)

            def copy_half(u, banks=2):
                act.activation(half[:, u % 2, 0:banks, :], bank2(u)[:, 0:banks, T:2 * T],
                               ACT.Copy).then_inc(half_copied, 1)

            def square_x(squared, used, turn, i):
                if i >= 2:
                    act.wait_ge(used.sem, used.at(turn, i - 1))
                act.activation(sq[:, i % 2, :, :], xT[:, 2 * i:2 * i + 2, :], ACT.Square).then_inc(squared.sem, 1)

            def norm(l, which):
                act.wait_ge(norm_summed.sem, norm_summed.at(l, which + 1))
                act.activation(rs[:, 0:T], X[:, which, 0:T], ACT.Sqrt, bias=eps, scale=1.0 / D).then_inc(norm_root.sem, 1)
                for i in range(8):
                    act.wait_ge(h_scaled.sem, h_scaled.at(l, 16 * which + 2 * i + 2))
                    act.activation(hx[:, 2 * i:2 * i + 2, 0:T], htmp[:, i % 2, :, :], ACT.Copy).then_inc(h_high.sem, 1)

            def up(l, g, par, r, k, ur, u):
                turn = l * NG + g
                for s in range(8):
                    split(r, k + s + 2)
                    f = s // 4
                    if s % 2:
                        act.wait_ge(slot_free, r * SLOTS + (k + s + 1 + SLOTS))
                        act.wait_ge(unit_free, ur * 2 + u + s // 2 + 1)
                        copy_half(u + s // 2)
                    if s % 4 == 3:
                        act.wait_ge(conv_step.sem, conv_step.at(turn, 12 * f + 6))
                        act.activation(yg, yg, ACT.Silu).then_inc(gate_done.sem, 1)
                        act.wait_ge(product_done.sem, product_done.at(turn, f + 1))
                        m = GROUP * par + 2 * f
                        act.activation(mid[:, m:m + 2, 0:T], yu, ACT.Copy).then_inc(mid_high.sem, 1)

            def down(l, g, par, r, k, ur, u):
                for q in range(4):
                    if k + q + 2 < CHUNKS:
                        split(r, k + q + 2)
                    if k + 4 == CHUNKS:
                        for i in range(2 * q, 2 * q + 2):
                            act.wait_ge(unit_free, ur * 2 + u + i + 3)
                            square_x(in_squared, in_square_used, l + 1, i)

            act.wait_ge(angle_small, 1)
            act.activation(rs[:, 0:T], sin[:, :], ACT.Abs).then_inc(table_step, 1)
            act.wait_ge(angle_small, 2)
            act.activation(cos[:, :], rs[:, T:2 * T], ACT.Sin).then_inc(table_step, 1)
            act.wait_ge(table_step, 2)
            act.activation(sin[:, :], sin[:, :], ACT.Sin).then_inc(table_step, 1)

            for i in range(8):
                act.wait_ge(x_copied, i + 1)
                square_x(in_squared, in_square_used, 0, i)

            with act.Fori(0, DEPTH) as l:
                r = l * ROUNDS

                def copy_uq(j):
                    split(r, K_UQ + j + 2)
                    act.wait_ge(unit_done, l * MID_UNITS + j + 1)
                    copy_half(U_UQ + 2 * j)
                    act.wait_ge(slot_free, r * SLOTS + K_UQ + j + 1 + SLOTS)
                    copy_half(U_UQ + 2 * j + 1, 1)

                def o_square(h):
                    act.activation(sq[:, h % 2, :, :], oT[:, :, h * T:(h + 1) * T], ACT.Square).then_inc(o_squared.sem, 1)

                def o_mean_root(h):
                    act.wait_ge(o_summed.sem, o_summed.at(l, h + 1))
                    act.activation(rs[:, (h % 2) * T:(h % 2 + 1) * T], X[:, h, 0:T], ACT.Sqrt,
                                   bias=eps, scale=1.0 / GDV).then_inc(o_root.sem, 1)

                def o_round(h):
                    act.wait_ge(o_gated.sem, o_gated.at(l, h + 1))
                    act.activation(hx[:, 8 + 2 * h:10 + 2 * h, 0:T], oT[:, :, h * T:(h + 1) * T], ACT.Copy).then_inc(o_high.sem, 1)

                def qk_square(j):
                    u = U_UQ + 2 * j + 2 if j < 4 else U_UKV + (0, 1, 3, 4)[j - 4] + 1
                    act.wait_ge(unit_free, l * UNITS + u + 2)
                    if j >= 1:
                        act.wait_ge(qk_summed.sem, qk_summed.at(l, j))
                    heads = qn[:, 2 * j:2 * j + 2, :] if j < 4 else kn[:, 2 * j - 8:2 * j - 6, :]
                    act.activation(sq[:, 0, :, :], heads, ACT.Square).then_inc(qk_squared.sem, 1)
                    act.activation(sq[:, 1, 0, :], qkr[:, j, :], ACT.Square).then_inc(qk_squared.sem, 1)

                def qk_mean_root(j):
                    act.wait_ge(qk_summed.sem, qk_summed.at(l, j + 1))
                    act.activation(norms[:, 4 * j:4 * j + 4], X[:, j % 2, 0:4], ACT.Sqrt, bias=eps_q if j < 4 else eps,
                                   scale=1.0 if j < 4 else 1.0 / QK).then_inc(qk_root.sem, 1)

                split(r, 0)
                split(r, 1)
                act.wait_ge(params_set.sem, params_set.at(l, 1))
                norm(l, 0)
                for k in range(4):
                    split(r, k + 2, l)
                for k in range(K_MISC, K_MISC + 2):
                    split(r, k + 2)
                act.wait_ge(slot_free, r * SLOTS + K_MISC + 2 + SLOTS)
                act.activation(rs[0:80, 0:T], X[0:80, 1, T:2 * T], ACT.Copy).then_inc(misc_half.sem, 1)
                for q in range(4):
                    split(r, K_TOK[1] + q + 2)
                act.wait_ge(gate_logits.sem, gate_logits.at(l, 1))
                act.activation(la, X[:, 2:4, :], ACT.Abs).then_inc(gate_soft.sem, 1)
                act.wait_ge(gate_soft.sem, gate_soft.at(l, 1))
                act.activation(la, la, ACT.Exp, scale=-1.0).then_inc(gate_soft.sem, 1)
                act.wait_ge(gate_soft.sem, gate_soft.at(l, 2))
                act.activation(la, la, ACT.Ln, bias=ones[:, 0:1]).then_inc(gate_soft.sem, 1)
                for q in range(4):
                    split(r, K_TOK[2] + q + 2)
                act.wait_ge(gate_sums.sem, gate_sums.at(l, 1))
                act.activation(la, X[:, 2:4, :], ACT.Exp, scale=1.0 / TAU).then_inc(gate_decay.sem, 1)
                act.activation(decay, X[:, 1, 0:16], ACT.Exp, scale=1.0 / TAU).then_inc(gate_decay.sem, 1)
                for i in range(9):
                    split(r, K_FEAT + 2 * i + 2)
                    split(r, K_FEAT + 2 * i + 3)
                    act.wait_ge(slot_free, r * SLOTS + K_FEAT + 2 * i + 2 + SLOTS)
                    copy_half(U_FEAT + i)
                    if 2 <= i <= 4:
                        act.wait_ge(unit_free, l * UNITS + U_FEAT + i + 1 + 2)
                        if i == 4:
                            act.wait_ge(c_square_used.sem, c_square_used.at(l, 1))
                        act.activation(sq[:, i % 2, :, :], z[:, 2 * i:2 * i + 2, :], ACT.Square).then_inc(c_squared.sem, 1)
                    if i == 5:
                        act.wait_ge(c_square_used.sem, c_square_used.at(l, 3))
                        act.wait_ge(misc_ready.sem, misc_ready.at(l, 1))
                        act.activation(rs[:, 0:T], X[:, 3, 0:T], ACT.Sqrt, bias=eps, scale=1.0 / Q_LORA).then_inc(c_root.sem, 1)
                        act.activation(rs[:, T:2 * T], X[:, 3, T:2 * T], ACT.Sqrt, bias=eps, scale=1.0 / KV_LORA).then_inc(c_root.sem, 1)
                    if i == 6:
                        for n in range(3):
                            act.wait_ge(c_scaled.sem, c_scaled.at(l, 2 * n + 2))
                            act.activation(mid[:, 2 * n:2 * n + 2, 0:T], z[:, Z_CQ + 2 * n:Z_CQ + 2 * n + 2, :], ACT.Copy).then_inc(c_high.sem, 1)
                        act.wait_ge(reads_copied.sem, reads_copied.at(l, 4))
                        o_square(0)
                        o_square(1)
                    if i == 7:
                        o_mean_root(0)
                        o_mean_root(1)
                        o_square(2)
                        o_square(3)
                    if i == 8:
                        act.wait_ge(o_scaled.sem, o_scaled.at(l, 4))
                        o_mean_root(2)
                        o_mean_root(3)
                act.wait_ge(unit_free, l * UNITS + U_UQ + 2)
                act.activation(z[:, Z_G:Z_G + 8, :], z[:, Z_G:Z_G + 8, :], ACT.Silu).then_inc(g_silu.sem, 1)
                copy_uq(0)
                o_round(0)
                act.wait_ge(c_ready.sem, c_ready.at(l, 3))
                for i in range(2):
                    act.activation(qkr[64 * i:64 * i + 64, 4:8, :],
                                   zm[0:64, :].rearrange("p (o t) -> p o t", o=1).to_broadcast([64, 4, T]),
                                   ACT.Copy).then_inc(kr_spread.sem, 1)
                copy_uq(1)
                o_round(1)
                qk_square(0)
                copy_uq(2)
                o_round(2)
                qk_mean_root(0)
                qk_square(1)
                copy_uq(3)
                o_round(3)
                qk_mean_root(1)
                qk_square(2)
                act.wait_ge(kr_spread.sem, kr_spread.at(l, 2))
                for j in range(2):
                    split(r, K_UKV + j + 2)
                    for i in range(2):
                        act.wait_ge(unit_done, l * MID_UNITS + 4 + 2 * j + i + 1)
                        copy_half(U_UKV + 3 * j + i)
                    qk_mean_root(2 + j)
                    qk_square(3 + j)
                for i in range(4):
                    split(r, K_OUT + i + 2)
                    qk_mean_root(4 + i)
                    if i < 3:
                        qk_square(5 + i)
                for h in range(HEADS):
                    act.wait_ge(tops_scaled.sem, tops_scaled.at(l, h + 1))
                    if h >= 2:
                        act.wait_ge(probs_turned.sem, probs_turned.at(l, h - 1))
                    for b in range(TT):
                        a0, a1 = (0, P) if b == 0 else (P, 3 * P)
                        at = 2 * (h % 2) + b
                        act.activation(prob[:, h % 2, a0:a1], X[:, h % 2, a0:a1], ACT.Exp,
                                       bias=ntop[:, at:at + 1], scale=norms[:, 2 * h + b:2 * h + b + 1],
                                       accum_out=sums[:, at:at + 1]).then_inc(exps_done.sem, 1)
                    if h % 2 == 0:
                        split(r, K_OUT + 4 + h // 2 + 2)
                    act.wait_ge(probs_turned.sem, probs_turned.at(l, h + 1))
                    if h >= 2:
                        act.wait_ge(values_done.sem, values_done.at(l, h - 1))
                    act.activation(probT[:, h % 2, 0:3 * P], X[:, 2, 0:3 * P], ACT.Copy).then_inc(probs_copied.sem, 1)
                    if h >= 1:
                        a_square(l, h - 1)
                a_square(l, HEADS - 1)
                act.wait_ge(a_summed.sem, a_summed.at(l, 1))
                act.activation(rs[:, 0:T], X[:, 0, 0:T], ACT.Sqrt, bias=eps, scale=1.0 / (HEADS * VD)).then_inc(a_root.sem, 1)
                for i in range(4):
                    act.wait_ge(a_scaled.sem, a_scaled.at(l, 2 * i + 2))
                    act.activation(hx[:, 2 * i:2 * i + 2, 0:T], qn[:, 2 * i:2 * i + 2, :], ACT.Copy).then_inc(a_high.sem, 1)
                for i in range(8):
                    split(r, K_OUT + 8 + i + 2)
                    act.wait_ge(unit_free, l * UNITS + U_OUT + 8 + i + 1 + 2)
                    square_x(ff_squared, ff_square_used, l, i)
                norm(l, 1)
                mlp_order(act, l, up, down)

        @block.vector
        def _(dve):
            def split(r, k):
                n = 640 if k in (K_MISC, K_MISC + 1) else WORDS
                s = k % SLOTS
                dve.wait_ge(hi_ready, r * SLOTS + k + 1)
                if K_UQ <= k < K_UKV:
                    for (_, part), (h, _), (dst, _) in zip(head_parts(raw, k), head_parts(hi, k), head_parts(lo, k)):
                        ins = dve.tensor_tensor(dst, part, h.bitcast(F32), ALU.subtract)
                    ins.then_inc(lo_ready, 1)
                else:
                    dve.tensor_tensor(lo[:, s, 0:n], raw[:, s, 0:n], hi[:, s, 0:n].bitcast(F32),
                                      ALU.subtract).then_inc(lo_ready, 1)

            def add_halves(u, dst, banks=2):
                dve.tensor_tensor(dst, bank2(u)[:, 0:banks, 0:T], half[:, u % 2, 0:banks, :],
                                  ALU.add).then_inc(unit_free, 1)

            def add_to_x(l, u, n, tile):
                two = xT[:, tile:tile + 2, :]
                dve.tensor_tensor(two, bank2(u)[:, :, 0:T], two, ALU.add).then_inc(x_added, 1)
                dve.wait_ge(x_added, l * X_ADDS + n + 1)
                dve.tensor_tensor(two, bank2(u)[:, :, T:2 * T], two, ALU.add).then_inc(unit_free, 1)

            def norm(l, which):
                col = G_FFN if which else G_ATTN
                dve.wait_ge(norm_root.sem, norm_root.at(l, which + 1))
                dve.reciprocal(rs[:, 0:T], rs[:, 0:T]).then_inc(norm_scale.sem, 1)
                dve.wait_ge(norm_scale.sem, norm_scale.at(l, which + 1))
                def round_off(i):
                    dve.wait_ge(h_high.sem, h_high.at(l, 8 * which + i + 1))
                    dve.tensor_tensor(hx[:, 2 * i:2 * i + 2, T:2 * T], htmp[:, i % 2, :, :],
                                      hx[:, 2 * i:2 * i + 2, 0:T].bitcast(F32), ALU.subtract).then_inc(h_ready.sem, 1)

                for i in range(8):
                    if i >= 2:
                        dve.wait_ge(h_ready.sem, h_ready.at(l, 8 * which + i - 1))
                    for j in range(2):
                        dve.scalar_tensor_tensor(htmp[:, i % 2, j, :], xT[:, 2 * i + j, :], gain(col + 2 * i + j),
                                                 rs[:, 0:T], ALU.mult, ALU.mult).then_inc(h_scaled.sem, 1)
                    if i >= 1:
                        round_off(i - 1)
                round_off(7)

            def up(l, g, par, r, k, ur, u):
                turn = l * NG + g
                if k > K_FFN:
                    dve.wait_ge(mid_ready.sem, mid_ready.at(turn, 0))
                dve.tensor_copy(conv_p[:, :, :, :], conv_all[:, bass.ds(l, 1), :, :, bass.ds(g * GROUP, GROUP)]
                                .rearrange("p o j s f -> p (o j) s f")).then_inc(taps_set.sem, 1)
                for s in range(8):
                    split(r, k + s + 2)
                    if s % 2 == 0:
                        continue
                    f, side = s // 4, s // 2 % 2
                    ub, y = ubuf[side], (yg, yu)[side]
                    un = u + s // 2
                    dve.wait_ge(half_copied, l * HALF_COPIES + g * 4 + (H_FFN + s // 2 + 1))
                    if s == 5:
                        dve.wait_ge(mid_ready.sem, mid_ready.at(turn, 1))
                    add_halves(un, ub[:, :, CONV - 1:CONV - 1 + T])
                    dve.wait_ge(unit_free, ur * 2 + un + 3)
                    if s == 1:
                        dve.wait_ge(taps_set.sem, taps_set.at(turn, 1))
                    step = 12 * f + 6 * side
                    for n, j in enumerate((2, 1, 0)):
                        if n:
                            dve.wait_ge(conv_step.sem, conv_step.at(turn, step + 2 * n))
                        for i in range(2):
                            tap = conv_p[:, j, side, 2 * f + i:2 * f + i + 1]
                            if n == 0:
                                dve.tensor_scalar(y[:, i, :], ub[:, i, j:j + T], tap,
                                                  conv_p[:, CONV, side, 2 * f + i:2 * f + i + 1],
                                                  ALU.mult, ALU.add).then_inc(conv_step.sem, 1)
                            else:
                                dve.scalar_tensor_tensor(y[:, i, :], ub[:, i, j:j + T], tap, y[:, i, :],
                                                         ALU.mult, ALU.add).then_inc(conv_step.sem, 1)
                    if side == 1:
                        dve.wait_ge(conv_step.sem, conv_step.at(turn, 12 * f + 12))
                        dve.wait_ge(gate_done.sem, gate_done.at(turn, f + 1))
                        dve.tensor_tensor(yu, yg, yu, ALU.mult).then_inc(product_done.sem, 1)
                        m = GROUP * par + 2 * f
                        dve.wait_ge(mid_high.sem, mid_high.at(turn, f + 1))
                        dve.tensor_tensor(mid[:, m:m + 2, T:2 * T], yu, mid[:, m:m + 2, 0:T].bitcast(F32),
                                          ALU.subtract).then_inc(mid_ready.sem, 1)

            def down(l, g, par, r, k, ur, u):
                for q in range(4):
                    if k + q + 2 < CHUNKS:
                        split(r, k + q + 2)
                    for i in range(2):
                        if i == 0:
                            dve.wait_ge(unit_done, l * MID_UNITS + g * 4 + (8 + q + 1))
                        else:
                            dve.wait_ge(slot_free, r * SLOTS + (k + q + 1 + SLOTS))
                        add_to_x(l, u + 2 * q + i, g * 8 + (16 + 2 * q + i), 4 * q + 2 * i)

            dve.sem_inc(lo_ready, SLOTS)
            dve.sem_inc(unit_free, 2)
            dve.memset(zm[64:96, :], 1.0).then_inc(zeroed, 1)
            dve.wait_ge(zeroed, 1)
            for s in range(8):
                dve.wait_ge(x_turned, s + 1)
                dve.tensor_copy(xT[:, 2 * s:2 * s + 2, :], X[:, s % 4, :].rearrange("p (a t) -> p a t", a=2)).then_inc(x_copied, 1)
            for l in range(DEPTH):
                dve.wait_ge(rows_turned, l + 1)
                dve.tensor_copy(params_all[:, l, :], G[:, l, 0:PARAMS]).then_inc(rows_copied, 1)
            dve.wait_ge(rows_landed, ROW_LOADS * 16)
            dve.wait_ge(const_landed, 16)
            dve.tensor_copy(rs[:, 0:T], cos[:, :].bitcast(I32)).then_inc(angle_step, 1)
            dve.wait_ge(angle_step, 1)
            dve.tensor_scalar(sin[:, :], rs[:, 0:T], freq, None, ALU.mult).then_inc(angle_step, 1)
            dve.wait_ge(angle_step, 2)
            dve.tensor_scalar(rs[:, T:2 * T], sin[:, :], 1.0 / TWO_PI, ROUNDER, ALU.mult, ALU.add).then_inc(angle_step, 1)
            dve.wait_ge(angle_step, 3)
            dve.tensor_scalar(rs[:, T:2 * T], rs[:, T:2 * T], ROUNDER, None, ALU.subtract).then_inc(angle_step, 1)
            dve.wait_ge(angle_step, 4)
            for i, part in enumerate(TURN_PARTS):
                dve.scalar_tensor_tensor(sin[:, :], rs[:, T:2 * T], -part, sin[:, :], ALU.mult, ALU.add).then_inc(angle_step, 1)
                dve.wait_ge(angle_step, 5 + i)
            dve.tensor_scalar(sin[:, :], sin[:, :], NEARLY_PI, -NEARLY_PI, ALU.min, ALU.max).then_inc(angle_small, 1)
            dve.wait_ge(table_step, 1)
            dve.tensor_scalar(rs[:, T:2 * T], rs[:, 0:T], -1.0, TWO_PI / 4, ALU.mult, ALU.add).then_inc(angle_small, 1)
            dve.wait_ge(rows_copied, DEPTH)
            dve.wait_ge(x_copied, 8)
            dve.wait_ge(table_step, 3)

            with dve.Fori(0, DEPTH) as l:
                r, ur = l * ROUNDS, l * PAIRS
                dve.tensor_copy(gains[:, :], params_all[:, bass.ds(l, 1), 0:GAINS]
                                .rearrange("p o g -> p (o g)")).then_inc(params_set.sem, 1)
                dve.wait_ge(params_set.sem, params_set.at(l, 1))
                split(r, 0)
                split(r, 1)
                norm(l, 0)
                def tokens_out(j):
                    for q in range(4):
                        split(r, K_TOK[j] + q + 2)
                    dve.wait_ge(slot_free, r * SLOTS + K_TOK[j] + 4 + SLOTS)
                    dst = gk if j == 0 else gv[:, :, 512 * (j - 1):512 * j]
                    dve.tensor_copy(dst, bank2(U_TOK + j)).then_inc(unit_free, 1)

                def state_step(n):
                    dve.wait_ge(update_done.sem, update_done.at(l, n + 1))
                    if n >= 1:
                        dve.wait_ge(reads_done.sem, reads_done.at(l, n))
                        dve.wait_ge(state_ready.sem, state_ready.at(l, 4 * n))
                    for h in range(GH):
                        new = X[:, h // 2, (h % 2) * GDV:(h % 2 + 1) * GDV]
                        if n == 0:
                            dve.tensor_copy(state[:, h, :], new).then_inc(state_ready.sem, 1)
                        else:
                            dve.scalar_tensor_tensor(state[:, h, :], state[:, h, :], decay[:, 4 * h + n:4 * h + n + 1],
                                                     new, ALU.mult, ALU.add).then_inc(state_ready.sem, 1)

                def copy_reads(n):
                    dve.wait_ge(reads_done.sem, reads_done.at(l, n + 1))
                    o_chunk = oT.rearrange("p e (h t) -> p h e t", h=GH)[:, :, :, n * CHUNK:(n + 1) * CHUNK]
                    dve.tensor_scalar(o_chunk, X[:, 2, :].rearrange("p (h e t) -> p h e t", h=GH, e=2),
                                      GDK ** -0.5, None, ALU.mult).then_inc(reads_copied.sem, 1)

                def o_normed(h):
                    s = rs[:, (h % 2) * T:(h % 2 + 1) * T]
                    dve.wait_ge(o_root.sem, o_root.at(l, h + 1))
                    dve.reciprocal(s, s).then_inc(o_scale.sem, 1)
                    dve.wait_ge(o_scale.sem, o_scale.at(l, h + 1))
                    for e in range(2):
                        o = oT[:, e, h * T:(h + 1) * T]
                        dve.scalar_tensor_tensor(o, o, gain(G_GLA + e), s, ALU.mult, ALU.mult).then_inc(o_scaled.sem, 1)

                def o_gate(h):
                    o = oT[:, :, h * T:(h + 1) * T]
                    dve.tensor_tensor(o, o, z[:, Z_G + 2 * h:Z_G + 2 * h + 2, :], ALU.mult).then_inc(o_gated.sem, 1)

                def o_round_off(h):
                    m = 8 + 2 * h
                    dve.wait_ge(o_high.sem, o_high.at(l, h + 1))
                    dve.tensor_tensor(hx[:, m:m + 2, T:2 * T], oT[:, :, h * T:(h + 1) * T],
                                      hx[:, m:m + 2, 0:T].bitcast(F32), ALU.subtract).then_inc(o_ready.sem, 1)

                tokens_out(0)
                for s in range(2):
                    split(r, K_MISC + s + 2)
                dve.wait_ge(misc_half.sem, misc_half.at(l, 1))
                dve.tensor_tensor(zm[0:80, :], X[0:80, 1, 0:T], rs[0:80, 0:T], ALU.add).then_inc(misc_ready.sem, 1)
                dve.tensor_tensor(gain_qk, gain(G_QN), gain(G_KN), ALU.mult).then_inc(gains_joined.sem, 1)
                tokens_out(1)
                dve.wait_ge(gate_soft.sem, gate_soft.at(l, 3))
                dve.scalar_tensor_tensor(la, X[:, 2:4, :], 0.0, la, ALU.min, ALU.subtract).then_inc(gate_log.sem, 1)
                tokens_out(2)
                dve.wait_ge(gate_decay.sem, gate_decay.at(l, 1))
                dve.tensor_tensor(gk, gk, la, ALU.mult).then_inc(keys_decayed.sem, 1)
                dve.wait_ge(gate_decay.sem, gate_decay.at(l, 2))
                for i in range(9):
                    split(r, K_FEAT + 2 * i + 2)
                    split(r, K_FEAT + 2 * i + 3)
                    dve.wait_ge(half_copied, l * HALF_COPIES + H_FEAT + i + 1)
                    add_halves(U_FEAT + i, z[:, 2 * i:2 * i + 2, :])
                    if 1 <= i <= 4:
                        state_step(i - 1)
                    if 2 <= i <= 5:
                        copy_reads(i - 2)
                    if i == 5:
                        dve.wait_ge(c_root.sem, c_root.at(l, 2))
                        dve.reciprocal(rs[:, :], rs[:, :]).then_inc(c_scale.sem, 1)
                        dve.wait_ge(c_scale.sem, c_scale.at(l, 1))
                        for n in range(6):
                            tile = z[:, Z_CQ + n, :]
                            dve.scalar_tensor_tensor(tile, tile, gain(G_CQ + n), rs[:, 0:T] if n < 4 else rs[:, T:2 * T],
                                                     ALU.mult, ALU.mult).then_inc(c_scaled.sem, 1)
                    if i == 6:
                        for n in range(3):
                            dve.wait_ge(c_high.sem, c_high.at(l, n + 1))
                            dve.tensor_tensor(mid[:, 2 * n:2 * n + 2, T:2 * T], z[:, Z_CQ + 2 * n:Z_CQ + 2 * n + 2, :],
                                              mid[:, 2 * n:2 * n + 2, 0:T].bitcast(F32), ALU.subtract).then_inc(c_ready.sem, 1)
                    if i in (7, 8):
                        o_normed(2 * i - 14)
                        o_normed(2 * i - 13)
                dve.wait_ge(o_scaled.sem, o_scaled.at(l, 2 * GH))
                dve.wait_ge(c_ready.sem, c_ready.at(l, 3))

                def uq_out(j):
                    split(r, K_UQ + j + 2)
                    dve.wait_ge(half_copied, l * HALF_COPIES + H_UQ + 2 * j + 1)
                    add_halves(U_UQ + 2 * j, qn[:, 2 * j:2 * j + 2, :])
                    dve.wait_ge(half_copied, l * HALF_COPIES + H_UQ + 2 * j + 2)
                    add_halves(U_UQ + 2 * j + 1, qkr[:, j:j + 1, :], 1)

                def q_gain(j):
                    dve.wait_ge(qk_squared.sem, qk_squared.at(l, 2 * j + 2))
                    dve.tensor_scalar(qkr[:, j, :], qkr[:, j, :], gain(G_QR), None, ALU.mult).then_inc(qk_normed.sem, 1)

                def inverse(j):
                    dve.wait_ge(qk_root.sem, qk_root.at(l, j + 1))
                    dve.reciprocal(norms[:, 4 * j:4 * j + 4], norms[:, 4 * j:4 * j + 4]).then_inc(qk_inverse.sem, 1)

                def k_diagonals(j):
                    inverse(j)
                    dve.wait_ge(qk_inverse.sem, qk_inverse.at(l, j + 1))
                    if j >= 5:
                        dve.wait_ge(k_scale_spread.sem, k_scale_spread.at(l, j - 4))
                    dve.tensor_tensor(diag, ident.rearrange("p (o t) -> p o t", o=1).to_broadcast([P, 4, P]),
                                      norms[:, 4 * j:4 * j + 4].rearrange("p (c o) -> p c o", o=1).to_broadcast([P, 4, P]),
                                      ALU.mult).then_inc(diag_ready.sem, 1)

                def k_normed(j):
                    dve.wait_ge(k_scale_spread.sem, k_scale_spread.at(l, j - 3))
                    two = kn[:, 2 * j - 8:2 * j - 6, :]
                    dve.scalar_tensor_tensor(two, two, gain_qk, X[:, j % 2, :].rearrange("p (a t) -> p a t", a=2),
                                             ALU.mult, ALU.mult).then_inc(qk_normed.sem, 1)
                    for i in range(2):
                        lanes = slice(64 * i, 64 * i + 64)
                        one = qkr[lanes, j, :]
                        dve.scalar_tensor_tensor(one, one, gains[lanes, G_KR:G_KR + 1], X[lanes, j % 2, i * T:(i + 1) * T],
                                                 ALU.mult, ALU.mult).then_inc(qk_normed.sem, 1)

                def rope(j):
                    dve.wait_ge(rope_turned.sem, rope_turned.at(l, j + 1))
                    if j >= 2:
                        dve.wait_ge(rope_done.sem, rope_done.at(l, j - 1))
                    dve.tensor_tensor(rope_tmp[:, j % 2, :], X[:, 2 + j % 2, 0:T], sin[:, :],
                                      ALU.mult).then_inc(rope_parts.sem, 1)
                    dve.tensor_tensor(qkr[:, j, :], qkr[:, j, :], cos[:, :], ALU.mult).then_inc(rope_parts.sem, 1)
                    dve.wait_ge(rope_parts.sem, rope_parts.at(l, 2 * j + 2))
                    dve.tensor_tensor(qkr[:, j, :], qkr[:, j, :], rope_tmp[:, j % 2, :], ALU.add).then_inc(rope_done.sem, 1)

                def out_g(i):
                    dve.wait_ge(slot_free, r * SLOTS + K_OUT + i + 1 + SLOTS)
                    add_to_x(l, U_OUT + i, i, 2 * i)

                uq_out(0)
                dve.wait_ge(g_silu.sem, g_silu.at(l, 1))
                o_gate(0)
                uq_out(1)
                o_gate(1)
                o_round_off(0)
                uq_out(2)
                o_gate(2)
                o_round_off(1)
                q_gain(0)
                uq_out(3)
                o_gate(3)
                o_round_off(2)
                inverse(0)
                q_gain(1)
                for j in range(2):
                    split(r, K_UKV + j + 2)
                    for i in range(2):
                        dve.wait_ge(half_copied, l * HALF_COPIES + H_UKV + 2 * j + i + 1)
                        add_halves(U_UKV + 3 * j + i, kn[:, 4 * j + 2 * i:4 * j + 2 * i + 2, :])
                    dve.wait_ge(slot_free, r * SLOTS + K_UKV + j + 1 + SLOTS)
                    dve.tensor_copy(v[:, :, 512 * j:512 * j + 512], bank2(U_UKV + 3 * j + 2)).then_inc(unit_free, 1)
                    if j == 0:
                        o_round_off(3)
                        dve.wait_ge(o_ready.sem, o_ready.at(l, GH))
                    dve.wait_ge(qk_normed.sem, qk_normed.at(l, j + 1))
                    rope(j)
                    inverse(1 + j)
                    q_gain(2 + j)
                split(r, K_OUT + 2)
                out_g(0)
                rope(2)
                inverse(3)
                split(r, K_OUT + 3)
                k_diagonals(4)
                out_g(1)
                rope(3)
                split(r, K_OUT + 4)
                k_diagonals(5)
                k_normed(4)
                out_g(2)
                split(r, K_OUT + 5)
                k_diagonals(6)
                k_normed(5)
                rope(4)
                out_g(3)
                k_diagonals(7)
                k_normed(6)
                rope(5)
                k_normed(7)
                rope(6)
                rope(7)

                def find_top(h):
                    dve.wait_ge(scores_done.sem, scores_done.at(l, h + 1))
                    dve.memset(X[0:CHUNK, h % 2, P - CHUNK:P], NEG).then_inc(scores_masked.sem, 1)
                    dve.memset(X[0:CHUNK, h % 2, 3 * P - CHUNK:3 * P], NEG).then_inc(scores_masked.sem, 1)
                    dve.wait_ge(scores_masked.sem, scores_masked.at(l, 2 * h + 2))
                    at = 2 * (h % 2)
                    dve.tensor_reduce(top[:, at:at + 1], X[:, h % 2, 0:P], AX_X, ALU.max).then_inc(tops_found.sem, 1)
                    dve.tensor_reduce(top[:, at + 1:at + 2], X[:, h % 2, P:3 * P], AX_X, ALU.max).then_inc(tops_found.sem, 1)
                    dve.wait_ge(tops_found.sem, tops_found.at(l, 2 * h + 2))
                    dve.scalar_tensor_tensor(ntop[:, at:at + 2], top[:, at:at + 2], -1.0, norms[:, 2 * h:2 * h + 2],
                                             ALU.mult, ALU.mult).then_inc(tops_scaled.sem, 1)

                def copy_values(h):
                    dve.wait_ge(values_done.sem, values_done.at(l, h + 1))
                    dve.tensor_copy(qn[:, h, :], X[:, 3, 0:T]).then_inc(values_copied.sem, 1)

                dve.wait_ge(qk_inverse.sem, qk_inverse.at(l, 4))
                find_top(0)
                for h in range(HEADS):
                    if h + 1 < HEADS:
                        find_top(h + 1)
                    at = 2 * (h % 2)
                    dve.wait_ge(exps_done.sem, exps_done.at(l, 2 * h + 2))
                    dve.reciprocal(rsum[:, at:at + 2], sums[:, at:at + 2]).then_inc(sums_inverted.sem, 1)
                    dve.wait_ge(sums_inverted.sem, sums_inverted.at(l, h + 1))
                    for b in range(TT):
                        part = prob[:, h % 2, 0:P] if b == 0 else prob[:, h % 2, P:3 * P]
                        dve.tensor_scalar(part, part, rsum[:, at + b:at + b + 1], None, ALU.mult).then_inc(probs_ready.sem, 1)
                    if h % 2 == 0:
                        split(r, K_OUT + 4 + h // 2 + 2)
                    if h >= 1:
                        copy_values(h - 1)
                    if h % 2 == 1:
                        out_g(4 + h // 2)
                copy_values(HEADS - 1)
                dve.wait_ge(a_root.sem, a_root.at(l, 1))
                dve.reciprocal(rs[:, 0:T], rs[:, 0:T]).then_inc(a_scale.sem, 1)
                dve.wait_ge(a_scale.sem, a_scale.at(l, 1))

                def a_round_off(i):
                    dve.wait_ge(a_high.sem, a_high.at(l, i + 1))
                    dve.tensor_tensor(hx[:, 2 * i:2 * i + 2, T:2 * T], qn[:, 2 * i:2 * i + 2, :],
                                      hx[:, 2 * i:2 * i + 2, 0:T].bitcast(F32), ALU.subtract).then_inc(a_ready.sem, 1)

                for h in range(HEADS):
                    dve.scalar_tensor_tensor(qn[:, h, :], qn[:, h, :], gain(G_MLA + h), rs[:, 0:T],
                                             ALU.mult, ALU.mult).then_inc(a_scaled.sem, 1)
                    if h in (3, 5, 7):
                        a_round_off(h // 2 - 1)
                a_round_off(3)
                for i in range(8):
                    split(r, K_OUT + 8 + i + 2)
                    dve.wait_ge(slot_free, r * SLOTS + K_OUT + 8 + i + 1 + SLOTS)
                    add_to_x(l, U_OUT + 8 + i, 8 + i, 2 * i)
                for side in range(2):
                    dve.memset(ubuf[side][:, :, 0:CONV - 1], 0.0).then_inc(pads_zeroed.sem, 1)
                dve.wait_ge(pads_zeroed.sem, pads_zeroed.at(l, 2))
                dve.wait_ge(unit_free, l * UNITS + U_FFN + 2)
                norm(l, 1)
                mlp_order(dve, l, up, down)
                dve.wait_ge(unit_free, l * UNITS + UNITS + 2)
            for n in range(8):
                dve.wait_ge(out_turned, n + 1)
                dve.tensor_copy(xtok[n // 4][:, (n % 4) * 512:(n % 4 + 1) * 512], X[:, n % 4, :]).then_inc(out_copied, 1)

        @block.tensor
        def _(pe):
            def take(r, k):
                pe.wait_ge(lo_ready, r * SLOTS + (k + 1 + SLOTS))
                return hi[:, k % SLOTS, :], lo[:, k % SLOTS, :]

            def tile_pass(bank, w_hi, w_lo, x2, first, last):
                pe.matmul(bank, w_hi, x2, start=first, stop=False)
                return pe.matmul(bank[:, T:2 * T], w_lo, x2[:, 0:T], start=False, stop=last)

            def bank_free(ur, u):
                pe.wait_ge(unit_free, ur * 2 + (u + 3 - (2 if u < U_FFN + 2 else 4)))

            def pair_chunk(r, k, u, half_of_k, src, first, last, ready=None, ready_at=0):
                w_hi, w_lo = take(r, k)
                for i in range(2):
                    for a in range(8):
                        if ready is not None and i == 0 and a % 2 == 0:
                            pe.wait_ge(ready.sem, ready_at + a // 2 + 1)
                        at = a * 256 + i * P
                        mm = tile_pass(bank2(u)[:, i, :], w_hi[:, at:at + P], w_lo[:, at:at + P],
                                       src[:, 8 * half_of_k + a, :], first and a == 0, last and a == 7)
                mm.then_inc(slot_free, 1)

            def up(l, g, par, r, k, ur, u):
                for s in range(8):
                    un = u + s // 2
                    if s % 2 == 0:
                        bank_free(ur, un)
                    fresh = k == K_FFN and s < 2
                    pair_chunk(r, k + s, un, s % 2, hx, s % 2 == 0, s % 2 == 1,
                               h_ready if fresh else None, h_ready.at(l, 8 + 4 * s))

            def down(l, g, par, r, k, ur, u):
                pe.wait_ge(mid_ready.sem, mid_ready.at(l * NG + g, 2))
                for q in range(4):
                    w_hi, w_lo = take(r, k + q)
                    for i in range(4):
                        un = u + 2 * q + i // 2
                        if i % 2 == 0:
                            bank_free(ur, un)
                        for a in range(GROUP):
                            at = a * 512 + i * P
                            mm = tile_pass(bank2(un)[:, i % 2, :], w_hi[:, at:at + P], w_lo[:, at:at + P],
                                           mid[:, GROUP * par + a, :], a == 0, a == GROUP - 1)
                        if i == 1:
                            mm.then_inc(unit_done, 1)
                    mm.then_inc(slot_free, 1)

            pe.sem_inc(slot_free, SLOTS)
            pe.wait_ge(const_landed, 16)
            pe.wait_ge(x_landed, 32)
            for s in range(8):
                if s >= 4:
                    pe.wait_ge(x_copied, s - 3)
                for j in range(2):
                    for i in range(TT):
                        mm = pe.transpose(X[:, s % 4, j * T + i * P:j * T + (i + 1) * P],
                                          xtok[i][:, (2 * s + j) * P:(2 * s + j + 1) * P], ident)
                mm.then_inc(x_turned, 1)
            pe.wait_ge(rows_landed, ROW_LOADS * 16)
            for l in range(DEPTH):
                pe.transpose(G[:, l, 0:GAINS], rows[0:GAINS, l * P:(l + 1) * P], ident[0:GAINS, 0:GAINS])
                for j in range(CONV + 1):
                    at = (DEPTH + l * (CONV + 1) + j) * P
                    mm = pe.transpose(G[:, l, GAINS + j * FT2:GAINS + (j + 1) * FT2], rows[0:FT2, at:at + P],
                                      ident[0:FT2, 0:FT2])
                mm.then_inc(rows_turned, 1)
            pe.wait_ge(rows_copied, DEPTH)
            pe.wait_ge(x_copied, 8)

            with pe.Fori(0, DEPTH) as l:
                r, ur = l * ROUNDS, l * PAIRS

                def norm_sums(which, squared, used, turn):
                    pe.wait_ge(used.sem, used.at(turn, 6))
                    for j in range(2):
                        pe.matmul(X[:, which, 0:T], ones, sq_sum[:, j, :], start=j == 0, stop=False)
                    pe.wait_ge(squared.sem, squared.at(turn, 8))
                    for j in range(2):
                        mm = pe.matmul(X[:, which, 0:T], ones, sq[:, 1, j, :], start=False, stop=j == 1)
                    mm.then_inc(norm_summed.sem, 1)

                def tokens_block(j):
                    bank_free(ur, U_TOK + j)
                    for q in range(4):
                        w_hi, w_lo = take(r, K_TOK[j] + q)
                        for a in range(4):
                            kt = 4 * q + a
                            if j == 0 and a % 2 == 0:
                                pe.wait_ge(h_ready.sem, h_ready.at(l, kt // 2 + 1))
                            for i in range(TT):
                                x_hi, x_lo = (hx[:, kt, b * T + i * P:b * T + (i + 1) * P] for b in range(2))
                                bank = bank2(U_TOK + j)[:, i, :]
                                pe.matmul(bank, x_hi, w_hi[:, 512 * a:512 * a + 512], start=kt == 0, stop=False)
                                pe.matmul(bank, x_lo, w_hi[:, 512 * a:512 * a + 512], start=False, stop=False)
                                mm = pe.matmul(bank, x_hi, w_lo[:, 512 * a:512 * a + 512], start=False, stop=kt == KT - 1)
                        mm.then_inc(slot_free, 1)

                def update(n):
                    if n >= 1:
                        pe.wait_ge(state_ready.sem, state_ready.at(l, 4 * n))
                    lanes, i = slice(64 * (n % 2), 64 * (n % 2) + 64), n // 2
                    for h in range(GH):
                        mm = pe.matmul(X[:, h // 2, (h % 2) * GDV:(h % 2 + 1) * GDV], gk[lanes, i, h * GDK:(h + 1) * GDK],
                                       gv[lanes, i, h * GDV:(h + 1) * GDV], start=True, stop=True)
                    mm.then_inc(update_done.sem, 1)

                def reads(n):
                    pe.wait_ge(state_ready.sem, state_ready.at(l, 4 * n + 4))
                    if n >= 1:
                        pe.wait_ge(reads_copied.sem, reads_copied.at(l, n))
                    for h in range(GH):
                        for e in range(2):
                            mm = pe.matmul(X[:, 2, (2 * h + e) * CHUNK:(2 * h + e + 1) * CHUNK],
                                           state[:, h, e * P:(e + 1) * P], z[:, Z_GQ + h, n * CHUNK:(n + 1) * CHUNK],
                                           start=True, stop=True)
                    mm.then_inc(reads_done.sem, 1)

                def c_sum(i):
                    pe.wait_ge(c_squared.sem, c_squared.at(l, i + 1))
                    for j in range(2):
                        mm = pe.matmul(X[:, 3, 0:T] if i < 2 else X[:, 3, T:2 * T], ones, sq[:, i % 2, j, :],
                                       start=i != 1 and j == 0, stop=i != 0 and j == 1)
                    mm.then_inc(c_square_used.sem, 1)

                def o_sum(h):
                    pe.wait_ge(o_squared.sem, o_squared.at(l, h + 1))
                    for e in range(2):
                        mm = pe.matmul(X[:, h, 0:T], ones, sq[:, h % 2, e, :], start=e == 0, stop=e == 1)
                    mm.then_inc(o_summed.sem, 1)

                norm_sums(0, in_squared, in_square_used, l)
                tokens_block(0)
                for h in range(2):
                    w_hi, w_lo = take(r, K_MISC + h)
                    for a in range(8):
                        kt = 8 * h + a
                        mm = tile_pass(X[0:80, 1, :], w_hi[:, 80 * a:80 * a + 80], w_lo[:, 80 * a:80 * a + 80],
                                       hx[:, kt, :], kt == 0, kt == KT - 1)
                    mm.then_inc(slot_free, 1)
                tokens_block(1)
                pe.wait_ge(misc_ready.sem, misc_ready.at(l, 1))
                pe.wait_ge(gate_landed.sem, gate_landed.at(l, 32))
                for i in range(TT):
                    mm = pe.matmul(X[:, 2 + i, :], zm[64:64 + RANK + 1, i * P:(i + 1) * P], wg[64:64 + RANK + 1, :],
                                   start=True, stop=True)
                mm.then_inc(gate_logits.sem, 1)
                tokens_block(2)
                pe.wait_ge(gate_log.sem, gate_log.at(l, 1))
                for i in range(TT):
                    pe.matmul(X[:, 2 + i, :], suf, la[:, i, :], start=True, stop=True)
                for h in range(GH):
                    for i in range(TT):
                        mm = pe.matmul(X[:, 1, 4 * h + 2 * i:4 * h + 2 * i + 2], la[:, i, h * GDK:(h + 1) * GDK], ind,
                                       start=True, stop=True)
                mm.then_inc(gate_sums.sem, 1)
                for i in range(9):
                    bank_free(ur, U_FEAT + i)
                    for h in range(2):
                        pair_chunk(r, K_FEAT + 2 * i + h, U_FEAT + i, h, hx, h == 0, h == 1)
                    if i == 1:
                        pe.wait_ge(keys_decayed.sem, keys_decayed.at(l, 1))
                        pe.wait_ge(gate_decay.sem, gate_decay.at(l, 2))
                    if 1 <= i <= 4:
                        update(i - 1)
                    if i == 2:
                        pe.wait_ge(unit_free, l * UNITS + U_FEAT + 2 + 2)
                    if 2 <= i <= 5:
                        reads(i - 2)
                    if 3 <= i <= 5:
                        c_sum(i - 3)
                    if i == 6:
                        pe.wait_ge(c_root.sem, c_root.at(l, 2))
                    if i in (7, 8):
                        o_sum(2 * i - 14)
                        o_sum(2 * i - 13)

                def uq(j):
                    w_hi, w_lo = take(r, K_UQ + j)
                    for i in range(3):
                        un = U_UQ + 2 * j + i // 2
                        if i != 1:
                            bank_free(ur, un)
                        for a in range(4):
                            at = a * 384 + i * P
                            mm = tile_pass(bank2(un)[:, i % 2, :], w_hi[:, at:at + P], w_lo[:, at:at + P],
                                           mid[:, a, :], a == 0, a == 3)
                        if i == 1:
                            mm.then_inc(unit_done, 1)
                    mm.then_inc(slot_free, 1)

                def ukv(j):
                    w_hi, w_lo = take(r, K_UKV + j)
                    for i in range(4):
                        un = U_UKV + 3 * j + i // 2
                        if i % 2 == 0:
                            bank_free(ur, un)
                        for a in range(2):
                            at = a * 1024 + i * 256
                            mm = tile_pass(bank2(un)[:, i % 2, :], w_hi[:, at:at + P], w_lo[:, at:at + P],
                                           mid[:, 4 + a, :], a == 0, a == 1)
                        if i % 2:
                            mm.then_inc(unit_done, 1)
                    un = U_UKV + 3 * j + 2
                    bank_free(ur, un)
                    for a in range(2):
                        wv_hi, wv_lo = (w[:, a * 1024:(a + 1) * 1024].rearrange("p (h c) -> p h c", h=4)[:, :, NOPE:]
                                        for w in (w_hi, w_lo))
                        for i in range(TT):
                            x_hi, x_lo = (mid[:, 4 + a, b * T + i * P:b * T + (i + 1) * P] for b in range(2))
                            bank = bank2(un)[:, i, :].rearrange("p (h c) -> p h c", h=4)
                            pe.matmul(bank, x_hi, wv_hi, start=a == 0, stop=False)
                            pe.matmul(bank, x_lo, wv_hi, start=False, stop=False)
                            mm = pe.matmul(bank, x_hi, wv_lo, start=False, stop=a == 1)
                    mm.then_inc(slot_free, 1)

                def qk_sum(j):
                    pe.wait_ge(qk_squared.sem, qk_squared.at(l, 2 * j + 2))
                    if j == 0:
                        pe.wait_ge(o_root.sem, o_root.at(l, 4))
                    elif 2 <= j < 6:
                        pe.wait_ge(qk_root.sem, qk_root.at(l, j - 1))
                    elif j >= 6:
                        pe.wait_ge(qk_normed.sem, qk_normed.at(l, 4 + 3 * (j - 5)))
                    for b in range(TT):
                        tokens = slice(b * P, (b + 1) * P)
                        for i in range(2):
                            where = X[:, j % 2, 2 * i + b:2 * i + b + 1]
                            pe.matmul(where, sq[:, 1, 0, tokens], sel[i][:, 0:1], start=True, stop=False)
                            mm = pe.matmul(where, sq[:, 0, i, tokens], ones[:, 0:1], start=False, stop=True)
                    mm.then_inc(qk_summed.sem, 1)

                def spread(j):
                    pe.wait_ge(diag_ready.sem, diag_ready.at(l, j - 3))
                    pe.matmul(X[:, j % 2, :], ones, diag.rearrange("p c t -> p (c t)"), start=True,
                              stop=True).then_inc(k_scale_spread.sem, 1)

                def exchange(j):
                    pe.wait_ge(qk_normed.sem, qk_normed.at(l, j + 1 if j < 4 else 4 + 3 * (j - 3)))
                    if j >= 2:
                        pe.wait_ge(rope_parts.sem, rope_parts.at(l, 2 * j - 2))
                    pe.matmul(X[:, 2 + j % 2, 0:T], rot, qkr[:, j, :], start=True, stop=True).then_inc(rope_turned.sem, 1)

                def out_g(i):
                    bank_free(ur, U_OUT + i)
                    pair_chunk(r, K_OUT + i, U_OUT + i, 1, hx, True, True)

                pe.wait_ge(c_ready.sem, c_ready.at(l, 3))
                uq(0)
                uq(1)
                uq(2)
                qk_sum(0)
                uq(3)
                qk_sum(1)
                exchange(0)
                ukv(0)
                qk_sum(2)
                exchange(1)
                ukv(1)
                qk_sum(3)
                exchange(2)
                pe.wait_ge(o_ready.sem, o_ready.at(l, GH))
                out_g(0)
                qk_sum(4)
                exchange(3)
                out_g(1)
                qk_sum(5)
                spread(4)
                out_g(2)
                qk_sum(6)
                spread(5)
                exchange(4)
                out_g(3)
                qk_sum(7)
                spread(6)
                exchange(5)
                spread(7)
                exchange(6)
                exchange(7)

                def scores(h):
                    if h >= 2:
                        pe.wait_ge(exps_done.sem, exps_done.at(l, 2 * h - 2))
                    lanes = slice(64 * (h % 2), 64 * (h % 2) + 64)
                    for b in range(TT):
                        where = X[:, h % 2, 0:P] if b == 0 else X[:, h % 2, P:3 * P]
                        qs, ks = slice(b * P, (b + 1) * P), slice(0, (b + 1) * P)
                        pe.matmul(where, qn[:, h, qs], kn[:, h, ks], start=True, stop=False)
                        mm = pe.matmul(where, qkr[lanes, h // 2, qs], qkr[lanes, 4 + h // 2, ks], start=False, stop=True)
                    mm.then_inc(scores_done.sem, 1)

                pe.wait_ge(rope_done.sem, rope_done.at(l, 8))
                scores(0)
                scores(1)
                for h in range(HEADS):
                    pe.wait_ge(probs_ready.sem, probs_ready.at(l, 2 * h + 2))
                    if h >= 1:
                        pe.wait_ge(probs_copied.sem, probs_copied.at(l, h))
                    for i in range(3):
                        mm = pe.transpose(X[:, 2, i * P:(i + 1) * P], prob[:, h % 2, i * P:(i + 1) * P], ident)
                    mm.then_inc(probs_turned.sem, 1)
                    if h + 2 < HEADS:
                        scores(h + 2)
                    if h % 2 == 0:
                        out_g(4 + h // 2)
                    pe.wait_ge(probs_copied.sem, probs_copied.at(l, h + 1))
                    if h >= 1:
                        pe.wait_ge(values_copied.sem, values_copied.at(l, h))
                    turned = probT[:, h % 2, :]
                    pe.matmul(X[:, 3, 0:T], v[:, 0, h * VD:(h + 1) * VD], turned[:, 0:T], start=True, stop=False)
                    pe.matmul(X[:, 3, P:T], v[:, 1, h * VD:(h + 1) * VD], turned[:, T:T + P], start=False,
                              stop=True).then_inc(values_done.sem, 1)
                pe.wait_ge(a_square_used.sem, a_square_used.at(l, 6))
                pe.matmul(X[:, 0, 0:T], ones, a_sum, start=True, stop=False)
                pe.wait_ge(a_squared.sem, a_squared.at(l, HEADS))
                pe.matmul(X[:, 0, 0:T], ones, a_sq[:, 1, :], start=False, stop=True).then_inc(a_summed.sem, 1)
                for i in range(8):
                    bank_free(ur, U_OUT + 8 + i)
                    pair_chunk(r, K_OUT + 8 + i, U_OUT + 8 + i, 0, hx, True, True, a_ready if i == 0 else None, a_ready.at(l, 0))
                norm_sums(1, ff_squared, ff_square_used, l)
                mlp_order(pe, l, up, down)
            pe.wait_ge(unit_free, UNITS * DEPTH + 2)
            for n in range(8):
                if n >= 4:
                    pe.wait_ge(out_copied, n - 3)
                for i in range(4):
                    mm = pe.transpose(X[:, n % 4, i * P:(i + 1) * P],
                                      xT[:, 4 * (n % 4) + i, (n // 4) * P:(n // 4 + 1) * P], ident)
                mm.then_inc(out_turned, 1)


def shape_constants():
    c = np.zeros((P, CONSTS), np.float32)
    at = np.arange(P)
    c[:, CO_ID:CO_ID + P] = np.eye(P)
    c[:, CO_ONES:CO_ONES + P] = 1
    for i in range(2):
        c[64 * i:64 * i + 64, CO_SEL + i * P:CO_SEL + (i + 1) * P] = 1
    c[:, CO_SUF:CO_SUF + P] = (at[:, None] > at[None, :]) & (at[:, None] // CHUNK == at[None, :] // CHUNK)
    for m in range(P):
        if m % ROPE < ROPE // 2:
            c[m + ROPE // 2, CO_ROT + m] = -1
        else:
            c[m - ROPE // 2, CO_ROT + m] = 1
    for i in range(2):
        c[64 * i:64 * i + 64, CO_IND + i] = 1
    c[:, CO_FREQ] = (ROPE_BASE ** (-(at % (ROPE // 2)) * 2.0 / ROPE)).astype(np.float32)
    c[:, CO_EPS] = EPS
    c[:, CO_EPSQ] = EPS * QK
    return c


def kernel(**inputs):
    import concourse.bacc as bacc
    from concourse.bass_utils import run_bass_kernel_spmd

    nc = bacc.Bacc("TRN2", target_bir_lowering=False, num_devices=1)
    arrays, aps = {}, {}
    for name, a in [*inputs.items(), ("consts", shape_constants())]:
        a = np.ascontiguousarray(a)
        arrays[f"in_{name}"] = a
        aps[name] = nc.dram_tensor(f"in_{name}", a.shape, mybir.dt.from_np(a.dtype), kind="ExternalInput").ap()
    out = nc.dram_tensor("out_0", (1, T, D), F32, kind="ExternalOutput").ap()
    trunk_program(nc, aps, out)
    r = run_bass_kernel_spmd(nc, [arrays], core_ids=[0])
    return r.results[0]["out_0"]
```

```python
from contextlib import ExitStack

import numpy as np

import concourse.bass as bass
from concourse import mybir

F32 = mybir.dt.float32
F32R = mybir.dt.float32r
I32 = mybir.dt.int32
ACT = mybir.ActivationFunctionType
ALU = mybir.AluOpType
AX_X = mybir.AxisListType.X

P = 128
T = 256
TT = T // P
D = 2048
KT = D // P
DEPTH = 2
EPS = 1e-6
NEG = -1e30

Q_LORA, KV_LORA, ROPE, NOPE, VD, HEADS = 512, 256, 64, 128, 128, 8
QK = NOPE + ROPE
GH, GDK, GDV, RANK, TAU, CHUNK = 4, 128, 256, 16, 16.0, 64
GK_W, GV_W = GH * GDK, GH * GDV
C_CQ, C_CKV = 0, Q_LORA
C_KR = C_CKV + KV_LORA
C_GQ = C_KR + ROPE
C_GK = C_GQ + GK_W
C_GV = C_GK + GK_W
C_A = C_GV + GV_W
C_G = C_A + RANK
D_FF = 5632
FT = D_FF // P
GROUP = 4
NG = FT // GROUP
CONV = 3

SLOTS = 3
WORDS = 2048

K_TOK = [0, 6, 10]
K_MISC = 4
K_FEAT = K_TOK[2] + 4
K_UKV = K_FEAT + 18
K_UQ = K_UKV + HEADS // 4
K_OUT = K_UQ + HEADS // 2
K_FFN = K_OUT + 16
GROUP_CHUNKS = 12
CHUNKS = K_FFN + NG * GROUP_CHUNKS
ROUNDS = CHUNKS // SLOTS
U_TOK = 0
U_FEAT = U_TOK + 3
U_UKV = U_FEAT + 9
U_UQ = U_UKV + 6
U_OUT = U_UQ + HEADS
U_FFN = U_OUT + 16
GROUP_UNITS = 12
UNITS = U_FFN + NG * GROUP_UNITS
PAIRS = UNITS // 2
assert DEPTH == 2
assert CHUNKS % SLOTS == 0 and UNITS % 2 == 0 and K_FFN % SLOTS == 0 and U_FFN % 2 == 0

FEAT_COLS = [C_GQ, C_GQ + 256, C_CQ, C_CQ + 256, C_CKV, C_G, C_G + 256, C_G + 512, C_G + 768]
Z_GQ, Z_CQ, Z_CKV, Z_G = 0, 4, 8, 10
H_FEAT, H_UKV, H_UQ, H_FFN = 0, 9, 13, 21
HALF_COPIES = H_FFN + NG * 4
MID_UNITS = 8 + NG * 4
ROW_LOADS = 11 + 3 * DEPTH
TWO_PI = 6.283185307179586
TURN_PARTS = (6.28125, 0.0019350051879882812, 3.01991598196686e-07)
NEARLY_PI = 3.1415925
ROUNDER = 12582912.0
ROPE_BASE = 10000.0

G_ATTN, G_FFN, G_CQ, G_CKV, G_MLA, G_GLA, G_QN, G_QR, G_KN, G_KR = 0, 16, 32, 36, 38, 46, 48, 49, 50, 51
GAINS = 52
FT2 = 2 * FT
PARAMS = GAINS + (CONV + 1) * FT2
CO_ID, CO_ONES, CO_SUF, CO_ROT, CO_IND = 0, P, 2 * P, 3 * P, 4 * P
CO_FREQ, CO_EPS, CO_EPSQ, CO_ONE_HOT = CO_IND + 2, CO_IND + 3, CO_IND + 4, CO_IND + 5
CONSTS = CO_ONE_HOT + 3


class Signal:

    def __init__(self, sem, n):
        self.sem, self.n = sem, n

    def at(self, turn, count):
        return turn * self.n + count


def trunk_program(nc, t, out):
    with ExitStack() as ctx:
        def sb(name, shape, dt=F32):
            return ctx.enter_context(nc.sbuf_tensor(name, shape, dt))

        def semaphore(name):
            return ctx.enter_context(nc.semaphore(name))

        def signal(name, n):
            return Signal(semaphore(name), n)

        raw = sb("raw", [P, SLOTS, WORDS])
        hi = sb("hi", [P, SLOTS, WORDS], F32R)
        lo = sb("lo", [P, SLOTS, WORDS], F32R)
        xT = sb("xT", [P, KT, T])
        hx = sb("hx", [P, KT, 2 * T], F32R)
        mid = sb("mid", [P, 2 * GROUP, 2 * T], F32R)
        z = sb("z", [P, 18, T])
        zm = sb("zm", [P, T])
        qkn = sb("qkn", [P, 16, T])
        gv = sb("gv", [P, TT, GV_W])
        v = sb("v", [P, TT, HEADS * VD])
        half = sb("half", [P, 2, 2, T])
        sq = sb("sq", [P, 2, 2, T])
        gains = sb("gains", [P, GAINS])
        conv_p = sb("conv_p", [P, CONV + 1, 2, GROUP])
        params_all = sb("params_all", [P, DEPTH, PARAMS])
        cst = sb("cst", [P, CONSTS])
        cos = sb("cos", [P, T])
        sin = sb("sin", [P, T])
        x_scale = sb("x_scale", [P, T])
        rs = sb("rs", [P, 2 * T])
        small = sb("small", [P, 68])

        xtok = [z[:, 0:8, :].rearrange("p a b -> p (a b)"), qkn[:, 0:8, :].rearrange("p a b -> p (a b)")]
        rows = gv[:, :, :].rearrange("p a b -> p (a b)")
        gk = qkn[:, 8:12, :].rearrange("p a b -> p (a b)").rearrange("p (t c) -> p t c", t=TT)
        la = qkn[:, 12:16, :].rearrange("p a b -> p (a b)").rearrange("p (t c) -> p t c", t=TT)
        state = v[:, 0, :].rearrange("p (h e) -> p h e", h=GH)
        oT = qkn[:, 0:8, :].rearrange("p (e h) t -> p e (h t)", e=2)
        qn = gv[:, :, :].rearrange("p a b -> p (a b)").rearrange("p (h t) -> p h t", t=T)
        kn = qkn[:, 8:16, :]
        rope_tmp = rs[:, :].rearrange("p (a t) -> p a t", a=2)
        diag = z[:, 8:10, :].rearrange("p a b -> p (a b)").rearrange("p (c t) -> p c t", t=P)
        sq_sum = z[:, 10:12, :]
        a_sq = z[:, 14:16, :]
        a_sum = z[:, 16, :]
        wg = z[:, 16:18, :].rearrange("p a b -> p (a b)")
        qkr = z[:, 0:8, :]
        prob = half[:, :, :, :].rearrange("p a b t -> p a (b t)")
        probT = sq[:, :, :, :].rearrange("p a b t -> p a (b t)")
        vflat = v[:, :, :].rearrange("p a b -> p (a b)")
        yg = vflat[:, 0:512].rearrange("p (a t) -> p a t", a=2)
        yu = vflat[:, 512:1024].rearrange("p (a t) -> p a t", a=2)
        qkn_flat = qkn[:, :, :].rearrange("p a b -> p (a b)")
        ubuf = [x[:, 0:2 * (T + CONV - 1)].rearrange("p (a t) -> p a t", a=2) for x in (vflat[:, 1024:2048], qkn_flat)]

        conv_all = params_all[:, :, GAINS:PARAMS].rearrange("p l (j s f) -> p l j s f", j=CONV + 1, s=2)
        ident = cst[:, CO_ID:CO_ID + P]
        ones = cst[:, CO_ONES:CO_ONES + P]
        to_column = [cst[:, CO_ONE_HOT + 1 - i:CO_ONE_HOT + 3 - i] for i in range(2)]
        suf = cst[:, CO_SUF:CO_SUF + P]
        rot = cst[:, CO_ROT:CO_ROT + P]
        ind = cst[:, CO_IND:CO_IND + 2]
        freq = cst[:, CO_FREQ:CO_FREQ + 1]
        eps = cst[:, CO_EPS:CO_EPS + 1]
        eps_q = cst[:, CO_EPSQ:CO_EPSQ + 1]
        decay = small[:, 0:16]
        top = small[:, 16:20]
        ntop = small[:, 20:24]
        sums = small[:, 24:28]
        rsum = small[:, 28:32]
        norms = small[:, 32:64]
        gain_qk = small[:, 64:65]
        x_scale_rows = small[:, 65:67]

        G = ctx.enter_context(nc.psum_tensor("G", [P, 4, 512], F32))
        X = ctx.enter_context(nc.psum_tensor("X", [P, 4, 512], F32))

        def h_slot(which, tile):
            return (tile + 8 * which) % KT

        def turn_of(j):
            return (j + 4) % 8

        def normed_at(j):
            order = [4, 5, 6, 0, 7, 1, 2, 3]
            return sum(3 if i >= 4 else 1 for i in order[:order.index(j) + 1])

        def gain(col):
            return gains[:, col:col + 1]

        def x_bank(s):
            return (X, G)[s // 4][:, s % 4, :]

        OUT_BY_ACT = 5

        def out_tok(n):
            return xtok[n % 2][:, (n // 2) * 512:(n // 2 + 1) * 512]

        def out_bank(n):
            return G[:, n % 4, :] if n < 6 else X[:, n % 4, :]

        def bank2(u):
            if u >= U_FFN and (u - U_FFN) % 4 >= 2:
                return X[:, 2 * (u % 2):2 * (u % 2) + 2, :]
            return G[:, 2 * (u % 2):2 * (u % 2) + 2, :]

        def head_parts(buf, k):
            rows = buf[:, k % SLOTS, 0:4 * 2 * QK].rearrange("p (a c) -> p a c", a=4)
            as_loaded = rows.rearrange("p a (h c) -> p a h c", h=2)
            for a, b in ((0, NOPE), (NOPE, QK)):
                used = rows[:, :, 2 * a:2 * b].rearrange("p a (h c) -> p a h c", h=2)
                yield used, as_loaded[:, :, :, a:b]

        raw_landed = [semaphore(f"raw_landed{s}") for s in range(SLOTS)]
        hi_ready = semaphore("hi_ready")
        lo_ready = semaphore("lo_ready")
        slot_free = semaphore("slot_free")
        unit_done = semaphore("unit_done")
        unit_free = semaphore("unit_free")
        half_copied = semaphore("half_copied")
        const_landed = semaphore("const_landed")
        rows_landed = semaphore("rows_landed")
        at_column_0 = semaphore("at_column_0")
        x_landed = semaphore("x_landed")
        zeroed = semaphore("zeroed")
        rows_turned = semaphore("rows_turned")
        rows_copied = semaphore("rows_copied")
        x_turned = semaphore("x_turned")
        x_copied = semaphore("x_copied")
        out_turned = semaphore("out_turned")
        out_copied = [semaphore(f"out_copied{i}") for i in range(2)]
        out_stored = semaphore("out_stored")
        params_set = signal("params_set", 1)
        gate_landed = signal("gate_landed", 32)
        misc_landed = [signal(f"misc_landed{i}", 16) for i in range(2)]
        in_squared = signal("in_squared", 8)
        in_square_used = signal("in_square_used", 6)
        ff_squared = signal("ff_squared", 8)
        ff_square_used = signal("ff_square_used", 6)
        norm_summed = signal("norm_summed", 2)
        norm_root = signal("norm_root", 3)
        norm_scale = signal("norm_scale", 3)
        h_high = signal("h_high", 32)
        h_ready = signal("h_ready", 32)
        misc_done = signal("misc_done", 1)
        misc_half = signal("misc_half", 1)
        misc_ready = signal("misc_ready", 1)
        misc_added = signal("misc_added", 1)
        z_scaled = signal("z_scaled", 9)
        c_squared = signal("c_squared", 3)
        c_square_used = signal("c_square_used", 3)
        c_root = signal("c_root", 2)
        c_scale = signal("c_scale", 1)
        c_scaled = signal("c_scaled", 6)
        c_high = signal("c_high", 3)
        c_ready = signal("c_ready", 3)
        gate_logits = signal("gate_logits", 1)
        gate_soft = signal("gate_soft", 3)
        gate_log = signal("gate_log", 1)
        gate_sums = signal("gate_sums", 1)
        gate_decay = signal("gate_decay", 2)
        keys_decayed = signal("keys_decayed", 1)
        update_done = signal("update_done", 4)
        state_ready = signal("state_ready", 16)
        reads_done = signal("reads_done", 4)
        reads_copied = signal("reads_copied", 4)
        o_squared = signal("o_squared", 4)
        o_summed = signal("o_summed", 4)
        o_root = signal("o_root", 4)
        o_scale = signal("o_scale", 4)
        o_scaled = signal("o_scaled", 8)
        g_silu = signal("g_silu", 1)
        o_gated = signal("o_gated", 4)
        o_high = signal("o_high", 4)
        o_ready = signal("o_ready", 4)
        kr_spread = signal("kr_spread", 2)
        qk_squared = signal("qk_squared", 16)
        qk_summed = signal("qk_summed", 8)
        qk_root = signal("qk_root", 8)
        qk_inverse = signal("qk_inverse", 8)
        diag_ready = signal("diag_ready", 4)
        k_scale_spread = signal("k_scale_spread", 4)
        gains_joined = signal("gains_joined", 1)
        qk_normed = signal("qk_normed", 16)
        rope_turned = signal("rope_turned", 8)
        rope_parts = signal("rope_parts", 16)
        rope_done = signal("rope_done", 8)
        scores_done = signal("scores_done", HEADS)
        scores_masked = signal("scores_masked", 2 * HEADS)
        tops_found = signal("tops_found", 2 * HEADS)
        tops_scaled = signal("tops_scaled", HEADS)
        exps_done = signal("exps_done", 2 * HEADS)
        sums_inverted = signal("sums_inverted", HEADS)
        probs_ready = signal("probs_ready", 2 * HEADS)
        probs_turned = signal("probs_turned", HEADS)
        probs_copied = signal("probs_copied", HEADS)
        values_done = signal("values_done", HEADS)
        values_copied = signal("values_copied", HEADS)
        a_squared = signal("a_squared", HEADS)
        a_square_used = signal("a_square_used", 6)
        a_summed = signal("a_summed", 1)
        a_root = signal("a_root", 1)
        a_scale = signal("a_scale", 1)
        a_scaled = signal("a_scaled", 8)
        a_high = signal("a_high", 4)
        a_ready = signal("a_ready", 4)
        x_added = semaphore("x_added")
        pads_zeroed = signal("pads_zeroed", 2)
        X_ADDS = U_FFN - U_OUT + NG * 8
        positions_landed = signal("positions_landed", 16)
        angle_step = signal("angle_step", 7)
        angle_small = signal("angle_small", 2)
        table_step = signal("table_step", 3)
        taps_set = signal("taps_set", 1)
        conv_step = signal("conv_step", 28)
        gate_done = signal("gate_done", 2)
        product_done = signal("product_done", 2)
        mid_high = signal("mid_high", 2)
        mid_ready = signal("mid_ready", 2)

        w_in = t["w_in"].rearrange("l (k p) n -> l p k n", p=P)
        w_uq = t["w_uq"].rearrange("l (k p) n -> l p k n", p=P)
        w_ukv = t["w_ukv"].rearrange("l (k p) n -> l p k n", p=P)
        w_out = t["w_out"].rearrange("l (k p) n -> l p k n", p=P)
        w_up = t["w_up"].rearrange("l (k p) n -> l p k n", p=P)
        w_down = t["w_down"].rearrange("l (k p) n -> l p k n", p=P)

        TURN_ROUNDS, TURN_PAIRS = 2 * GROUP_CHUNKS // SLOTS, GROUP_UNITS

        def mlp_order(e, l, up, down):
            r0, p0 = l * ROUNDS, l * PAIRS
            up(l, 0, 0, r0, K_FFN, p0, U_FFN)
            with e.Fori(0, (NG - 1) // 2) as j:
                r, p = r0 + j * TURN_ROUNDS, p0 + j * TURN_PAIRS
                up(l, 2 * j + 1, 1, r, K_FFN + 8, p, U_FFN + 4)
                down(l, 2 * j, 0, r, K_FFN + 16, p, U_FFN + 8)
                up(l, 2 * j + 2, 0, r, K_FFN + 20, p, U_FFN + 16)
                down(l, 2 * j + 1, 1, r, K_FFN + 28, p, U_FFN + 20)
            down(l, NG - 1, 0, r0, CHUNKS - 4, p0, UNITS - 8)

        block = ctx.enter_context(nc.Block())

        @block.sync
        def _(sp):
            def load(r, k, shape, src, at_start=False):
                n = shape[0] * shape[1]
                dst = raw[:, k % SLOTS, 0:n].rearrange("p (a b) -> p a b", a=shape[0])
                sp.wait_ge(lo_ready, r * SLOTS + k + 1)
                if at_start:
                    sp.sem_inc(at_column_0, 1)
                sp.dma_start(dst, src.rearrange("o p k n -> p (o k) n")).then_inc(raw_landed[k % SLOTS], 16)

            sp.dma_start(cst[:, :], t["consts"]).then_inc(const_landed, 16)
            for i in range(TT):
                sp.dma_start(xtok[i], t["x"][0, i * P:(i + 1) * P, :]).then_inc(x_landed, 16)

            def first_chunks(r, k, layer, which=(0, 1)):
                for q in which:
                    load(r, k + q, (4, 512), w_in[layer:layer + 1, :, 4 * q:4 * q + 4, C_GK:C_GK + 512])

            first_chunks(0, 0, 0, (0,))

            def row(l, at, n, src):
                sp.dma_start(rows[at:at + n, l * P:(l + 1) * P], src).then_inc(rows_landed, 16)

            def both_rows(at, n, src):
                sp.dma_start(rows[at:at + n, 0:DEPTH * P].rearrange("a (l b) -> a l b", l=DEPTH),
                             src.rearrange("l (a b) -> a l b", b=P)).then_inc(rows_landed, 16)

            for l in range(DEPTH):
                row(l, G_ATTN, 16, t["attn_norm"][(l + 1) % DEPTH].rearrange("(a b) -> a b", b=P))
            both_rows(G_FFN, 16, t["ffn_norm"])
            both_rows(G_CQ, 4, t["cq_norm"])
            both_rows(G_CKV, 2, t["ckv_norm"])
            both_rows(G_MLA, 8, t["mla_out_norm"])
            both_rows(G_GLA, 2, t["gla_out_norm"])
            for col, name in ((G_QN, "q_norm"), (G_KN, "k_norm")):
                both_rows(col, 1, t[name][:, 0:NOPE])
                for i in range(2):
                    dst = rows[col + 1:col + 2, 0:DEPTH * P].rearrange("a (l b) -> a l b", l=DEPTH)
                    sp.dma_start(dst[:, :, i * ROPE:(i + 1) * ROPE],
                                 t[name][:, NOPE:QK].rearrange("l (a b) -> a l b", b=ROPE)).then_inc(rows_landed, 16)
            for l in range(DEPTH):
                at = (DEPTH + l * (CONV + 1)) * P
                sp.dma_start(rows[0:FT2, at:at + CONV * P].rearrange("a (j b) -> a j b", j=CONV),
                             t["conv_w"][l].rearrange("j (a b) -> a j b", b=P)).then_inc(rows_landed, 16)
                sp.dma_start(rows[0:FT2, at + CONV * P:at + (CONV + 1) * P],
                             t["conv_b"][l].rearrange("(a b) -> a b", b=P)).then_inc(rows_landed, 16)

            def up(l, g, par, r, k, ur, u):
                for f in range(2):
                    for side in range(2):
                        for h in range(2):
                            load(r, k + 4 * f + 2 * side + h, (8, 256),
                                 w_up[bass.ds(l, 1), :, 8 * h:8 * h + 8,
                                      bass.ds(g * (GROUP * P) + (f * 256 + side * D_FF), 256)])

            def down(l, g, par, r, k, ur, u):
                for q in range(4):
                    load(r, k + q, (4, 512),
                         w_down[bass.ds(l, 1), :, bass.ds(g * GROUP, GROUP), 512 * q:512 * q + 512])

            first_chunks(0, 0, 0, (1,))
            with sp.Fori(0, DEPTH) as l:
                L, r = bass.ds(l, 1), l * ROUNDS
                def tokens_block(j, first=0):
                    for q in range(first, 4):
                        c0 = C_GK + 512 * j
                        load(r, K_TOK[j] + q, (4, 512), w_in[L, :, 4 * q:4 * q + 4, c0:c0 + 512])

                tokens_block(0, 2)
                for h in range(2):
                    k = K_MISC + h
                    dst = raw[:, k % SLOTS, 0:8 * 80].rearrange("p (a b) -> p a b", a=8)
                    sp.wait_ge(lo_ready, r * SLOTS + k + 1)
                    for a, b, c0 in ((0, ROPE, C_KR), (ROPE, ROPE + RANK, C_A)):
                        src = w_in[L, :, 8 * h:8 * h + 8, c0:c0 + b - a].rearrange("o p k n -> p (o k) n")
                        if a == 0:
                            sp.dma_start(dst[:, :, a:b], src).then_inc(raw_landed[k % SLOTS], 16)
                        else:
                            sp.dma_start(dst[:, :, a:b], src).then_inc(misc_landed[h].sem, 16)
                tokens_block(1)
                tokens_block(2)
                for i, c0 in enumerate(FEAT_COLS):
                    for h in range(2):
                        load(r, K_FEAT + 2 * i + h, (8, 256), w_in[L, :, 8 * h:8 * h + 8, c0:c0 + 256], c0 + h == 0)
                for j in range(2):
                    load(r, K_UKV + j, (2, 1024), w_ukv[L, :, :, 1024 * j:1024 * j + 1024])
                for j in range(4):
                    load(r, K_UQ + j, (4, 384), w_uq[L, :, :, 384 * j:384 * j + 384])
                for h in (1, 0):
                    for i in range(8):
                        load(r, K_OUT + 8 * (1 - h) + i, (8, 256), w_out[L, :, 8 * h:8 * h + 8, 256 * i:256 * i + 256],
                             i + h == 0)
                mlp_order(sp, l, up, down)
                first_chunks(r, CHUNKS, DEPTH - 1)
            for n in range(8):
                g, i = n // 2, n % 2
                if n < OUT_BY_ACT:
                    sp.wait_ge(out_copied[0], n + 1)
                else:
                    sp.wait_ge(out_copied[1], n + 1 - OUT_BY_ACT)
                sp.dma_start(out[0, i * P:(i + 1) * P, 512 * g:512 * g + 512], out_tok(n)).then_inc(out_stored, 16)
            sp.wait_ge(out_stored, 16 * 8)

        @block.gpsimd
        def _(pool):
            def sum_squares(squared, used, turn):
                for i in range(1, 7):
                    pool.wait_ge(squared.sem, squared.at(turn, i + 1))
                    if i > 1:
                        pool.wait_ge(used.sem, used.at(turn, i - 1))
                    pool.tensor_tensor(sq_sum, sq[:, 0, :, :] if i == 1 else sq_sum, sq[:, i % 2, :, :],
                                       ALU.add).then_inc(used.sem, 1)

            sum_squares(in_squared, in_square_used, 0)
            with pool.Fori(0, DEPTH) as l:
                pool.wait_ge(params_set.sem, params_set.at(l, 1))
                pool.dma_start(wg[64:64 + RANK, :], t["w_gate"][bass.ds(l, 1)].rearrange("o a b -> (o a) b")).then_inc(gate_landed.sem, 16)
                pool.dma_start(wg[64 + RANK:64 + RANK + 1, :], t["b_gate"][bass.ds(l, 1)]).then_inc(gate_landed.sem, 16)
                pool.dma_start(cos[:, :].bitcast(I32), t["positions"].to_broadcast([P, T])).then_inc(positions_landed.sem, 16)

                def o_gate(h):
                    o = oT[:, :, h * T:(h + 1) * T]
                    pool.wait_ge(o_scaled.sem, o_scaled.at(l, 2 * h + 2))
                    pool.tensor_tensor(o, o, z[:, Z_G + 2 * h:Z_G + 2 * h + 2, :], ALU.mult).then_inc(o_gated.sem, 1)

                def o_round_off(h):
                    m = 8 + 2 * h
                    pool.wait_ge(o_high.sem, o_high.at(l, h + 1))
                    pool.tensor_tensor(hx[:, m:m + 2, T:2 * T], oT[:, :, h * T:(h + 1) * T],
                                       hx[:, m:m + 2, 0:T].bitcast(F32), ALU.subtract).then_inc(o_ready.sem, 1)

                pool.wait_ge(g_silu.sem, g_silu.at(l, 1))
                o_gate(0)
                for h in range(1, GH):
                    o_gate(h)
                    o_round_off(h - 1)
                o_round_off(GH - 1)
                for h in range(1, HEADS - 1):
                    pool.wait_ge(a_squared.sem, a_squared.at(l, h + 1))
                    if h > 1:
                        pool.wait_ge(a_square_used.sem, a_square_used.at(l, h - 1))
                    pool.tensor_tensor(a_sum, a_sq[:, 0, :] if h == 1 else a_sum, a_sq[:, h % 2, :],
                                       ALU.add).then_inc(a_square_used.sem, 1)
                sum_squares(ff_squared, ff_square_used, l)
                sum_squares(in_squared, in_square_used, l + 1)

        @block.scalar
        def _(act):
            def a_square(l, h):
                act.wait_ge(values_copied.sem, values_copied.at(l, h + 1))
                if h >= 2:
                    act.wait_ge(a_square_used.sem, a_square_used.at(l, h - 1))
                act.activation(a_sq[:, h % 2, :], qn[:, h, :], ACT.Square).then_inc(a_squared.sem, 1)

            def split(r, k, l=None):
                n = WORDS
                if k in (K_MISC, K_MISC + 1):
                    n = 640
                    act.wait_ge(misc_landed[k - K_MISC].sem, misc_landed[k - K_MISC].at(l, 16))
                act.wait_ge(raw_landed[k % SLOTS], (r + k // SLOTS + 1) * 16)
                act.wait_ge(slot_free, r * SLOTS + k + 1)
                if K_UQ <= k < K_OUT:
                    for (_, part), (dst, _) in zip(head_parts(raw, k), head_parts(hi, k)):
                        ins = act.activation(dst, part, ACT.Copy)
                    ins.then_inc(hi_ready, 1)
                else:
                    act.activation(hi[:, k % SLOTS, 0:n], raw[:, k % SLOTS, 0:n], ACT.Copy).then_inc(hi_ready, 1)

            def copy_half(u, banks=2):
                act.activation(half[:, u % 2, 0:banks, :], bank2(u)[:, 0:banks, T:2 * T],
                               ACT.Copy).then_inc(half_copied, 1)

            def square_x(squared, used, turn, i):
                if i >= 2:
                    act.wait_ge(used.sem, used.at(turn, i - 1))
                act.activation(sq[:, i % 2, :, :], xT[:, 2 * i:2 * i + 2, :], ACT.Square).then_inc(squared.sem, 1)

            def norm_mean_root(l, which):
                act.wait_ge(norm_summed.sem, norm_summed.at(l, which + 1))
                act.activation(x_scale[:, :], X[:, which, 0:T], ACT.Sqrt, bias=eps, scale=1.0 / D).then_inc(norm_root.sem, 1)
                if which == 0:
                    act.activation(x_scale_rows, X[:, which, T:T + 2], ACT.Sqrt, bias=eps, scale=1.0 / D).then_inc(norm_root.sem, 1)

            def round_x(which, i, gain_at):
                for j in range(2):
                    tile = 2 * i + j
                    act.activation(hx[:, h_slot(which, tile), 0:T], xT[:, tile, :], ACT.Copy,
                                   scale=gain_at[:, tile:tile + 1]).then_inc(h_high.sem, 1)

            def mid_round(l, g, par, f):
                act.wait_ge(product_done.sem, product_done.at(l * NG + g, f + 1))
                m = GROUP * par + 2 * f
                act.activation(mid[:, m:m + 2, 0:T], yu, ACT.Copy).then_inc(mid_high.sem, 1)

            def up(l, g, par, r, k, ur, u):
                turn = l * NG + g
                for s in range(8):
                    split(r, k + s + 2)
                    f = s // 4
                    if k == K_FFN and s == 1:
                        norm_mean_root(l, 1)
                    if s % 4 == 2:
                        act.wait_ge(conv_step.sem, conv_step.at(turn, 14 * f + 7))
                        act.activation(yg, yg, ACT.Silu).then_inc(gate_done.sem, 1)
                    if s == 5:
                        mid_round(l, g, par, 0)
                    if s % 2:
                        act.wait_ge(slot_free, r * SLOTS + (k + s + 1 + SLOTS))
                        act.wait_ge(unit_free, ur * 2 + u + s // 2 + 1)
                        copy_half(u + s // 2)
                if k == K_FFN:
                    mid_round(l, g, par, 1)

            def down(l, g, par, r, k, ur, u):
                for q in range(4):
                    split(r, k + q + 2)
                    if q == 1 and k + 4 < CHUNKS:
                        mid_round(l, g + 1, 1 - par, 1)
                    if k + 4 == CHUNKS:
                        for i in ((), (0, 1), (2, 3), (4, 5, 6, 7))[q]:
                            act.wait_ge(unit_free, ur * 2 + u + i + 3)
                            square_x(in_squared, in_square_used, l + 1, i)
                            round_x(0, i, gains[:, G_ATTN:G_ATTN + KT])

            split(0, 0)
            for i in range(3):
                act.wait_ge(x_copied, i + 1)
                square_x(in_squared, in_square_used, 0, i)
            act.wait_ge(rows_copied, DEPTH)
            for i in range(8):
                act.wait_ge(x_copied, i + 1)
                round_x(0, i, params_all[:, DEPTH - 1, G_ATTN:G_ATTN + KT])
                if i == 1:
                    square_x(in_squared, in_square_used, 0, 3)
                    split(0, 1)
                if i % 2:
                    act.wait_ge(x_copied, 5 + i // 2)
                    square_x(in_squared, in_square_used, 0, 4 + i // 2)

            with act.Fori(0, DEPTH) as l:
                r = l * ROUNDS

                def copy_uq(j):
                    act.wait_ge(unit_done, l * MID_UNITS + 4 + j + 1)
                    copy_half(U_UQ + 2 * j)
                    split(r, K_UQ + j + 2)
                    act.wait_ge(slot_free, r * SLOTS + K_UQ + j + 1 + SLOTS)
                    copy_half(U_UQ + 2 * j + 1, 1)

                def copy_ukv(j):
                    for i in range(2):
                        act.wait_ge(unit_done, l * MID_UNITS + 2 * j + i + 1)
                        copy_half(U_UKV + 3 * j + i)
                        if i == 0:
                            split(r, K_UKV + j + 2)

                def o_square(h):
                    act.activation(sq[:, h % 2, :, :], oT[:, :, h * T:(h + 1) * T], ACT.Square).then_inc(o_squared.sem, 1)

                def o_mean_root(h):
                    act.wait_ge(o_summed.sem, o_summed.at(l, h + 1))
                    act.activation(rs[:, (h % 2) * T:(h % 2 + 1) * T], X[:, h, 0:T], ACT.Sqrt,
                                   bias=eps, scale=1.0 / GDV).then_inc(o_root.sem, 1)

                def o_round(h):
                    act.wait_ge(o_gated.sem, o_gated.at(l, h + 1))
                    act.activation(hx[:, 8 + 2 * h:10 + 2 * h, 0:T], oT[:, :, h * T:(h + 1) * T], ACT.Copy).then_inc(o_high.sem, 1)

                def qk_square(j):
                    u = U_UQ + 2 * j + 2 if j < 4 else U_UKV + (0, 1, 3, 4)[j - 4] + 1
                    act.wait_ge(unit_free, l * UNITS + u + 2)
                    if turn_of(j) >= 1:
                        act.wait_ge(qk_summed.sem, qk_summed.at(l, turn_of(j)))
                    heads = qn[:, 2 * j:2 * j + 2, :] if j < 4 else kn[:, 2 * j - 8:2 * j - 6, :]
                    act.activation(sq[:, 0, :, :], heads, ACT.Square).then_inc(qk_squared.sem, 1)
                    act.activation(sq[:, 1, 0, :], qkr[:, j, :], ACT.Square).then_inc(qk_squared.sem, 1)

                def qk_mean_root(j):
                    act.wait_ge(qk_summed.sem, qk_summed.at(l, turn_of(j) + 1))
                    act.activation(norms[:, 4 * j:4 * j + 4], X[:, j % 2, 0:4], ACT.Sqrt, bias=eps_q if j < 4 else eps,
                                   scale=1.0 if j < 4 else 1.0 / QK).then_inc(qk_root.sem, 1)

                for k in range(4):
                    split(r, k + 2, l)
                norm_mean_root(l, 0)
                for k in range(K_MISC, K_MISC + 2):
                    split(r, k + 2)
                act.wait_ge(slot_free, r * SLOTS + K_MISC + 2 + SLOTS)
                act.activation(rs[0:80, 0:T], X[0:80, 1, T:2 * T], ACT.Copy).then_inc(misc_half.sem, 1)
                for q in range(4):
                    split(r, K_TOK[1] + q + 2)
                act.wait_ge(gate_logits.sem, gate_logits.at(l, 1))
                act.activation(la, X[:, 2:4, :], ACT.Abs).then_inc(gate_soft.sem, 1)
                split(r, K_TOK[2] + 2)
                act.wait_ge(gate_soft.sem, gate_soft.at(l, 1))
                act.activation(la, la, ACT.Exp, scale=-1.0).then_inc(gate_soft.sem, 1)
                split(r, K_TOK[2] + 3)
                act.wait_ge(gate_soft.sem, gate_soft.at(l, 2))
                act.activation(la, la, ACT.Ln, bias=ones[:, 0:1]).then_inc(gate_soft.sem, 1)
                for q in range(2, 4):
                    split(r, K_TOK[2] + q + 2)
                act.wait_ge(angle_small.sem, angle_small.at(l, 1))
                act.activation(rs[:, 0:T], sin[:, :], ACT.Abs).then_inc(table_step.sem, 1)
                act.wait_ge(gate_sums.sem, gate_sums.at(l, 1))
                act.activation(la, X[:, 2:4, :], ACT.Exp, scale=1.0 / TAU).then_inc(gate_decay.sem, 1)
                act.activation(decay, X[:, 1, 0:16], ACT.Exp, scale=1.0 / TAU).then_inc(gate_decay.sem, 1)
                for i in range(9):
                    split(r, K_FEAT + 2 * i + 2)
                    split(r, K_FEAT + 2 * i + 3)
                    act.wait_ge(slot_free, r * SLOTS + K_FEAT + 2 * i + 2 + SLOTS)
                    copy_half(U_FEAT + i)
                    if i == 0:
                        act.wait_ge(angle_small.sem, angle_small.at(l, 2))
                        act.activation(cos[:, :], rs[:, T:2 * T], ACT.Sin).then_inc(table_step.sem, 1)
                        act.activation(sin[:, :], sin[:, :], ACT.Sin).then_inc(table_step.sem, 1)
                    if 2 <= i <= 4:
                        act.wait_ge(z_scaled.sem, z_scaled.at(l, i + 1))
                        if i == 4:
                            act.wait_ge(c_square_used.sem, c_square_used.at(l, 1))
                        act.activation(sq[:, i % 2, :, :], z[:, 2 * i:2 * i + 2, :], ACT.Square).then_inc(c_squared.sem, 1)
                    if i == 5:
                        act.wait_ge(c_square_used.sem, c_square_used.at(l, 3))
                        act.wait_ge(misc_ready.sem, misc_ready.at(l, 1))
                        act.activation(rs[:, 0:T], X[:, 3, 0:T], ACT.Sqrt, bias=eps, scale=1.0 / Q_LORA).then_inc(c_root.sem, 1)
                        act.activation(rs[:, T:2 * T], X[:, 3, T:2 * T], ACT.Sqrt, bias=eps, scale=1.0 / KV_LORA).then_inc(c_root.sem, 1)
                    if i == 6:
                        for n in range(3):
                            act.wait_ge(c_scaled.sem, c_scaled.at(l, 2 * n + 2))
                            act.activation(mid[:, 2 * n:2 * n + 2, 0:T], z[:, Z_CQ + 2 * n:Z_CQ + 2 * n + 2, :], ACT.Copy).then_inc(c_high.sem, 1)
                        act.wait_ge(reads_copied.sem, reads_copied.at(l, 4))
                        o_square(0)
                        o_square(1)
                    if i == 7:
                        o_mean_root(0)
                        o_mean_root(1)
                        o_square(2)
                        o_square(3)
                        act.wait_ge(c_ready.sem, c_ready.at(l, 3))
                        for i in range(2):
                            act.activation(qkr[64 * i:64 * i + 64, 4:8, :],
                                           zm[0:64, :].rearrange("p (o t) -> p o t", o=1).to_broadcast([64, 4, T]),
                                           ACT.Copy).then_inc(kr_spread.sem, 1)
                    if i == 8:
                        act.wait_ge(o_scaled.sem, o_scaled.at(l, 4))
                        o_mean_root(2)
                        o_mean_root(3)
                copy_ukv(0)
                act.wait_ge(z_scaled.sem, z_scaled.at(l, 9))
                act.activation(z[:, Z_G:Z_G + 8, :], z[:, Z_G:Z_G + 8, :], ACT.Silu).then_inc(g_silu.sem, 1)
                copy_ukv(1)
                act.wait_ge(kr_spread.sem, kr_spread.at(l, 2))
                qk_square(4)
                o_round(0)
                o_round(1)
                for j in range(4):
                    qk_mean_root(4 + j)
                    qk_square((5 + j) % 8)
                    copy_uq(j)
                    if j < 2:
                        o_round(2 + j)
                for j in range(4):
                    qk_mean_root(j)
                    if j < 3:
                        qk_square(j + 1)
                    split(r, K_OUT + j + 2)
                def exps(h):
                    act.wait_ge(tops_scaled.sem, tops_scaled.at(l, h + 1))
                    if h >= 2:
                        act.wait_ge(probs_turned.sem, probs_turned.at(l, h - 1))
                    for b in range(TT):
                        a0, a1 = (0, P) if b == 0 else (P, 3 * P)
                        at = 2 * (h % 2) + b
                        act.activation(prob[:, h % 2, a0:a1], X[:, h % 2, a0:a1], ACT.Exp,
                                       bias=ntop[:, at:at + 1], scale=norms[:, 2 * h + b:2 * h + b + 1],
                                       accum_out=sums[:, at:at + 1]).then_inc(exps_done.sem, 1)

                exps(0)
                split(r, K_OUT + 6)
                for h in range(HEADS):
                    if h + 1 < HEADS:
                        exps(h + 1)
                    act.wait_ge(probs_turned.sem, probs_turned.at(l, h + 1))
                    if h >= 2:
                        act.wait_ge(values_done.sem, values_done.at(l, h - 1))
                    act.activation(probT[:, h % 2, 0:3 * P], X[:, 2, 0:3 * P], ACT.Copy).then_inc(probs_copied.sem, 1)
                    if h in (1, 3, 5):
                        split(r, K_OUT + 7 + h // 2)
                    if h >= 1:
                        a_square(l, h - 1)
                act.activation(small[:, 67:68], eps, ACT.Sqrt)
                a_square(l, HEADS - 1)
                act.wait_ge(a_summed.sem, a_summed.at(l, 1))
                act.activation(rs[:, 0:T], X[:, 0, 0:T], ACT.Sqrt, bias=eps, scale=1.0 / (HEADS * VD)).then_inc(a_root.sem, 1)
                for i in range(4):
                    act.wait_ge(a_scaled.sem, a_scaled.at(l, 2 * i + 2))
                    act.activation(hx[:, 2 * i:2 * i + 2, 0:T], qn[:, 2 * i:2 * i + 2, :], ACT.Copy).then_inc(a_high.sem, 1)
                def x_pair(i):
                    act.wait_ge(unit_free, l * UNITS + U_OUT + 8 + i + 1 + 2)
                    square_x(ff_squared, ff_square_used, l, i)

                for i in range(8):
                    split(r, K_OUT + 8 + i + 2)
                    if i >= 1:
                        x_pair(i - 1)
                    if 1 <= i <= 4:
                        round_x(1, i - 1, gains[:, G_FFN:G_FFN + KT])
                act.wait_ge(slot_free, r * SLOTS + K_FFN + SLOTS)
                for i in range(4, 8):
                    if i == 7:
                        x_pair(7)
                    round_x(1, i, gains[:, G_FFN:G_FFN + KT])
                mlp_order(act, l, up, down)
            for n in range(OUT_BY_ACT):
                act.wait_ge(out_turned, n + 1)
                act.activation(out_tok(n), out_bank(n), ACT.Copy).then_inc(out_copied[0], 1)

        @block.vector
        def _(dve):
            def split(r, k):
                n = 640 if k in (K_MISC, K_MISC + 1) else WORDS
                s = k % SLOTS
                dve.wait_ge(hi_ready, r * SLOTS + k + 1)
                if K_UQ <= k < K_OUT:
                    for (_, part), (h, _), (dst, _) in zip(head_parts(raw, k), head_parts(hi, k), head_parts(lo, k)):
                        ins = dve.tensor_tensor(dst, part, h.bitcast(F32), ALU.subtract)
                    ins.then_inc(lo_ready, 1)
                else:
                    dve.tensor_tensor(lo[:, s, 0:n], raw[:, s, 0:n], hi[:, s, 0:n].bitcast(F32),
                                      ALU.subtract).then_inc(lo_ready, 1)

            def add_halves(u, dst, banks=2):
                dve.tensor_tensor(dst, bank2(u)[:, 0:banks, 0:T], half[:, u % 2, 0:banks, :],
                                  ALU.add).then_inc(unit_free, 1)

            def add_to_x(l, u, n, tile):
                two = xT[:, tile:tile + 2, :]
                dve.tensor_tensor(two, bank2(u)[:, :, 0:T], two, ALU.add).then_inc(x_added, 1)
                dve.wait_ge(x_added, l * X_ADDS + n + 1)
                dve.tensor_tensor(two, bank2(u)[:, :, T:2 * T], two, ALU.add).then_inc(unit_free, 1)

            def norm_scale_x(l, which):
                dve.wait_ge(norm_root.sem, norm_root.at(l, 2 + which))
                dve.reciprocal(x_scale[:, :], x_scale[:, :]).then_inc(norm_scale.sem, 1)
                if which == 0:
                    dve.reciprocal(x_scale_rows, x_scale_rows).then_inc(norm_scale.sem, 1)
                dve.wait_ge(norm_scale.sem, norm_scale.at(l, 2 + which))

            def round_off_x(turn, which, i, gain_at):
                dve.wait_ge(h_high.sem, h_high.at(turn, 16 * which + 2 * i + 2))
                for j in range(2):
                    tile = 2 * i + j
                    h = hx[:, h_slot(which, tile), :]
                    dve.scalar_tensor_tensor(h[:, T:2 * T], xT[:, tile, :], gain_at[:, tile:tile + 1],
                                             h[:, 0:T].bitcast(F32), ALU.mult, ALU.subtract).then_inc(h_ready.sem, 1)

            def scaled(two):
                return two, two, x_scale[:, :].rearrange("p (o t) -> p o t", o=1).to_broadcast([P, 2, T]), ALU.mult

            def gated_product(l, g, f):
                turn = l * NG + g
                dve.wait_ge(conv_step.sem, conv_step.at(turn, 14 * f + 14))
                dve.wait_ge(gate_done.sem, gate_done.at(turn, f + 1))
                dve.tensor_tensor(yu, yg, yu, ALU.mult).then_inc(product_done.sem, 1)

            def mid_round_off(l, g, par, f):
                m = GROUP * par + 2 * f
                dve.wait_ge(mid_high.sem, mid_high.at(l * NG + g, f + 1))
                dve.tensor_tensor(mid[:, m:m + 2, T:2 * T], yu, mid[:, m:m + 2, 0:T].bitcast(F32),
                                  ALU.subtract).then_inc(mid_ready.sem, 1)

            def up(l, g, par, r, k, ur, u):
                turn = l * NG + g
                if k > K_FFN:
                    dve.wait_ge(mid_ready.sem, mid_ready.at(turn, 0))
                dve.tensor_copy(conv_p[:, :, :, :], conv_all[:, bass.ds(l, 1), :, :, bass.ds(g * GROUP, GROUP)]
                                .rearrange("p o j s f -> p (o j) s f")).then_inc(taps_set.sem, 1)
                for s in range(8):
                    split(r, k + s + 2)
                    if s == 4:
                        gated_product(l, g, 0)
                    if s == 6:
                        mid_round_off(l, g, par, 0)
                    if s % 2 == 0:
                        continue
                    if k == K_FFN and s == 1:
                        norm_scale_x(l, 1)
                    f, side = s // 4, s // 2 % 2
                    ub, y = ubuf[side], (yg, yu)[side]
                    un = u + s // 2
                    dve.wait_ge(half_copied, l * HALF_COPIES + g * 4 + (H_FFN + s // 2 + 1))
                    if s == 5:
                        dve.wait_ge(product_done.sem, product_done.at(turn, 1))
                    if s == 7:
                        dve.wait_ge(mid_ready.sem, mid_ready.at(turn, 1))
                    add_halves(un, ub[:, :, CONV - 1:CONV - 1 + T])
                    dve.wait_ge(unit_free, ur * 2 + un + 3)
                    if s == 1:
                        dve.wait_ge(taps_set.sem, taps_set.at(turn, 1))
                    step = 14 * f + 7 * side
                    dve.tensor_tensor(*scaled(ub[:, :, CONV - 1:CONV - 1 + T])).then_inc(conv_step.sem, 1)
                    for n, j in enumerate((2, 1, 0)):
                        dve.wait_ge(conv_step.sem, conv_step.at(turn, step + 2 * n + 1))
                        for i in range(2):
                            tap = conv_p[:, j, side, 2 * f + i:2 * f + i + 1]
                            if n == 0:
                                dve.tensor_scalar(y[:, i, :], ub[:, i, j:j + T], tap,
                                                  conv_p[:, CONV, side, 2 * f + i:2 * f + i + 1],
                                                  ALU.mult, ALU.add).then_inc(conv_step.sem, 1)
                            else:
                                dve.scalar_tensor_tensor(y[:, i, :], ub[:, i, j:j + T], tap, y[:, i, :],
                                                         ALU.mult, ALU.add).then_inc(conv_step.sem, 1)
                if k == K_FFN:
                    gated_product(l, g, 1)
                    mid_round_off(l, g, par, 1)

            def down(l, g, par, r, k, ur, u):
                for q in range(4):
                    if k + q + 2 <= CHUNKS:
                        split(r, k + q + 2)
                    if q == 0 and k + 4 < CHUNKS:
                        gated_product(l, g + 1, 1)
                    if q == 2 and k + 4 < CHUNKS:
                        mid_round_off(l, g + 1, 1 - par, 1)
                    for i in range(2):
                        if i == 0:
                            dve.wait_ge(unit_done, l * MID_UNITS + g * 4 + (8 + q + 1))
                        else:
                            dve.wait_ge(slot_free, r * SLOTS + (k + q + 1 + SLOTS))
                        add_to_x(l, u + 2 * q + i, g * 8 + (16 + 2 * q + i), 4 * q + 2 * i)
                    if k + q + 2 > CHUNKS:
                        split(r, k + q + 2)
                    if k + 4 == CHUNKS and q >= 1:
                        round_off_x(l + 1, 0, 2 * q - 2, gains[:, G_ATTN:G_ATTN + KT])
                        round_off_x(l + 1, 0, 2 * q - 1, gains[:, G_ATTN:G_ATTN + KT])
                if k + 4 == CHUNKS:
                    round_off_x(l + 1, 0, 6, gains[:, G_ATTN:G_ATTN + KT])
                    round_off_x(l + 1, 0, 7, gains[:, G_ATTN:G_ATTN + KT])

            dve.sem_inc(lo_ready, SLOTS)
            dve.sem_inc(unit_free, 2)
            dve.memset(zm[64:96, :], 1.0).then_inc(zeroed, 1)
            dve.wait_ge(zeroed, 1)
            def x_out(s):
                dve.wait_ge(x_turned, s + 1)
                dve.tensor_copy(xT[:, 2 * s:2 * s + 2, :], x_bank(s).rearrange("p (a t) -> p a t", a=2)).then_inc(x_copied, 1)

            for s in range(4):
                x_out(s)
            split(0, 0)
            for l in range(DEPTH):
                dve.wait_ge(rows_turned, l + 1)
                dve.tensor_copy(params_all[:, l, :], X[:, l, 0:PARAMS]).then_inc(rows_copied, 1)
            x_out(4)
            x_out(5)
            dve.wait_ge(rows_copied, DEPTH)
            for i in range(8):
                round_off_x(0, 0, i, params_all[:, DEPTH - 1, G_ATTN:G_ATTN + KT])
                if i == 0:
                    x_out(6)
                    x_out(7)
                if i == 1:
                    split(0, 1)

            with dve.Fori(0, DEPTH) as l:
                r, ur = l * ROUNDS, l * PAIRS
                dve.wait_ge(h_ready.sem, h_ready.at(l, 16))
                dve.tensor_copy(gains[:, :], params_all[:, bass.ds(l, 1), 0:GAINS]
                                .rearrange("p o g -> p (o g)")).then_inc(params_set.sem, 1)
                dve.wait_ge(params_set.sem, params_set.at(l, 1))
                def tokens_out(j):
                    for q in range(4):
                        split(r, K_TOK[j] + q + 2)
                        if j == 2 and q == 1:
                            dve.wait_ge(gate_soft.sem, gate_soft.at(l, 3))
                            dve.scalar_tensor_tensor(la, X[:, 2:4, :], 0.0, la, ALU.min, ALU.subtract).then_inc(gate_log.sem, 1)
                    dve.wait_ge(slot_free, r * SLOTS + K_TOK[j] + 4 + SLOTS)
                    if j == 0:
                        norm_scale_x(l, 0)
                    dst = gk if j == 0 else gv[:, :, 512 * (j - 1):512 * j]
                    for b in range(TT):
                        ins = dve.tensor_scalar(dst[:, b, :], bank2(U_TOK + j)[:, b, :], x_scale_rows[:, b:b + 1], None, ALU.mult)
                    ins.then_inc(unit_free, 1)

                def state_step(n):
                    dve.wait_ge(update_done.sem, update_done.at(l, n + 1))
                    if n >= 1:
                        dve.wait_ge(reads_done.sem, reads_done.at(l, n))
                        dve.wait_ge(state_ready.sem, state_ready.at(l, 4 * n))
                    for h in range(GH):
                        new = X[:, h // 2, (h % 2) * GDV:(h % 2 + 1) * GDV]
                        if n == 0:
                            dve.tensor_copy(state[:, h, :], new).then_inc(state_ready.sem, 1)
                        else:
                            dve.scalar_tensor_tensor(state[:, h, :], state[:, h, :], decay[:, 4 * h + n:4 * h + n + 1],
                                                     new, ALU.mult, ALU.add).then_inc(state_ready.sem, 1)

                def copy_reads(n):
                    dve.wait_ge(reads_done.sem, reads_done.at(l, n + 1))
                    o_chunk = oT.rearrange("p e (h t) -> p h e t", h=GH)[:, :, :, n * CHUNK:(n + 1) * CHUNK]
                    dve.tensor_scalar(o_chunk, X[:, 2, :].rearrange("p (h e t) -> p h e t", h=GH, e=2),
                                      GDK ** -0.5, None, ALU.mult).then_inc(reads_copied.sem, 1)

                def o_normed(h):
                    s = rs[:, (h % 2) * T:(h % 2 + 1) * T]
                    dve.wait_ge(o_root.sem, o_root.at(l, h + 1))
                    dve.reciprocal(s, s).then_inc(o_scale.sem, 1)
                    dve.wait_ge(o_scale.sem, o_scale.at(l, h + 1))
                    for e in range(2):
                        o = oT[:, e, h * T:(h + 1) * T]
                        dve.scalar_tensor_tensor(o, o, gain(G_GLA + e), s, ALU.mult, ALU.mult).then_inc(o_scaled.sem, 1)

                tokens_out(0)
                for s in range(2):
                    split(r, K_MISC + s + 2)
                dve.wait_ge(misc_half.sem, misc_half.at(l, 1))
                dve.tensor_tensor(zm[0:80, :], X[0:80, 1, 0:T], rs[0:80, 0:T], ALU.add).then_inc(misc_added.sem, 1)
                dve.wait_ge(misc_added.sem, misc_added.at(l, 1))
                dve.tensor_tensor(zm[0:80, :], zm[0:80, :], x_scale[0:80, :], ALU.mult).then_inc(misc_ready.sem, 1)
                dve.tensor_tensor(gain_qk, gain(G_QN), gain(G_KN), ALU.mult).then_inc(gains_joined.sem, 1)
                tokens_out(1)
                dve.wait_ge(positions_landed.sem, positions_landed.at(l, 16))
                dve.wait_ge(misc_ready.sem, misc_ready.at(l, 1))
                dve.tensor_copy(rs[:, 0:T], cos[:, :].bitcast(I32)).then_inc(angle_step.sem, 1)
                dve.wait_ge(angle_step.sem, angle_step.at(l, 1))
                dve.tensor_scalar(sin[:, :], rs[:, 0:T], freq, None, ALU.mult).then_inc(angle_step.sem, 1)
                dve.wait_ge(angle_step.sem, angle_step.at(l, 2))
                dve.tensor_scalar(rs[:, T:2 * T], sin[:, :], 1.0 / TWO_PI, ROUNDER, ALU.mult, ALU.add).then_inc(angle_step.sem, 1)
                dve.wait_ge(angle_step.sem, angle_step.at(l, 3))
                dve.tensor_scalar(rs[:, T:2 * T], rs[:, T:2 * T], ROUNDER, None, ALU.subtract).then_inc(angle_step.sem, 1)
                for i, part in enumerate(TURN_PARTS):
                    dve.wait_ge(angle_step.sem, angle_step.at(l, 4 + i))
                    dve.scalar_tensor_tensor(sin[:, :], rs[:, T:2 * T], -part, sin[:, :], ALU.mult, ALU.add).then_inc(angle_step.sem, 1)
                dve.wait_ge(angle_step.sem, angle_step.at(l, 7))
                dve.tensor_scalar(sin[:, :], sin[:, :], NEARLY_PI, -NEARLY_PI, ALU.min, ALU.max).then_inc(angle_small.sem, 1)
                tokens_out(2)
                dve.wait_ge(gate_decay.sem, gate_decay.at(l, 1))
                dve.tensor_tensor(gk, gk, la, ALU.mult).then_inc(keys_decayed.sem, 1)
                dve.wait_ge(table_step.sem, table_step.at(l, 1))
                dve.tensor_scalar(rs[:, T:2 * T], rs[:, 0:T], -1.0, TWO_PI / 4, ALU.mult, ALU.add).then_inc(angle_small.sem, 1)
                dve.wait_ge(gate_decay.sem, gate_decay.at(l, 2))
                for i in range(9):
                    split(r, K_FEAT + 2 * i + 2)
                    split(r, K_FEAT + 2 * i + 3)
                    dve.wait_ge(half_copied, l * HALF_COPIES + H_FEAT + i + 1)
                    add_halves(U_FEAT + i, z[:, 2 * i:2 * i + 2, :])
                    dve.wait_ge(unit_free, l * UNITS + U_FEAT + i + 1 + 2)
                    dve.tensor_tensor(*scaled(z[:, 2 * i:2 * i + 2, :])).then_inc(z_scaled.sem, 1)
                    if 1 <= i <= 4:
                        state_step(i - 1)
                    if 2 <= i <= 5:
                        copy_reads(i - 2)
                    if i == 5:
                        dve.wait_ge(c_root.sem, c_root.at(l, 2))
                        dve.reciprocal(rs[:, :], rs[:, :]).then_inc(c_scale.sem, 1)
                        dve.wait_ge(c_scale.sem, c_scale.at(l, 1))
                        for n in range(6):
                            tile = z[:, Z_CQ + n, :]
                            dve.scalar_tensor_tensor(tile, tile, gain(G_CQ + n), rs[:, 0:T] if n < 4 else rs[:, T:2 * T],
                                                     ALU.mult, ALU.mult).then_inc(c_scaled.sem, 1)
                    if i == 6:
                        for n in range(3):
                            dve.wait_ge(c_high.sem, c_high.at(l, n + 1))
                            dve.tensor_tensor(mid[:, 2 * n:2 * n + 2, T:2 * T], z[:, Z_CQ + 2 * n:Z_CQ + 2 * n + 2, :],
                                              mid[:, 2 * n:2 * n + 2, 0:T].bitcast(F32), ALU.subtract).then_inc(c_ready.sem, 1)
                    if i == 7:
                        o_normed(0)
                        o_normed(1)
                dve.wait_ge(c_ready.sem, c_ready.at(l, 3))

                def uq_out(j):
                    dve.wait_ge(half_copied, l * HALF_COPIES + H_UQ + 2 * j + 1)
                    add_halves(U_UQ + 2 * j, qn[:, 2 * j:2 * j + 2, :])
                    split(r, K_UQ + j + 2)
                    dve.wait_ge(half_copied, l * HALF_COPIES + H_UQ + 2 * j + 2)
                    add_halves(U_UQ + 2 * j + 1, qkr[:, j:j + 1, :], 1)

                def ukv_out(j):
                    for i in range(2):
                        dve.wait_ge(half_copied, l * HALF_COPIES + H_UKV + 2 * j + i + 1)
                        add_halves(U_UKV + 3 * j + i, kn[:, 4 * j + 2 * i:4 * j + 2 * i + 2, :])
                        if i == 0:
                            split(r, K_UKV + j + 2)
                    dve.wait_ge(slot_free, r * SLOTS + K_UKV + j + 1 + SLOTS)
                    dve.tensor_copy(v[:, :, 512 * j:512 * j + 512], bank2(U_UKV + 3 * j + 2)).then_inc(unit_free, 1)

                def q_gain(j):
                    dve.wait_ge(qk_squared.sem, qk_squared.at(l, 2 * turn_of(j) + 2))
                    dve.tensor_scalar(qkr[:, j, :], qkr[:, j, :], gain(G_QR), None, ALU.mult).then_inc(qk_normed.sem, 1)

                def inverse(j):
                    dve.wait_ge(qk_root.sem, qk_root.at(l, turn_of(j) + 1))
                    dve.reciprocal(norms[:, 4 * j:4 * j + 4], norms[:, 4 * j:4 * j + 4]).then_inc(qk_inverse.sem, 1)

                def k_diagonals(j):
                    inverse(j)
                    dve.wait_ge(qk_inverse.sem, qk_inverse.at(l, turn_of(j) + 1))
                    if j >= 5:
                        dve.wait_ge(k_scale_spread.sem, k_scale_spread.at(l, j - 4))
                    dve.tensor_tensor(diag, ident.rearrange("p (o t) -> p o t", o=1).to_broadcast([P, 4, P]),
                                      norms[:, 4 * j:4 * j + 4].rearrange("p (c o) -> p c o", o=1).to_broadcast([P, 4, P]),
                                      ALU.mult).then_inc(diag_ready.sem, 1)

                def k_normed(j):
                    dve.wait_ge(k_scale_spread.sem, k_scale_spread.at(l, j - 3))
                    two = kn[:, 2 * j - 8:2 * j - 6, :]
                    dve.scalar_tensor_tensor(two, two, gain_qk, X[:, j % 2, :].rearrange("p (a t) -> p a t", a=2),
                                             ALU.mult, ALU.mult).then_inc(qk_normed.sem, 1)
                    for i in range(2):
                        lanes = slice(64 * i, 64 * i + 64)
                        one = qkr[lanes, j, :]
                        dve.scalar_tensor_tensor(one, one, gains[lanes, G_KR:G_KR + 1], X[lanes, j % 2, i * T:(i + 1) * T],
                                                 ALU.mult, ALU.mult).then_inc(qk_normed.sem, 1)

                def rope(j):
                    n = turn_of(j)
                    dve.wait_ge(rope_turned.sem, rope_turned.at(l, n + 1))
                    if n >= 2:
                        dve.wait_ge(rope_done.sem, rope_done.at(l, n - 1))
                    dve.wait_ge(qk_normed.sem, qk_normed.at(l, normed_at(j)))
                    dve.tensor_tensor(rope_tmp[:, j % 2, :], X[:, 2 + j % 2, 0:T], sin[:, :],
                                      ALU.mult).then_inc(rope_parts.sem, 1)
                    dve.tensor_tensor(qkr[:, j, :], qkr[:, j, :], cos[:, :], ALU.mult).then_inc(rope_parts.sem, 1)
                    dve.wait_ge(rope_parts.sem, rope_parts.at(l, 2 * n + 2))
                    dve.tensor_tensor(qkr[:, j, :], qkr[:, j, :], rope_tmp[:, j % 2, :], ALU.add).then_inc(rope_done.sem, 1)

                def out_g(i):
                    dve.wait_ge(slot_free, r * SLOTS + K_OUT + i + 1 + SLOTS)
                    add_to_x(l, U_OUT + i, i, 2 * i)

                dve.wait_ge(table_step.sem, table_step.at(l, 3))
                ukv_out(0)
                o_normed(2)
                ukv_out(1)
                o_normed(3)
                dve.wait_ge(o_scaled.sem, o_scaled.at(l, 2 * GH))
                k_diagonals(4)
                uq_out(0)
                k_diagonals(5)
                k_normed(4)
                uq_out(1)
                k_diagonals(6)
                k_normed(5)
                rope(4)
                uq_out(2)
                k_diagonals(7)
                k_normed(6)
                rope(5)
                uq_out(3)
                inverse(0)
                q_gain(0)
                k_normed(7)
                rope(6)
                split(r, K_OUT + 2)
                out_g(0)
                inverse(1)
                q_gain(1)
                rope(7)
                rope(0)
                split(r, K_OUT + 3)
                out_g(1)
                inverse(2)
                q_gain(2)
                rope(1)
                split(r, K_OUT + 4)
                out_g(2)
                inverse(3)
                q_gain(3)
                rope(2)
                split(r, K_OUT + 5)
                out_g(3)
                rope(3)

                def find_top(h):
                    dve.wait_ge(scores_done.sem, scores_done.at(l, h + 1))
                    dve.memset(X[0:CHUNK, h % 2, P - CHUNK:P], NEG).then_inc(scores_masked.sem, 1)
                    dve.memset(X[0:CHUNK, h % 2, 3 * P - CHUNK:3 * P], NEG).then_inc(scores_masked.sem, 1)
                    dve.wait_ge(scores_masked.sem, scores_masked.at(l, 2 * h + 2))
                    at = 2 * (h % 2)
                    dve.tensor_reduce(top[:, at:at + 1], X[:, h % 2, 0:P], AX_X, ALU.max).then_inc(tops_found.sem, 1)
                    dve.tensor_reduce(top[:, at + 1:at + 2], X[:, h % 2, P:3 * P], AX_X, ALU.max).then_inc(tops_found.sem, 1)
                    dve.wait_ge(tops_found.sem, tops_found.at(l, 2 * h + 2))
                    dve.scalar_tensor_tensor(ntop[:, at:at + 2], top[:, at:at + 2], -1.0, norms[:, 2 * h:2 * h + 2],
                                             ALU.mult, ALU.mult).then_inc(tops_scaled.sem, 1)

                def copy_values(h):
                    dve.wait_ge(values_done.sem, values_done.at(l, h + 1))
                    dve.tensor_copy(qn[:, h, :], X[:, 3, 0:T]).then_inc(values_copied.sem, 1)

                dve.wait_ge(qk_inverse.sem, qk_inverse.at(l, 8))
                def probs_normed(h):
                    at = 2 * (h % 2)
                    dve.wait_ge(exps_done.sem, exps_done.at(l, 2 * h + 2))
                    dve.reciprocal(rsum[:, at:at + 2], sums[:, at:at + 2]).then_inc(sums_inverted.sem, 1)
                    dve.wait_ge(sums_inverted.sem, sums_inverted.at(l, h + 1))
                    for b in range(TT):
                        part = prob[:, h % 2, 0:P] if b == 0 else prob[:, h % 2, P:3 * P]
                        dve.tensor_scalar(part, part, rsum[:, at + b:at + b + 1], None, ALU.mult).then_inc(probs_ready.sem, 1)

                find_top(0)
                find_top(1)
                probs_normed(0)
                split(r, K_OUT + 6)
                for h in range(HEADS):
                    if h + 1 < HEADS:
                        probs_normed(h + 1)
                    if h + 2 < HEADS:
                        find_top(h + 2)
                    if h >= 1:
                        copy_values(h - 1)
                    if h in (1, 3, 5):
                        split(r, K_OUT + 7 + h // 2)
                        out_g(4 + h // 2)
                copy_values(HEADS - 1)
                dve.wait_ge(a_root.sem, a_root.at(l, 1))
                dve.reciprocal(rs[:, 0:T], rs[:, 0:T]).then_inc(a_scale.sem, 1)
                dve.wait_ge(a_scale.sem, a_scale.at(l, 1))

                def a_round_off(i):
                    dve.wait_ge(a_high.sem, a_high.at(l, i + 1))
                    dve.tensor_tensor(hx[:, 2 * i:2 * i + 2, T:2 * T], qn[:, 2 * i:2 * i + 2, :],
                                      hx[:, 2 * i:2 * i + 2, 0:T].bitcast(F32), ALU.subtract).then_inc(a_ready.sem, 1)

                for h in range(HEADS):
                    dve.scalar_tensor_tensor(qn[:, h, :], qn[:, h, :], gain(G_MLA + h), rs[:, 0:T],
                                             ALU.mult, ALU.mult).then_inc(a_scaled.sem, 1)
                    if h in (3, 5, 7):
                        a_round_off(h // 2 - 1)
                a_round_off(3)
                out_g(7)
                for i in range(8):
                    if i < 7:
                        split(r, K_OUT + 8 + i + 2)
                    dve.wait_ge(slot_free, r * SLOTS + K_OUT + 8 + i + 1 + SLOTS)
                    add_to_x(l, U_OUT + 8 + i, 8 + i, 2 * i)
                    if i == 7:
                        split(r, K_OUT + 8 + i + 2)
                    if 1 <= i <= 4:
                        round_off_x(l, 1, i - 1, gains[:, G_FFN:G_FFN + KT])
                for side in range(2):
                    dve.memset(ubuf[side][:, :, 0:CONV - 1], 0.0).then_inc(pads_zeroed.sem, 1)
                dve.wait_ge(pads_zeroed.sem, pads_zeroed.at(l, 2))
                for i in range(4, 8):
                    round_off_x(l, 1, i, gains[:, G_FFN:G_FFN + KT])
                mlp_order(dve, l, up, down)
                dve.wait_ge(unit_free, l * UNITS + UNITS + 2)
            for n in range(OUT_BY_ACT, 8):
                dve.wait_ge(out_turned, n + 1)
                dve.tensor_copy(out_tok(n), out_bank(n)).then_inc(out_copied[1], 1)

        @block.tensor
        def _(pe):
            def take(r, k):
                pe.wait_ge(lo_ready, r * SLOTS + (k + 1 + SLOTS))
                return hi[:, k % SLOTS, :], lo[:, k % SLOTS, :]

            def tile_pass(bank, w_hi, w_lo, x2, first, last):
                pe.matmul(bank, w_hi, x2, start=first, stop=False)
                return pe.matmul(bank[:, T:2 * T], w_lo, x2[:, 0:T], start=False, stop=last)

            def norm_sums(l, which, squared, used, turn):
                if which == 0:
                    pe.wait_ge(unit_free, l * UNITS + 2)
                pe.wait_ge(used.sem, used.at(turn, 6))
                pe.wait_ge(squared.sem, squared.at(turn, 8))
                squares = [sq_sum[:, 0, :], sq_sum[:, 1, :], sq[:, 1, 0, :], sq[:, 1, 1, :]]
                for n, x in enumerate(squares):
                    mm = pe.matmul(X[:, which, 0:T], ones, x, start=n == 0, stop=n == 3)
                if which == 0:
                    for b in range(TT):
                        for n, x in enumerate(squares):
                            mm = pe.matmul(X[:, which, T + b:T + b + 1], x[:, b * P:(b + 1) * P], ones[:, 0:1],
                                           start=n == 0, stop=n == 3)
                mm.then_inc(norm_summed.sem, 1)

            def bank_free(ur, u):
                pe.wait_ge(unit_free, ur * 2 + (u + 3 - (2 if u < U_FFN + 2 else 4)))

            def pair_chunk(r, k, u, slots, first, last, ready=None, ready_at=0, tiles=(0, 1)):
                w_hi, w_lo = take(r, k)
                for i in tiles:
                    for a in range(8):
                        if ready is not None and i == 0 and a % 2 == 0:
                            pe.wait_ge(ready.sem, ready_at + (a + 2) // (1 if ready is h_ready else 2))
                        at = a * 256 + i * P
                        mm = tile_pass(bank2(u)[:, i, :], w_hi[:, at:at + P], w_lo[:, at:at + P],
                                       hx[:, slots + a, :], first and a == 0, last and a == 7)
                if 1 in tiles:
                    mm.then_inc(slot_free, 1)

            def up(l, g, par, r, k, ur, u):
                for s in range(8):
                    un = u + s // 2
                    if s % 2 == 0:
                        bank_free(ur, un)
                    fresh = k == K_FFN and s < 2
                    if k == K_FFN and s == 4:
                        pe.wait_ge(norm_root.sem, norm_root.at(l, 3))
                    pair_chunk(r, k + s, un, h_slot(1, 8 * (s % 2)), s % 2 == 0, s % 2 == 1,
                               h_ready if fresh else None, h_ready.at(l, 16 + 8 * s))
                    if k == K_FFN and s == 1:
                        norm_sums(l, 1, ff_squared, ff_square_used, l)

            def down(l, g, par, r, k, ur, u):
                pe.wait_ge(mid_ready.sem, mid_ready.at(l * NG + g, 2))
                for q in range(4):
                    w_hi, w_lo = take(r, k + q)
                    for i in range(4):
                        un = u + 2 * q + i // 2
                        if i % 2 == 0:
                            bank_free(ur, un)
                        for a in range(GROUP):
                            at = a * 512 + i * P
                            mm = tile_pass(bank2(un)[:, i % 2, :], w_hi[:, at:at + P], w_lo[:, at:at + P],
                                           mid[:, GROUP * par + a, :], a == 0, a == GROUP - 1)
                        if i == 1:
                            mm.then_inc(unit_done, 1)
                    mm.then_inc(slot_free, 1)

            pe.sem_inc(slot_free, SLOTS)
            pe.wait_ge(const_landed, 16)
            pe.wait_ge(x_landed, 32)
            for s in range(8):
                for j in range(2):
                    for i in range(TT):
                        mm = pe.transpose(x_bank(s)[:, j * T + i * P:j * T + (i + 1) * P],
                                          xtok[i][:, (2 * s + j) * P:(2 * s + j + 1) * P], ident)
                mm.then_inc(x_turned, 1)
            pe.wait_ge(rows_landed, ROW_LOADS * 16)
            for l in range(DEPTH):
                pe.wait_ge(x_copied, l + 1)
                pe.transpose(X[:, l, 0:GAINS], rows[0:GAINS, l * P:(l + 1) * P], ident[0:GAINS, 0:GAINS])
                for j in range(CONV + 1):
                    at = (DEPTH + l * (CONV + 1) + j) * P
                    mm = pe.transpose(X[:, l, GAINS + j * FT2:GAINS + (j + 1) * FT2], rows[0:FT2, at:at + P],
                                      ident[0:FT2, 0:FT2])
                mm.then_inc(rows_turned, 1)
            pe.wait_ge(rows_copied, DEPTH)
            pe.wait_ge(x_copied, 6)

            with pe.Fori(0, DEPTH) as l:
                r, ur = l * ROUNDS, l * PAIRS

                def tokens_block(j):
                    if j > 0:
                        bank_free(ur, U_TOK + j)
                    for q in range(4):
                        w_hi, w_lo = take(r, K_TOK[j] + q)
                        for a in range(4):
                            kt = 4 * q + a
                            if j == 0 and a % 2 == 0:
                                pe.wait_ge(h_ready.sem, h_ready.at(l, kt + 2))
                            for i in range(TT):
                                x_hi, x_lo = (hx[:, kt, b * T + i * P:b * T + (i + 1) * P] for b in range(2))
                                bank = bank2(U_TOK + j)[:, i, :]
                                pe.matmul(bank, x_hi, w_hi[:, 512 * a:512 * a + 512], start=kt == 0, stop=False)
                                pe.matmul(bank, x_lo, w_hi[:, 512 * a:512 * a + 512], start=False, stop=False)
                                mm = pe.matmul(bank, x_hi, w_lo[:, 512 * a:512 * a + 512], start=False, stop=kt == KT - 1)
                        mm.then_inc(slot_free, 1)

                def update(n):
                    if n >= 1:
                        pe.wait_ge(state_ready.sem, state_ready.at(l, 4 * n))
                    lanes, i = slice(64 * (n % 2), 64 * (n % 2) + 64), n // 2
                    for h in range(GH):
                        mm = pe.matmul(X[:, h // 2, (h % 2) * GDV:(h % 2 + 1) * GDV], gk[lanes, i, h * GDK:(h + 1) * GDK],
                                       gv[lanes, i, h * GDV:(h + 1) * GDV], start=True, stop=True)
                    mm.then_inc(update_done.sem, 1)

                def reads(n):
                    pe.wait_ge(state_ready.sem, state_ready.at(l, 4 * n + 4))
                    if n >= 1:
                        pe.wait_ge(reads_copied.sem, reads_copied.at(l, n))
                    for h in range(GH):
                        for e in range(2):
                            mm = pe.matmul(X[:, 2, (2 * h + e) * CHUNK:(2 * h + e + 1) * CHUNK],
                                           state[:, h, e * P:(e + 1) * P], z[:, Z_GQ + h, n * CHUNK:(n + 1) * CHUNK],
                                           start=True, stop=True)
                    mm.then_inc(reads_done.sem, 1)

                def c_sum(i):
                    pe.wait_ge(c_squared.sem, c_squared.at(l, i + 1))
                    for j in range(2):
                        mm = pe.matmul(X[:, 3, 0:T] if i < 2 else X[:, 3, T:2 * T], ones, sq[:, i % 2, j, :],
                                       start=i != 1 and j == 0, stop=i != 0 and j == 1)
                    mm.then_inc(c_square_used.sem, 1)

                def o_sum(h):
                    pe.wait_ge(o_squared.sem, o_squared.at(l, h + 1))
                    for e in range(2):
                        mm = pe.matmul(X[:, h, 0:T], ones, sq[:, h % 2, e, :], start=e == 0, stop=e == 1)
                    mm.then_inc(o_summed.sem, 1)

                tokens_block(0)
                norm_sums(l, 0, in_squared, in_square_used, l)
                for h in range(2):
                    w_hi, w_lo = take(r, K_MISC + h)
                    for a in range(8):
                        kt = 8 * h + a
                        mm = tile_pass(X[0:80, 1, :], w_hi[:, 80 * a:80 * a + 80], w_lo[:, 80 * a:80 * a + 80],
                                       hx[:, kt, :], kt == 0, kt == KT - 1)
                    mm.then_inc(slot_free, 1)
                tokens_block(1)
                pe.wait_ge(misc_ready.sem, misc_ready.at(l, 1))
                pe.wait_ge(gate_landed.sem, gate_landed.at(l, 32))
                for i in range(TT):
                    mm = pe.matmul(X[:, 2 + i, :], zm[64:64 + RANK + 1, i * P:(i + 1) * P], wg[64:64 + RANK + 1, :],
                                   start=True, stop=True)
                mm.then_inc(gate_logits.sem, 1)
                tokens_block(2)
                pe.wait_ge(gate_log.sem, gate_log.at(l, 1))
                for i in range(TT):
                    pe.matmul(X[:, 2 + i, :], suf, la[:, i, :], start=True, stop=True)
                for h in range(GH):
                    for i in range(TT):
                        mm = pe.matmul(X[:, 1, 4 * h + 2 * i:4 * h + 2 * i + 2], la[:, i, h * GDK:(h + 1) * GDK], ind,
                                       start=True, stop=True)
                mm.then_inc(gate_sums.sem, 1)
                for i in range(9):
                    bank_free(ur, U_FEAT + i)
                    for h in range(2):
                        pair_chunk(r, K_FEAT + 2 * i + h, U_FEAT + i, 8 * h, h == 0, h == 1)
                    if i == 1:
                        pe.wait_ge(keys_decayed.sem, keys_decayed.at(l, 1))
                        pe.wait_ge(gate_decay.sem, gate_decay.at(l, 2))
                    if 1 <= i <= 4:
                        update(i - 1)
                    if i == 2:
                        pe.wait_ge(z_scaled.sem, z_scaled.at(l, 2))
                    if 2 <= i <= 5:
                        reads(i - 2)
                    if 3 <= i <= 5:
                        c_sum(i - 3)
                    if i == 6:
                        pe.wait_ge(c_root.sem, c_root.at(l, 2))
                    if i in (7, 8):
                        o_sum(2 * i - 14)
                        o_sum(2 * i - 13)

                def uq(j):
                    w_hi, w_lo = take(r, K_UQ + j)
                    for i in range(3):
                        un = U_UQ + 2 * j + i // 2
                        if i != 1:
                            bank_free(ur, un)
                        for a in range(4):
                            at = a * 384 + i * P
                            mm = tile_pass(bank2(un)[:, i % 2, :], w_hi[:, at:at + P], w_lo[:, at:at + P],
                                           mid[:, a, :], a == 0, a == 3)
                        if i == 1:
                            mm.then_inc(unit_done, 1)
                    mm.then_inc(slot_free, 1)

                def ukv(j):
                    w_hi, w_lo = take(r, K_UKV + j)
                    for i in range(4):
                        un = U_UKV + 3 * j + i // 2
                        if i % 2 == 0:
                            bank_free(ur, un)
                        for a in range(2):
                            at = a * 1024 + i * 256
                            mm = tile_pass(bank2(un)[:, i % 2, :], w_hi[:, at:at + P], w_lo[:, at:at + P],
                                           mid[:, 4 + a, :], a == 0, a == 1)
                        if i % 2:
                            mm.then_inc(unit_done, 1)
                    un = U_UKV + 3 * j + 2
                    bank_free(ur, un)
                    for a in range(2):
                        wv_hi, wv_lo = (w[:, a * 1024:(a + 1) * 1024].rearrange("p (h c) -> p h c", h=4)[:, :, NOPE:]
                                        for w in (w_hi, w_lo))
                        for i in range(TT):
                            x_hi, x_lo = (mid[:, 4 + a, b * T + i * P:b * T + (i + 1) * P] for b in range(2))
                            bank = bank2(un)[:, i, :].rearrange("p (h c) -> p h c", h=4)
                            pe.matmul(bank, x_hi, wv_hi, start=a == 0, stop=False)
                            pe.matmul(bank, x_lo, wv_hi, start=False, stop=False)
                            mm = pe.matmul(bank, x_hi, wv_lo, start=False, stop=a == 1)
                    mm.then_inc(slot_free, 1)

                def qk_sum(j):
                    n = turn_of(j)
                    pe.wait_ge(qk_squared.sem, qk_squared.at(l, 2 * n + 2))
                    if n == 0:
                        pe.wait_ge(o_root.sem, o_root.at(l, 4))
                    elif 2 <= n < 6:
                        pe.wait_ge(qk_normed.sem, qk_normed.at(l, normed_at(n + 2)))
                    elif n >= 6:
                        pe.wait_ge(qk_root.sem, qk_root.at(l, n - 1))
                    for b in range(TT):
                        tokens = slice(b * P, (b + 1) * P)
                        where = X[:, j % 2, b:b + 3:2]
                        pe.matmul(where, sq[:, 1, 0, tokens], ind, start=True, stop=False)
                        for i in range(2):
                            mm = pe.matmul(where, sq[:, 0, i, tokens], to_column[i], start=False, stop=i == 1)
                    mm.then_inc(qk_summed.sem, 1)

                def spread(j):
                    pe.wait_ge(diag_ready.sem, diag_ready.at(l, j - 3))
                    pe.matmul(X[:, j % 2, :], ones, diag.rearrange("p c t -> p (c t)"), start=True,
                              stop=True).then_inc(k_scale_spread.sem, 1)

                def exchange(j):
                    pe.wait_ge(qk_normed.sem, qk_normed.at(l, normed_at(j)))
                    if turn_of(j) >= 2:
                        pe.wait_ge(rope_parts.sem, rope_parts.at(l, 2 * turn_of(j) - 2))
                    pe.matmul(X[:, 2 + j % 2, 0:T], rot, qkr[:, j, :], start=True, stop=True).then_inc(rope_turned.sem, 1)

                def out_g(i, tiles=(0, 1)):
                    bank_free(ur, U_OUT + i)
                    pair_chunk(r, K_OUT + i, U_OUT + i, 8, True, True, tiles=tiles)

                pe.wait_ge(c_ready.sem, c_ready.at(l, 3))
                ukv(0)
                ukv(1)
                qk_sum(4)
                uq(0)
                qk_sum(5)
                spread(4)
                uq(1)
                qk_sum(6)
                spread(5)
                exchange(4)
                uq(2)
                qk_sum(7)
                spread(6)
                exchange(5)
                uq(3)
                qk_sum(0)
                spread(7)
                exchange(6)
                pe.wait_ge(o_ready.sem, o_ready.at(l, GH))
                out_g(0)
                qk_sum(1)
                exchange(7)
                exchange(0)
                out_g(1)
                qk_sum(2)
                exchange(1)
                out_g(2)
                qk_sum(3)
                exchange(2)
                out_g(3, (0,))
                exchange(3)
                out_g(3, (1,))

                def scores(h):
                    if h >= 2:
                        pe.wait_ge(exps_done.sem, exps_done.at(l, 2 * h - 2))
                    else:
                        pe.wait_ge(qk_root.sem, qk_root.at(l, 7 + h))
                    if h % 2 == 0:
                        pe.wait_ge(rope_done.sem, rope_done.at(l, 5 + h // 2))
                    lanes = slice(64 * (h % 2), 64 * (h % 2) + 64)
                    for b in range(TT):
                        where = X[:, h % 2, 0:P] if b == 0 else X[:, h % 2, P:3 * P]
                        qs, ks = slice(b * P, (b + 1) * P), slice(0, (b + 1) * P)
                        pe.matmul(where, qn[:, h, qs], kn[:, h, ks], start=True, stop=False)
                        mm = pe.matmul(where, qkr[lanes, h // 2, qs], qkr[lanes, 4 + h // 2, ks], start=False, stop=True)
                    mm.then_inc(scores_done.sem, 1)

                scores(0)
                scores(1)
                out_g(4, (0,))
                for h in range(HEADS):
                    if h == 0:
                        pe.wait_ge(rope_done.sem, rope_done.at(l, 8))
                    pe.wait_ge(probs_ready.sem, probs_ready.at(l, 2 * h + 2))
                    if h >= 1:
                        pe.wait_ge(probs_copied.sem, probs_copied.at(l, h))
                    for i in range(3):
                        mm = pe.transpose(X[:, 2, i * P:(i + 1) * P], prob[:, h % 2, i * P:(i + 1) * P], ident)
                    mm.then_inc(probs_turned.sem, 1)
                    if h + 2 < HEADS:
                        scores(h + 2)
                    if h < 6:
                        out_g(4 + (h + 1) // 2, ((h + 1) % 2,))
                    pe.wait_ge(probs_copied.sem, probs_copied.at(l, h + 1))
                    if h >= 1:
                        pe.wait_ge(values_copied.sem, values_copied.at(l, h))
                    turned = probT[:, h % 2, :]
                    pe.matmul(X[:, 3, 0:T], v[:, 0, h * VD:(h + 1) * VD], turned[:, 0:T], start=True, stop=False)
                    pe.matmul(X[:, 3, P:T], v[:, 1, h * VD:(h + 1) * VD], turned[:, T:T + P], start=False,
                              stop=True).then_inc(values_done.sem, 1)
                pe.wait_ge(a_square_used.sem, a_square_used.at(l, 6))
                pe.matmul(X[:, 0, 0:T], ones, a_sum, start=True, stop=False)
                pe.wait_ge(a_squared.sem, a_squared.at(l, HEADS))
                pe.matmul(X[:, 0, 0:T], ones, a_sq[:, 1, :], start=False, stop=True).then_inc(a_summed.sem, 1)
                out_g(7, (1,))
                for i in range(8):
                    bank_free(ur, U_OUT + 8 + i)
                    pair_chunk(r, K_OUT + 8 + i, U_OUT + 8 + i, 0, True, True, a_ready if i == 0 else None, a_ready.at(l, 0))
                mlp_order(pe, l, up, down)
                pe.wait_ge(unit_free, l * UNITS + UNITS - 3 + 2)
            for n in range(8):
                pe.wait_ge(unit_free, UNITS * DEPTH + (2 if n >= 6 else 0))
                if 4 <= n < 6:
                    pe.wait_ge(out_copied[0], n - 3)
                for i in range(4):
                    mm = pe.transpose(out_bank(n)[:, i * P:(i + 1) * P],
                                      xT[:, 4 * (n // 2) + i, (n % 2) * P:(n % 2 + 1) * P], ident)
                mm.then_inc(out_turned, 1)


def shape_constants():
    c = np.zeros((P, CONSTS), np.float32)
    at = np.arange(P)
    c[:, CO_ID:CO_ID + P] = np.eye(P)
    c[:, CO_ONES:CO_ONES + P] = 1
    c[:, CO_ONE_HOT + 1] = 1
    c[:, CO_SUF:CO_SUF + P] = (at[:, None] > at[None, :]) & (at[:, None] // CHUNK == at[None, :] // CHUNK)
    for m in range(P):
        if m % ROPE < ROPE // 2:
            c[m + ROPE // 2, CO_ROT + m] = -1
        else:
            c[m - ROPE // 2, CO_ROT + m] = 1
    for i in range(2):
        c[64 * i:64 * i + 64, CO_IND + i] = 1
    c[:, CO_FREQ] = (ROPE_BASE ** (-(at % (ROPE // 2)) * 2.0 / ROPE)).astype(np.float32)
    c[:, CO_EPS] = EPS
    c[:, CO_EPSQ] = EPS * QK
    return c


def kernel(**inputs):
    import concourse.bacc as bacc
    from concourse.bass_utils import run_bass_kernel_spmd

    nc = bacc.Bacc("TRN2", target_bir_lowering=False, num_devices=1)
    arrays, aps = {}, {}
    for name, a in [*inputs.items(), ("consts", shape_constants())]:
        a = np.ascontiguousarray(a)
        arrays[f"in_{name}"] = a
        aps[name] = nc.dram_tensor(f"in_{name}", a.shape, mybir.dt.from_np(a.dtype), kind="ExternalInput").ap()
    out = nc.dram_tensor("out_0", (1, T, D), F32, kind="ExternalOutput").ap()
    trunk_program(nc, aps, out)
    r = run_bass_kernel_spmd(nc, [arrays], core_ids=[0])
    return r.results[0]["out_0"]
```
